# Optimizing a Trainium2 kernel written in Bass

```python
import math
import jax, jax.numpy as jnp
from jax import lax
import numpy as np

D_MODEL = 1024
BATCH = 1
SEQ = 1024
DEPTH = 2
DEC_BATCH = 1
DEC_SEQ = 32
PAST_LEN = 1024

CHUNK = 64
Q_BLOCK = 128
HEAD_DIM = 64
FOX_HEADS = 6
FOX_W = FOX_HEADS * HEAD_DIM
SWA_HEADS = 6
SWA_KV_HEADS = 2
SWA_GROUP = SWA_HEADS // SWA_KV_HEADS
SWA_W = SWA_HEADS * HEAD_DIM
SWA_KV_W = SWA_KV_HEADS * HEAD_DIM
WINDOW = 128
WINDOW_CHUNKS = WINDOW // CHUNK
MLA_HEADS = 4
MLA_Q_LORA = 256
MLA_KV_LORA = 128
MLA_NOPE = 64
MLA_ROPE = 32
MLA_V = 64
MLA_QK = MLA_NOPE + MLA_ROPE
MLA_W = MLA_HEADS * MLA_V
ROPE_BASE = 10000.0
MIX_W = FOX_W + SWA_W + MLA_W
D_FF = 2816
CONV_W = 3
EPS = 1e-6
NEG_INF = -1e30

IN_SIZES = (FOX_W, FOX_W, FOX_W, FOX_HEADS, SWA_W, SWA_KV_W, SWA_KV_W, MLA_Q_LORA, MLA_KV_LORA, MLA_ROPE)
IN_W = sum(IN_SIZES)
IN_CUTS = tuple(int(c) for c in np.cumsum(IN_SIZES)[:-1])

kernel_name = 'hybrid_fox_swa_mla_convffn_stream_step'

def _rmsnorm(x, g):
    xf = x.astype(jnp.float32)
    y = xf * lax.rsqrt(jnp.mean(xf * xf, axis=-1, keepdims=True) + EPS)
    return (y * g.astype(jnp.float32)).astype(x.dtype)

def _rope(x, pos):
    half = MLA_ROPE // 2
    inv = ROPE_BASE ** (-jnp.arange(half, dtype=jnp.float32) / half)
    ang = pos.astype(jnp.float32)[:, None] * inv[None, :]
    shape = (ang.shape[0],) + (1,) * (x.ndim - 3) + (half,)
    cos = jnp.cos(ang).reshape(shape)
    sin = jnp.sin(ang).reshape(shape)
    xf = x.astype(jnp.float32)
    x1, x2 = xf[..., :half], xf[..., half:]
    return jnp.concatenate([x1 * cos - x2 * sin, x1 * sin + x2 * cos], axis=-1).astype(x.dtype)

def _alibi_slopes(n):
    return jnp.asarray(2.0 ** (-8.0 * np.arange(1, n + 1) / n), dtype=jnp.float32)

def _sink_softmax(s, sink):
    sink = sink.astype(jnp.float32)
    m = jnp.maximum(jnp.max(s, axis=-1, keepdims=True), sink)
    e = jnp.exp(s - m)
    return e / (jnp.sum(e, axis=-1, keepdims=True) + jnp.exp(sink - m))

def _query_sweep(fn, *q_side):
    s = q_side[0].shape[1]
    if s <= Q_BLOCK:
        return fn(*q_side)
    nb = s // Q_BLOCK
    blocks = tuple(jnp.moveaxis(a.reshape((a.shape[0], nb, Q_BLOCK) + a.shape[2:]), 1, 0) for a in q_side)
    out = lax.map(lambda blk: fn(*blk), blocks)
    out = jnp.moveaxis(out, 0, 1)
    return out.reshape((out.shape[0], s) + out.shape[3:])

def _dense_attention(q, k, v, qpos, kpos, frame_causal, fq=None, fk=None):
    scale = q.shape[-1] ** -0.5
    kc = kpos // CHUNK

    def block(qb, qpb, *fqb):
        s = jnp.einsum('bqhd,bkhd->bhqk', qb, k, preferred_element_type=jnp.float32) * scale
        if fk is not None:
            s = s + jnp.swapaxes(fqb[0], 1, 2)[..., :, None] - jnp.swapaxes(fk, 1, 2)[..., None, :]
        qp = qpb[0]
        if frame_causal:
            allowed = kpos[None, :] <= qp[:, None]
        else:
            allowed = kc[None, :] <= (qp // CHUNK)[:, None]
        s = jnp.where(allowed, s, NEG_INF)
        p = jax.nn.softmax(s, axis=-1)
        return jnp.einsum('bhqk,bkhd->bqhd', p.astype(v.dtype), v)

    if fq is None:
        return _query_sweep(block, q, qpos[None, :])
    return _query_sweep(block, q, qpos[None, :], fq)

def _swa_banded(q, k, v, slopes, sinks):
    B, T, Hkv, G, d = q.shape
    nC = T // CHUNK
    NW = WINDOW_CHUNKS
    qc = q.reshape(B, nC, CHUNK, Hkv, G, d)

    def band(a):
        ac = a.reshape(B, nC, CHUNK, Hkv, d)
        ap = jnp.concatenate([jnp.zeros((B, NW - 1, CHUNK, Hkv, d), a.dtype), ac], axis=1)
        return jnp.concatenate([ap[:, w:w + nC] for w in range(NW)], axis=2)

    kb, vb = band(k), band(v)
    s = jnp.einsum('bcqngd,bcknd->bcngqk', qc, kb, preferred_element_type=jnp.float32) * d ** -0.5
    i = jnp.arange(CHUNK)[:, None]
    j = jnp.arange(NW * CHUNK)[None, :]
    dist = jnp.abs(i - j + (NW - 1) * CHUNK).astype(jnp.float32)
    s = s - slopes[:, :, None, None] * dist
    valid = (jnp.arange(nC)[:, None] + j // CHUNK) >= NW - 1
    s = jnp.where(valid[:, None, None, None, :], s, NEG_INF)
    p = _sink_softmax(s, sinks[:, :, None, None])
    o = jnp.einsum('bcngqk,bcknd->bcqngd', p.astype(v.dtype), vb)
    return o.reshape(B, T, Hkv * G * d)

def _swa_window(q, k, v, qpos, kpos, slopes, sinks):
    B, T, Hkv, G, d = q.shape
    s = jnp.einsum('bqngd,bknd->bngqk', q, k, preferred_element_type=jnp.float32) * d ** -0.5
    dist = jnp.abs(qpos[:, None] - kpos[None, :]).astype(jnp.float32)
    s = s - slopes[:, :, None, None] * dist
    qc = (qpos // CHUNK)[:, None]
    kc = (kpos // CHUNK)[None, :]
    allowed = (kc <= qc) & (kc > qc - WINDOW_CHUNKS)
    s = jnp.where(allowed, s, NEG_INF)
    p = _sink_softmax(s, sinks[:, :, None, None])
    o = jnp.einsum('bngqk,bknd->bqngd', p.astype(v.dtype), v)
    return o.reshape(B, T, Hkv * G * d)

def _token_mixers(h, p, past):
    B, T, _ = h.shape
    P = 0 if past is None else past['fox_k'].shape[1]
    qpos = P + jnp.arange(T, dtype=jnp.int32)
    kpos = jnp.arange(P + T, dtype=jnp.int32)
    (f_q, f_k, f_v, f_gate, s_q, s_k, s_v, m_cq, m_ckv, m_kr) = jnp.split(h @ p['w_in'], IN_CUTS, axis=-1)

    f_q = _rmsnorm(f_q.reshape(B, T, FOX_HEADS, HEAD_DIM), p['g_fox_q'])
    f_k = _rmsnorm(f_k.reshape(B, T, FOX_HEADS, HEAD_DIM), p['g_fox_k'])
    f_v = f_v.reshape(B, T, FOX_HEADS, HEAD_DIM)
    f_logf = jax.nn.log_sigmoid((f_gate + p['b_fox_f']).astype(jnp.float32))
    if past is None:
        fk_all, fv_all, lf_all = f_k, f_v, f_logf
    else:
        fk_all = jnp.concatenate([past['fox_k'], f_k], axis=1)
        fv_all = jnp.concatenate([past['fox_v'], f_v], axis=1)
        lf_all = jnp.concatenate([past['fox_logf'].astype(jnp.float32), f_logf], axis=1)
    F = jnp.cumsum(lf_all, axis=1)
    y_fox = _dense_attention(f_q, fk_all, fv_all, qpos, kpos, True, F[:, P:], F).reshape(B, T, FOX_W)

    s_q = _rmsnorm(s_q.reshape(B, T, SWA_HEADS, HEAD_DIM), p['g_swa_q']).reshape(B, T, SWA_KV_HEADS, SWA_GROUP, HEAD_DIM)
    s_k = _rmsnorm(s_k.reshape(B, T, SWA_KV_HEADS, HEAD_DIM), p['g_swa_k'])
    s_v = s_v.reshape(B, T, SWA_KV_HEADS, HEAD_DIM)
    slopes = _alibi_slopes(SWA_HEADS).reshape(SWA_KV_HEADS, SWA_GROUP)
    sinks = p['swa_sinks'].reshape(SWA_KV_HEADS, SWA_GROUP)
    if past is None:
        y_swa = _swa_banded(s_q, s_k, s_v, slopes, sinks)
        wc = min(WINDOW, T)
        swa_k_new, swa_v_new = s_k[:, T - wc:], s_v[:, T - wc:]
    else:
        wc = past['swa_k'].shape[1]
        sk_all = jnp.concatenate([past['swa_k'], s_k], axis=1)
        sv_all = jnp.concatenate([past['swa_v'], s_v], axis=1)
        spos = jnp.arange(P - wc, P + T, dtype=jnp.int32)
        y_swa = _swa_window(s_q, sk_all, sv_all, qpos, spos, slopes, sinks)
        swa_k_new, swa_v_new = sk_all[:, T:], sv_all[:, T:]

    q = (_rmsnorm(m_cq, p['g_mla_cq']) @ p['w_mla_uq']).reshape(B, T, MLA_HEADS, MLA_QK)
    q = _rmsnorm(jnp.concatenate([q[..., :MLA_NOPE], _rope(q[..., MLA_NOPE:], qpos)], axis=-1), p['g_mla_q'])
    ckv = _rmsnorm(m_ckv, p['g_mla_ckv'])
    kr = _rope(m_kr, qpos)
    if past is None:
        ckv_all, kr_all = ckv, kr
    else:
        ckv_all = jnp.concatenate([past['mla_ckv'], ckv], axis=1)
        kr_all = jnp.concatenate([past['mla_krope'], kr], axis=1)
    S = P + T
    kv = (ckv_all @ p['w_mla_ukv']).reshape(B, S, MLA_HEADS, MLA_NOPE + MLA_V)
    k = jnp.concatenate([kv[..., :MLA_NOPE], jnp.broadcast_to(kr_all[:, :, None, :], (B, S, MLA_HEADS, MLA_ROPE))], axis=-1)
    k = _rmsnorm(k, p['g_mla_k'])
    y_mla = _dense_attention(q, k, kv[..., MLA_NOPE:], qpos, kpos, False).reshape(B, T, MLA_W)

    g = p['g_mix_out']
    y = jnp.concatenate([_rmsnorm(y_fox, g[:FOX_W]),
                         _rmsnorm(y_swa, g[FOX_W:FOX_W + SWA_W]),
                         _rmsnorm(y_mla, g[FOX_W + SWA_W:])], axis=-1)
    return y @ p['w_out'], (f_k, f_v, f_logf, swa_k_new, swa_v_new, ckv, kr)

def _conv_ffn(h, p, prev):
    B, T, _ = h.shape
    a, b = jnp.split(h @ p['w_ffn_up'], 2, axis=-1)
    if prev is None:
        prev = jnp.zeros((B, CONV_W - 1, D_FF), a.dtype)
    a_ext = jnp.concatenate([prev.astype(a.dtype), a], axis=1)
    w = p['w_ffn_conv']
    c = p['b_ffn_conv']
    for j in range(CONV_W):
        c = c + a_ext[:, j:j + T] * w[j]
    u = jax.nn.gelu(c) * b
    return u @ p['w_ffn_down'], a_ext[:, T:]

def _layer(x, p, past):
    mix, st = _token_mixers(_rmsnorm(x, p['g_norm1']), p, past)
    x = x + mix
    ffn, conv_state = _conv_ffn(_rmsnorm(x, p['g_norm2']), p, None if past is None else past['ffn_conv'])
    return x + ffn, st + (conv_state,)

def setup_inputs(seed: int = 0) -> dict:
    key = jax.random.key(seed)
    ks = iter(jax.random.split(key, 40))

    def nrm(shape, scale=1.0):
        return scale * jax.random.normal(next(ks), shape, jnp.float32)

    def gain(shape):
        return 1.0 + 0.05 * nrm(shape)

    swa_len = min(WINDOW, PAST_LEN)
    return {
        'x_prompt': nrm((BATCH, SEQ, D_MODEL)),
        'x_sample': nrm((DEC_BATCH, DEC_SEQ, D_MODEL)),
        'cache_fox_k': nrm((DEPTH, DEC_BATCH, PAST_LEN, FOX_HEADS, HEAD_DIM)),
        'cache_fox_v': nrm((DEPTH, DEC_BATCH, PAST_LEN, FOX_HEADS, HEAD_DIM)),
        'cache_fox_logf': jax.nn.log_sigmoid(4.0 + nrm((DEPTH, DEC_BATCH, PAST_LEN, FOX_HEADS))),
        'cache_swa_k': nrm((DEPTH, DEC_BATCH, swa_len, SWA_KV_HEADS, HEAD_DIM)),
        'cache_swa_v': nrm((DEPTH, DEC_BATCH, swa_len, SWA_KV_HEADS, HEAD_DIM)),
        'cache_mla_ckv': nrm((DEPTH, DEC_BATCH, PAST_LEN, MLA_KV_LORA)),
        'cache_mla_krope': nrm((DEPTH, DEC_BATCH, PAST_LEN, MLA_ROPE)),
        'state_ffn_conv': nrm((DEPTH, DEC_BATCH, CONV_W - 1, D_FF)),
        'g_norm1': gain((DEPTH, D_MODEL)),
        'w_in': nrm((DEPTH, D_MODEL, IN_W), D_MODEL ** -0.5),
        'b_fox_f': jnp.linspace(2.0, 6.0, FOX_HEADS)[None, :] + 0.1 * nrm((DEPTH, FOX_HEADS)),
        'g_fox_q': gain((DEPTH, HEAD_DIM)),
        'g_fox_k': gain((DEPTH, HEAD_DIM)),
        'g_swa_q': gain((DEPTH, HEAD_DIM)),
        'g_swa_k': gain((DEPTH, HEAD_DIM)),
        'swa_sinks': nrm((DEPTH, SWA_HEADS), 0.5),
        'g_mla_cq': gain((DEPTH, MLA_Q_LORA)),
        'g_mla_ckv': gain((DEPTH, MLA_KV_LORA)),
        'w_mla_uq': nrm((DEPTH, MLA_Q_LORA, MLA_HEADS * MLA_QK), MLA_Q_LORA ** -0.5),
        'w_mla_ukv': nrm((DEPTH, MLA_KV_LORA, MLA_HEADS * (MLA_NOPE + MLA_V)), MLA_KV_LORA ** -0.5),
        'g_mla_q': gain((DEPTH, MLA_QK)),
        'g_mla_k': gain((DEPTH, MLA_QK)),
        'g_mix_out': gain((DEPTH, MIX_W)),
        'w_out': nrm((DEPTH, MIX_W, D_MODEL), MIX_W ** -0.5),
        'g_norm2': gain((DEPTH, D_MODEL)),
        'w_ffn_up': nrm((DEPTH, D_MODEL, 2 * D_FF), D_MODEL ** -0.5),
        'w_ffn_conv': nrm((DEPTH, CONV_W, D_FF), CONV_W ** -0.5),
        'b_ffn_conv': nrm((DEPTH, D_FF), 0.01),
        'w_ffn_down': nrm((DEPTH, D_FF, D_MODEL), D_FF ** -0.5),
    }

def reference(x_prompt, x_sample, cache_fox_k, cache_fox_v, cache_fox_logf, cache_swa_k, cache_swa_v,
              cache_mla_ckv, cache_mla_krope, state_ffn_conv, g_norm1, w_in, b_fox_f, g_fox_q, g_fox_k,
              g_swa_q, g_swa_k, swa_sinks, g_mla_cq, g_mla_ckv, w_mla_uq, w_mla_ukv, g_mla_q, g_mla_k,
              g_mix_out, w_out, g_norm2, w_ffn_up, w_ffn_conv, b_ffn_conv, w_ffn_down):
    xp, xs = x_prompt, x_sample
    states_p, states_s = [], []
    for l in range(DEPTH):
        p = dict(g_norm1=g_norm1[l], w_in=w_in[l], b_fox_f=b_fox_f[l], g_fox_q=g_fox_q[l], g_fox_k=g_fox_k[l],
                 g_swa_q=g_swa_q[l], g_swa_k=g_swa_k[l], swa_sinks=swa_sinks[l], g_mla_cq=g_mla_cq[l],
                 g_mla_ckv=g_mla_ckv[l], w_mla_uq=w_mla_uq[l], w_mla_ukv=w_mla_ukv[l], g_mla_q=g_mla_q[l],
                 g_mla_k=g_mla_k[l], g_mix_out=g_mix_out[l], w_out=w_out[l], g_norm2=g_norm2[l],
                 w_ffn_up=w_ffn_up[l], w_ffn_conv=w_ffn_conv[l], b_ffn_conv=b_ffn_conv[l], w_ffn_down=w_ffn_down[l])
        past = dict(fox_k=cache_fox_k[l], fox_v=cache_fox_v[l], fox_logf=cache_fox_logf[l],
                    swa_k=cache_swa_k[l], swa_v=cache_swa_v[l], mla_ckv=cache_mla_ckv[l],
                    mla_krope=cache_mla_krope[l], ffn_conv=state_ffn_conv[l])
        xp, st_p = _layer(xp, p, None)
        xs, st_s = _layer(xs, p, past)
        states_p.append(st_p)
        states_s.append(st_s)
    (fox_k_p, fox_v_p, fox_logf_p, swa_k_p, swa_v_p, mla_ckv_p, mla_krope_p, ffn_conv_p) = [
        jnp.stack([st[i] for st in states_p]) for i in range(8)]
    (fox_k_s, fox_v_s, fox_logf_s, swa_k_s, swa_v_s, mla_ckv_s, mla_krope_s, ffn_conv_s) = [
        jnp.stack([st[i] for st in states_s]) for i in range(8)]
    return (xp, xs,
            fox_k_p, fox_v_p, fox_logf_p, swa_k_p, swa_v_p, mla_ckv_p, mla_krope_p, ffn_conv_p,
            fox_k_s, fox_v_s, fox_logf_s, swa_k_s, swa_v_s, mla_ckv_s, mla_krope_s, ffn_conv_s)


_drawn_inputs = setup_inputs


def setup_inputs(seed=0):
    import zlib

    import numpy as np

    out = dict(_drawn_inputs(seed))
    spreads = {}
    factors = {'b_ffn_conv': 8.0}
    for name, (base, spread) in spreads.items():
        noise = np.random.default_rng([zlib.crc32(name.encode()), seed]).standard_normal(out[name].shape)
        drawn = base * np.exp(spread * noise) if base else spread * noise
        out[name] = __import__('jax').numpy.asarray(drawn.astype(out[name].dtype))
    for name, factor in factors.items():
        out[name] = (out[name] * factor).astype(out[name].dtype)
    return out
```

```python
import math
from contextlib import ExitStack

import numpy as np
import concourse.bass as bass
from concourse import mybir

F32 = mybir.dt.float32
F32R = mybir.dt.float32r
ACT = mybir.ActivationFunctionType
ALU = mybir.AluOpType
AX = mybir.AxisListType.X

P = 128
D = 1024
SEQ = 1024
DEC = 32
PAST = 1024
DEPTH = 2
TOK = SEQ + DEC
DC = D // P
QT = SEQ // P
TT = QT + 1
NT = 3
TN = TOK // NT
HD = 64
FOXH, SWAH, SWAKV, MLAH = 6, 6, 2, 4
CHUNK = 64
WIN = 128
QLORA, KVLORA, NOPE, ROPE = 256, 128, 64, 32
MQK = NOPE + ROPE
DFF = 2816
FC = DFF // P
CW = 3
EPS = 1e-6
BIG = -1e30
O_FQ, O_FK, O_FV, O_G = 0, 384, 768, 1152
O_SQ, O_SK, O_SV = 1158, 1542, 1670
O_CQ, O_CKV, O_KR = 1798, 2054, 2182
IN_W = 2214
WN = 246
WSTEPS = IN_W // WN
V_G1, V_G2, V_GM, V_CW, V_CB, V_ST = 0, 8, 16, 24, 24 + CW * FC, 24 + (CW + 1) * FC
V_N = V_ST + 2 * FC
R_FQ, R_FK, R_SQ, R_SK = 0, 64, 128, 192
R_CQ, R_CKV, R_MQ, R_MK, R_BF, R_SINK = 256, 512, 640, 736, 832, 838
R_N = 844
SLOPES = [2.0 ** (-8.0 * (h + 1) / SWAH) for h in range(SWAH)]


class Steps:

    def __init__(self, eng, sem, base=0):
        self.eng, self.sem, self.base, self.n = eng, sem, base, 0

    def mark(self, ins):
        ins.then_inc(self.sem, 1)
        self.n += 1
        return self.n

    def wait(self, n):
        self.eng.wait_ge(self.sem, self.base + n)

    def after(self, ins):
        self.wait(self.mark(ins))


def bcast(ap, shape, *axes):
    for a in axes:
        ap = ap.unsqueeze(a)
    return ap.broadcast_to(shape)


C_ID, C_TRI, C_ONE, C_MFOX, C_MMLA, C_DIST = 0, 128, 256, 384, 512, 640
C_COS = C_DIST + 2 * P
C_SIN = C_COS + TT * ROPE // 2
C_SLOPE = C_SIN + TT * ROPE // 2
C_MNEW = C_SLOPE + SWAH
C_SEL = C_MNEW + DEC
C_BSW = C_SEL + 2 * P
SKEYS = WIN - CHUNK + DEC
C_EPS = C_BSW + 2 * SKEYS
C_N = C_EPS + 1


def const_table():
    c = np.zeros((P, C_N), np.float32)
    p = np.arange(P)
    c[:, C_ID:C_ID + P] = np.eye(P)
    c[:, C_TRI:C_TRI + P] = p[:, None] <= p[None, :]
    c[:, C_ONE:C_ONE + P] = 1
    c[:, C_MFOX:C_MFOX + P] = np.where(p[None, :] <= p[:, None], 0, BIG)
    c[:, C_MMLA:C_MMLA + P] = np.where(p[None, :] // CHUNK <= p[:, None] // CHUNK, 0, BIG)
    j = np.arange(2 * P)[None, :]
    qc, kc = (P + p[:, None]) // CHUNK, j // CHUNK
    ok = (kc <= qc) & (kc > qc - WIN // CHUNK)
    c[:, C_DIST:C_DIST + 2 * P] = np.where(ok, np.abs(P + p[:, None] - j), -BIG / SLOPES[-1])
    half = ROPE // 2
    inv = (np.float32(10000.0) ** (-np.arange(half, dtype=np.float32) / np.float32(half))).astype(np.float32)
    for t in range(TT):
        ang = (np.float32(P * t) + p.astype(np.float32))[:, None] * inv[None, :]
        c[:, C_COS + t * half:C_COS + (t + 1) * half] = np.cos(ang.astype(np.float64))
        c[:, C_SIN + t * half:C_SIN + (t + 1) * half] = np.sin(ang.astype(np.float64))
    for h in range(SWAH):
        c[:, C_SLOPE + h] = -SLOPES[h]
    q = p % DEC
    c[:, C_MNEW:C_MNEW + DEC] = np.where(np.arange(DEC)[None, :] <= q[:, None], 0, BIG)
    qpos = PAST + q[:, None]
    kpos = PAST - (WIN - CHUNK) + np.arange(SKEYS)[None, :]
    for g in range(2):
        for r in range(P):
            h = 4 * g + r // DEC
            if h < FOXH:
                c[h, C_SEL + g * P + r] = c[32 + h, C_SEL + g * P + r] = 1
                c[r, C_BSW + g * SKEYS:C_BSW + (g + 1) * SKEYS] = -SLOPES[h] * np.abs(qpos[r] - kpos[0])
    c[:, C_EPS] = EPS
    return c


class Chip:
    pass


def load_tokens(nc, k):
    with ExitStack() as s:
        xin = s.enter_context(nc.sbuf_tensor("xin", [P, 2, D], F32))
        xT = s.enter_context(nc.sbuf_tensor("xT0", [P, DC, TOK], F32))
        ps = s.enter_context(nc.psum_tensor("xps", [P, 2, DC, P], F32))
        ident = k.const[:, C_ID:C_ID + P]
        sem = k.sems["tok"]
        const_in, stored = sem["const"], sem["stored"]
        rows_in, turned, copied = sem["a"], sem["b"], sem["c"]
        with nc.Block() as block:

            @block.sync
            def _(sp):
                sp.dma_start(k.const[:, :], k.consts).then_inc(const_in, 16)
                for t in range(TT):
                    if t >= 2:
                        sp.wait_ge(turned[t % 2], t // 2)
                    n = P if t < QT else DEC
                    src = k.x_prompt[t * P:t * P + n] if t < QT else k.x_sample
                    sp.dma_start(xin[0:n, t % 2, :], src).then_inc(rows_in[t % 2], 16)
                for t in range(TT):
                    sp.wait_ge(copied[t % 2], t // 2 + 1)
                sp.dma_start(k.x_dram, xT[:, :, :]).then_inc(stored, 16)
                sp.wait_ge(stored, 16)

            @block.tensor
            def _(pe):
                pe.wait_ge(const_in, 16)
                for t in range(TT):
                    n = P if t < QT else DEC
                    pe.wait_ge(rows_in[t % 2], 16 * (t // 2 + 1))
                    if t >= 2:
                        pe.wait_ge(copied[t % 2], t // 2)
                    for c in range(DC):
                        last = pe.transpose(ps[:, t % 2, c, 0:n], xin[0:n, t % 2, c * P:(c + 1) * P],
                                            ident[0:n, 0:n])
                    last.then_inc(turned[t % 2], 1)

            @block.scalar
            def _(act):
                act.wait_ge(const_in, 16)
                act.activation(k.identr[:, :], k.const[:, C_ID:C_ID + P], ACT.Copy)
                act.activation(k.mfoxr[:, :], k.const[:, C_MFOX:C_MFOX + P], ACT.Copy)
                act.activation(k.mmlar[:, :], k.const[:, C_MMLA:C_MMLA + P], ACT.Copy)
                for t in range(TT):
                    n = P if t < QT else DEC
                    act.wait_ge(turned[t % 2], t // 2 + 1)
                    act.activation(xT[:, :, t * P:t * P + n], ps[:, t % 2, :, 0:n], ACT.Copy)\
                       .then_inc(copied[t % 2], 1)


def store_tokens(nc, k):
    with ExitStack() as s:
        xT = s.enter_context(nc.sbuf_tensor("xT9", [P, DC, TOK], F32))
        xout = s.enter_context(nc.sbuf_tensor("xout", [P, 2, D], F32))
        ps = s.enter_context(nc.psum_tensor("yps", [P, 2, DC, P], F32))
        ident = k.const[:, C_ID:C_ID + P]
        sem = k.sems["out"]
        x_in, turned, copied, stored = sem["x"], sem["b"], sem["c"], sem["s"]
        with nc.Block() as block:

            @block.sync
            def _(sp):
                sp.dma_start(xT[:, :, :], k.x_dram).then_inc(x_in, 16)
                for t in range(TT):
                    n = P if t < QT else DEC
                    sp.wait_ge(copied[t % 2], t // 2 + 1)
                    dst = k.y_prompt[t * P:t * P + n] if t < QT else k.y_sample
                    sp.dma_start(dst, xout[0:n, t % 2, :]).then_inc(stored[t % 2], 16)
                sp.wait_ge(stored[0], 16 * (TT // 2 + 1))
                sp.wait_ge(stored[1], 16 * (TT // 2))

            @block.tensor
            def _(pe):
                pe.wait_ge(x_in, 16)
                for t in range(TT):
                    n = P if t < QT else DEC
                    if t >= 2:
                        pe.wait_ge(copied[t % 2], t // 2)
                    for c in range(DC):
                        last = pe.transpose(ps[0:n, t % 2, c, :], xT[:, c, t * P:t * P + n], ident)
                    last.then_inc(turned[t % 2], 1)

            @block.scalar
            def _(act):
                for t in range(TT):
                    n = P if t < QT else DEC
                    act.wait_ge(turned[t % 2], t // 2 + 1)
                    if t >= 2:
                        act.wait_ge(stored[t % 2], 16 * (t // 2))
                    act.activation(xout[0:n, t % 2, :], ps[0:n, t % 2, :, :].rearrange("p c n -> p (c n)"),
                                   ACT.Copy).then_inc(copied[t % 2], 1)


def load_vectors(nc, k, lay):
    with ExitStack() as s:
        st = s.enter_context(nc.sbuf_tensor("vstage", [P, 2, P], F32))
        ps = s.enter_context(nc.psum_tensor("vps", [P, 2, P], F32))
        sem = k.sems["vec"]
        loaded, turned, rows_in = sem["l"], sem["t"], sem["r"]
        rest = V_N - P
        feat = [(V_G1, k.g_norm1[lay].rearrange("(c p) -> c p", p=P)),
                (V_G2, k.g_norm2[lay].rearrange("(c p) -> c p", p=P)),
                (V_GM, k.g_mix_out[lay].rearrange("(c p) -> c p", p=P)),
                (V_CW, k.w_ffn_conv[lay].rearrange("w (c p) -> (w c) p", p=P)),
                (V_CB, k.b_ffn_conv[lay].rearrange("(c p) -> c p", p=P))]
        state = k.state_ffn_conv[lay, 0].rearrange("t (c p) -> (t c) p", p=P)
        split = P - V_ST
        free = [(R_FQ, k.g_fox_q), (R_FK, k.g_fox_k), (R_SQ, k.g_swa_q), (R_SK, k.g_swa_k),
                (R_CQ, k.g_mla_cq), (R_CKV, k.g_mla_ckv), (R_MQ, k.g_mla_q), (R_MK, k.g_mla_k),
                (R_BF, k.b_fox_f), (R_SINK, k.swa_sinks)]
        with nc.Block() as block:

            @block.sync
            def _(sp):
                for at, src in feat:
                    sp.dma_start(st[at:at + src.shape[0], 0, :], src).then_inc(loaded, 16)
                sp.dma_start(st[V_ST:P, 0, :], state[0:split]).then_inc(loaded, 16)
                sp.dma_start(st[0:rest, 1, :], state[split:2 * FC]).then_inc(loaded, 16)

            @block.scalar
            def _(act):
                for at, src in free:
                    act.dma_start(k.row[:, at:at + src.shape[1]], src[lay].partition_broadcast(P))\
                       .then_inc(rows_in, 16)
                act.wait_ge(turned, 1)
                act.activation(k.vec[:, 0:P], ps[:, 0, :], ACT.Copy)
                act.activation(k.vec[:, P:V_N], ps[:, 1, 0:rest], ACT.Copy)

            @block.tensor
            def _(pe):
                ident = k.const[:, C_ID:C_ID + P]
                pe.wait_ge(loaded, 16 * (len(feat) + 2))
                pe.transpose(ps[:, 0, :], st[:, 0, :], ident)
                pe.transpose(ps[:, 1, 0:rest], st[0:rest, 1, :], ident[0:rest, 0:rest]).then_inc(turned, 1)

            @block.vector
            def _(dve):
                dve.wait_ge(rows_in, 16 * len(free))
                chain = Steps(dve, sem["d"])
                for at, n, d in ((R_FQ, HD, HD), (R_SQ, HD, HD), (R_MQ, MQK, MQK)):
                    last = dve.tensor_scalar(k.row[:, at:at + n], k.row[:, at:at + n], float(d) ** -0.5, None, ALU.mult)
                chain.after(last)


def norm(nc, k, xT, hi, lo, gain, tag, groups, load=False):
    with ExitStack() as s:
        G = len(groups)
        sq = s.enter_context(nc.sbuf_tensor("nsq" + tag, [P, 2, TOK], F32))
        hf = s.enter_context(nc.sbuf_tensor("nhf" + tag, [P, 2, TOK], F32))
        rs = s.enter_context(nc.sbuf_tensor("nrs" + tag, [P, min(G, 2), NT, TN], F32))
        ps = s.enter_context(nc.psum_tensor("nps" + tag, [P, min(G, 2), NT, 512], F32))
        sem = k.sems["norm"]
        x_in, squared, summed, ln_done, rs_done, normed, hi_done, low = (sem[n] for n in
                                                         ("x", "sq", "sum", "ln", "rs", "hf", "hi", "lo"))
        ones = k.const[:, C_ONE:C_ONE + P]
        chunks = [(c, g) for g, (a, b) in enumerate(groups) for c in range(a, b)]
        with nc.Block() as block:

            if load:
                @block.sync
                def _(sp):
                    for c in range(DC):
                        sp.dma_start(xT[:, c, :], k.x_dram[:, c, :]).then_inc(x_in[c], 16)

            @block.scalar
            def _(act):
                def square(c):
                    if load:
                        act.wait_ge(x_in[c], 16)
                    if c >= 2:
                        act.wait_ge(summed, c - 1)
                    act.activation(sq[:, c % 2, :], xT[:, c, :], ACT.Square).then_inc(squared, 1)

                for c in range(*groups[0]):
                    square(c)
                for g, (a, b) in enumerate(groups):
                    act.wait_ge(summed, b)
                    if g >= 2:
                        act.wait_ge(normed, groups[g - 2][1])
                    for t in range(NT):
                        act.activation(rs[:, g % 2, t, :], ps[:, g % 2, t, 0:TN], ACT.Ln, scale=1.0 / (P * (b - a)),
                                       bias=k.const[:, C_EPS:C_EPS + 1]).then_inc(ln_done, 1)
                    for t in range(NT):
                        act.wait_ge(ln_done, NT * g + t + 1)
                        act.activation(rs[:, g % 2, t, :], rs[:, g % 2, t, :], ACT.Exp, scale=-0.5)\
                           .then_inc(rs_done, 1)
                    if g + 1 < G:
                        for c in range(*groups[g + 1]):
                            square(c)
                    for c in range(a, b):
                        act.wait_ge(normed, c + 1)
                        act.activation(hi[:, c, :], hf[:, c % 2, :], ACT.Copy).then_inc(hi_done, 1)

            @block.tensor
            def _(pe):
                for c, g in chunks:
                    pe.wait_ge(squared, c + 1)
                    if g >= 2:
                        pe.wait_ge(ln_done, NT * (g - 1))
                    for t in range(NT):
                        last = pe.matmul(ps[:, g % 2, t, 0:TN], ones, sq[:, c % 2, t * TN:(t + 1) * TN],
                                         start=(c == groups[g][0]), stop=(c == groups[g][1] - 1))
                    last.then_inc(summed, 1)

            @block.vector
            def _(dve):
                for c, g in chunks + [(DC, G)]:
                    if c < DC:
                        dve.wait_ge(rs_done, NT * (g + 1))
                        if c >= 2:
                            dve.wait_ge(low, c - 1)
                        dve.scalar_tensor_tensor(hf[:, c % 2, :], xT[:, c, :], k.vec[:, gain + c:gain + c + 1],
                                                 rs[:, g % 2, :, :].rearrange("p t n -> p (t n)"),
                                                 ALU.mult, ALU.mult).then_inc(normed, 1)
                    if c >= 1:
                        dve.wait_ge(hi_done, c)
                        dve.tensor_tensor(lo[:, c - 1, :], hf[:, (c - 1) % 2, :],
                                          hi[:, c - 1, :].bitcast(F32), ALU.subtract).then_inc(low, 1)
    restart(nc, k.lists["norm"])


def project_in(nc, k, lay, hi, lo, proj):
    with ExitStack() as s:
        raw = s.enter_context(nc.sbuf_tensor("wraw", [P, 2, DC, WN], F32))
        whi = s.enter_context(nc.sbuf_tensor("whi", [P, 2, DC, WN], F32R))
        wlo = s.enter_context(nc.sbuf_tensor("wlo", [P, 2, DC, WN], F32R))
        NB = 3
        ps = s.enter_context(nc.psum_tensor("wps", [P, NB, 512], F32))
        sem = k.sems["win"]
        raw_in, hi_done, lo_done, tile_done, tile_free = (sem[n] for n in ("raw", "hi", "lo", "done", "tf"))
        w_dram = k.w_in[lay].rearrange("(c p) n -> p c n", p=P)
        per = TT // NB

        def steps(eng, body):
            with eng.Fori(0, WSTEPS // 2) as i:
                for b in range(2):
                    body(i, b, 2 * i + b)
            body(WSTEPS // 2, 0, WSTEPS - 1)

        with nc.Block() as block:

            @block.sync
            def _(sp):
                def body(i, b, step):
                    sp.wait_ge(lo_done[b], i)
                    sp.dma_start(raw[:, b], w_dram[:, :, bass.ds(step * WN, WN)]).then_inc(raw_in[b], 16)
                steps(sp, body)

            @block.vector
            def _(dve):
                dve.memset(proj[32:64, QT, :], 0.0)
                dve.memset(proj[64:128, QT, :], 0.0)

            @block.gpsimd
            def _(pool):
                def body(i, b, step):
                    pool.wait_ge(hi_done[b], i + 1)
                    pool.wait_ge(lo_done[1 - b], i + b)
                    pool.tensor_tensor(wlo[:, b], raw[:, b], whi[:, b].bitcast(F32), ALU.subtract)\
                        .then_inc(lo_done[b], 1)
                steps(pool, body)

            @block.scalar
            def _(act):
                def split(i, b):
                    act.wait_ge(raw_in[b], 16 * i + 16)
                    act.activation(whi[:, b], raw[:, b], ACT.Copy).then_inc(hi_done[b], 1)

                def drain(i, b, step):
                    for t in range(TT):
                        n = P if t < QT else DEC
                        act.wait_ge(tile_done[t % NB], step * per + (t // NB + 1))
                        act.activation(proj[0:n, t, bass.ds(step * WN, WN)], ps[0:n, t % NB, 0:WN],
                                       ACT.Copy).then_inc(tile_free[t % NB], 1)
                split(0, 0)
                with act.Fori(0, WSTEPS // 2) as i:
                    split(i, 1)
                    drain(i, 0, 2 * i)
                    split(i + 1, 0)
                    drain(i, 1, 2 * i + 1)
                drain(WSTEPS // 2, 0, WSTEPS - 1)

            @block.tensor
            def _(pe):
                def body(i, b, step):
                    pe.wait_ge(lo_done[b], i + 1)
                    for t in range(TT):
                        n = P if t < QT else DEC
                        pe.wait_ge(tile_free[t % NB], step * per + t // NB)
                        at = slice(t * P, t * P + n)
                        for c in range(DC):
                            for m, (a, w) in enumerate(((hi, whi), (hi, wlo), (lo, whi))):
                                last = pe.matmul(ps[0:n, t % NB, 0:WN], a[:, c, at], w[:, b, c, :],
                                                 start=(c == 0 and m == 0), stop=(c == DC - 1 and m == 2))
                        last.then_inc(tile_done[t % NB], 1)
                steps(pe, body)


def fox_prepare(nc, k, lay, proj, aug, fs, qk_new):
    HF = 2 * FOXH
    with ExitStack() as s:
        ss = s.enter_context(nc.sbuf_tensor("fss", [P, TT, HF], F32))
        g = s.enter_context(nc.sbuf_tensor("fgate", [P, 6, TT, FOXH], F32))
        cl = s.enter_context(nc.sbuf_tensor("fcl", [P, TT, FOXH], F32))
        pre = s.enter_context(nc.sbuf_tensor("fpre", [P, 2, TT, FOXH], F32))
        ps = s.enter_context(nc.psum_tensor("fps", [P, 2, 512], F32))
        sem = k.sems["fox"]
        cached, stored = sem["cl"], sem["st"]
        squared, act_steps, dve_steps, sums, f_done = (sem[n] for n in ("sq", "act", "dve", "sum", "f"))
        x, ax, e, u, r, lf = (g[:, n] for n in range(6))
        gate = proj[:, :, O_G:O_G + FOXH]
        tri, ones = k.const[:, C_TRI:C_TRI + P], k.const[:, C_ONE:C_ONE + P]
        qk = proj[:, :, O_FQ:O_FV].rearrange("p t (h d) -> p t h d", d=HD)
        with nc.Block() as block:

            @block.sync
            def _(sp):
                sp.dma_start(cl[:, 0:QT, :], k.cache_fox_logf[lay, 0].rearrange("(t p) h -> p t h", p=P))\
                  .then_inc(cached, 16)
                v = proj[:, :, O_FV:O_G]
                sp.dma_start(k.fox_v_p[lay, 0].rearrange("(t p) h d -> p t (h d)", p=P), v[:, 0:QT])\
                  .then_inc(stored, 16)
                sp.dma_start(k.fox_v_s[lay, 0].rearrange("t h d -> t (h d)"), v[0:DEC, QT]).then_inc(stored, 16)
                sp.wait_ge(dve_steps, 8)
                sp.dma_start(k.fox_logf_p[lay, 0].rearrange("(t p) h -> p t h", p=P), lf[:, 0:QT])\
                  .then_inc(stored, 16)
                sp.dma_start(k.fox_logf_s[lay, 0], lf[0:DEC, QT]).then_inc(stored, 16)
                sp.wait_ge(dve_steps, 23)
                for t in range(QT):
                    sp.dma_start(k.fox_k_p[lay, 0, t * P:(t + 1) * P], aug[:, t, FOXH:HF, 0:HD])\
                      .then_inc(stored, 16)
                sp.dma_start(k.fox_k_s[lay, 0], aug[0:DEC, QT, FOXH:HF, 0:HD]).then_inc(stored, 16)
                sp.wait_ge(stored, 16 * (5 + QT))

            @block.scalar
            def _(act):
                for t in range(TT):
                    act.activation(aug[:, t, :, 0:HD], qk[:, t], ACT.Square).then_inc(squared, 1)
                act.wait_ge(dve_steps, 2)
                own = Steps(act, act_steps)
                own.after(act.activation(e, ax, ACT.Exp, scale=-1.0))
                act.wait_ge(dve_steps, 3)
                own.after(act.activation(ax, u, ACT.Ln))
                act.wait_ge(dve_steps, 9)
                own.after(act.activation(ss[:, :, :], ss[:, :, :], ACT.Ln, scale=1.0 / HD,
                                         bias=k.const[:, C_EPS:C_EPS + 1]))
                own.after(act.activation(ss[:, :, :], ss[:, :, :], ACT.Exp, scale=-0.5))

            @block.vector
            def _(dve):
                own = Steps(dve, dve_steps)
                own.after(dve.tensor_tensor(x, gate, bcast(k.row[:, R_BF:R_BF + FOXH], [P, TT, FOXH], 1), ALU.add))
                own.after(dve.scalar_tensor_tensor(ax, x, -1.0, x, ALU.mult, ALU.max))
                dve.wait_ge(act_steps, 1)
                own.after(dve.tensor_scalar(u, e, 1.0, None, ALU.add))
                own.after(dve.tensor_scalar(r, u, -1.0, None, ALU.add))
                own.after(dve.tensor_tensor(r, e, r, ALU.subtract))
                own.after(dve.tensor_scalar(x, x, 0.0, None, ALU.min))
                dve.wait_ge(act_steps, 2)
                own.after(dve.tensor_tensor(r, ax, r, ALU.add))
                own.after(dve.tensor_tensor(lf, x, r, ALU.subtract))
                for t in range(TT):
                    dve.wait_ge(squared, t + 1)
                    last = dve.tensor_reduce(ss[:, t, :], aug[:, t, :, 0:HD], AX, ALU.add)
                own.after(last)
                dve.wait_ge(cached, 16)
                dve.memset(cl[32:64, QT, :], 0.0)
                dve.memset(cl[64:128, QT, :], 0.0)
                dve.tensor_copy(cl[0:DEC, QT, :], lf[0:DEC, QT, :])
                own.after(dve.memset(pre[:, :, 0, :], 0.0))
                for t in range(1, TT):
                    if t < QT:
                        dve.tensor_tensor(pre[:, 0, t], pre[:, 0, t - 1], lf[:, t - 1], ALU.add)
                    last = dve.tensor_tensor(pre[:, 1, t], pre[:, 1, t - 1], cl[:, t - 1], ALU.add)
                    own.after(last)
                dve.wait_ge(f_done, 1)
                fp = ps[:, 0, 0:QT * FOXH].rearrange("p (t h) -> p t h", h=FOXH)
                dve.tensor_copy(aug[:, 0:QT, 0:FOXH, HD], fp)
                dve.tensor_scalar(aug[:, 0:QT, FOXH:HF, HD + 1], fp, -1.0, None, ALU.mult)
                dve.memset(aug[:, 0:QT, 0:FOXH, HD + 1], 1.0)
                dve.memset(aug[:, 0:QT, FOXH:HF, HD], 1.0)
                own.after(dve.tensor_copy(fs[:, :, :], ps[:, 1, 0:TT * FOXH].rearrange("p (t h) -> p t h", h=FOXH)))
                dve.wait_ge(act_steps, 4)
                for a, row in ((FOXH, R_FK), (0, R_FQ)):
                    own.after(dve.tensor_tensor(aug[:, :, a:a + FOXH, 0:HD], qk[:, :, a:a + FOXH],
                                                bcast(ss[:, :, a:a + FOXH], [P, TT, FOXH, HD], 3), ALU.mult))
                    own.after(dve.tensor_tensor(aug[:, :, a:a + FOXH, 0:HD], aug[:, :, a:a + FOXH, 0:HD],
                                                bcast(k.row[:, row:row + HD], [P, TT, FOXH, HD], 1, 1), ALU.mult))
                dve.tensor_copy(qk_new[:, :, :], aug[0:DEC, QT, :, 0:HD])

            @block.tensor
            def _(pe):
                pe.wait_ge(dve_steps, 18)
                pe.matmul(ps[:, 0, 0:QT * FOXH], tri, lf[:, 0:QT, :], start=True, stop=False)
                pe.matmul(ps[:, 0, 0:QT * FOXH], ones, pre[:, 0, 0:QT, :], start=False, stop=True)
                pe.matmul(ps[:, 1, 0:TT * FOXH], tri, cl[:, :, :], start=True, stop=False)
                pe.matmul(ps[:, 1, 0:TT * FOXH], ones, pre[:, 1], start=False, stop=True).then_inc(f_done, 1)


def attend_prompt(nc, k, kind, tag, heads, kdim, q_of, k_of, v_of, kv_of, yT, yc):
    N = heads * QT
    swa = kind == "swa"
    with ExitStack() as s:
        qT = [s.enter_context(nc.sbuf_tensor(f"qT{n}{tag}", [96, 2, SEQ], F32R)) for n in ("hi", "lo")]
        kT = [s.enter_context(nc.sbuf_tensor(f"kT{n}{tag}", [96, 2, SEQ], F32R)) for n in ("hi", "lo")]
        NPR = 3
        wid = 2 * P if swa else SEQ
        pr = s.enter_context(nc.sbuf_tensor("pr" + tag, [P, NPR, wid], F32))
        pT = s.enter_context(nc.sbuf_tensor("pT" + tag, [P, 2, wid // P, P], F32))
        st = s.enter_context(nc.sbuf_tensor("st" + tag, [P, 6, N], F32))
        nmax, tot, rtot, sk, zero = st[:, 0], st[:, 1], st[:, 2], st[:, 3], st[:, 5]
        psS = s.enter_context(nc.psum_tensor("psS" + tag, [P, 2, 2 * 512], F32))
        psX = s.enter_context(nc.psum_tensor("psX" + tag, [P, 4, P], F32))
        psT = s.enter_context(nc.psum_tensor("psT" + tag, [P, 8, P], F32))
        psO = s.enter_context(nc.psum_tensor("psO" + tag, [P, 512], F32))
        sem = k.sems["att"]
        (cleared, x_done, x_hi, x_lo, scored, maxed, expd, normed, turned, t_low, t_high, mixed, y_done,
         dve_steps, sunk) = (sem[n] for n in ("clr", "x", "xh", "xl", "s", "m", "e", "n", "t", "tl", "th", "o",
                                             "y", "d", "sk"))
        ident = k.const[:, C_ID:C_ID + P]

        def first(i):
            return max(i - 1, 0) if swa else 0

        def prep(h, g):
            return (qT if g < 2 else kT), (q_of(h) if g < 2 else k_of(kv_of(h))), 4 * (g % 2)

        def groups(m):
            h, i = m // QT + 1, m % QT
            return [(h, i - 2)] if h < heads and 2 <= i < 6 else []

        def high_tiles(m):
            return sum(1 for j in range(m + 1) if j % QT - first(j % QT) >= 4)

        with nc.Block() as block:

            @block.gpsimd
            def _(pool):
                if kdim < 96:
                    for n, t in enumerate((*qT, *kT)):
                        pool.memset(t[64:96].bitcast(F32), 0.0).then_inc(cleared, 1)
                        pool.wait_ge(cleared, n + 1)

            @block.tensor
            def _(pe):
                def turn_group(h, g):
                    n = 4 * h + g
                    dst, src, t0 = prep(h, g)
                    if n:
                        pe.wait_ge(x_lo, n)
                    for t in range(4):
                        last = pe.transpose(psX[0:kdim, t, :], src[:, t0 + t, :], ident)
                    last.then_inc(x_done, 1)

                for g in range(4):
                    turn_group(0, g)
                for m in range(N + 3):
                    if m < N:
                        h, i = divmod(m, QT)
                        pe.wait_ge(x_lo, 4 * h + 4)
                        if m >= 2:
                            pe.wait_ge(expd, m - 1)
                        f, w = first(i) * P, (i + 1 - first(i)) * P
                        for a in range(0, w, 512):
                            n = min(512, w - a)
                            diag = not swa and a + n == w
                            out = psS[:, m % 2, a:a + n]
                            for j, (x, y) in enumerate(((0, 0), (0, 1), (1, 0))):
                                last = pe.matmul(out, qT[x][:, h % 2, i * P:(i + 1) * P],
                                                 kT[y][:, h % 2, f + a:f + a + n],
                                                 start=(j == 0), stop=(j == 2 and not diag))
                            if diag:
                                last = pe.matmul(psS[:, m % 2, w - P:w], k.identr[:, :],
                                                 (k.mfoxr if kind == "fox" else k.mmlar)[:, :],
                                                 start=False, stop=True)
                        last.then_inc(scored, 1)
                        for g in groups(m):
                            turn_group(*g)
                    j = m - 2
                    if 0 <= j < N:
                        i = j % QT
                        pe.wait_ge(normed, j + 1)
                        if j:
                            pe.wait_ge(t_low, j)
                            if high_tiles(j - 1):
                                pe.wait_ge(t_high, high_tiles(j - 1))
                        for b in range(i + 1 - first(i)):
                            last = pe.transpose(psT[:, b, :], pr[:, j % NPR, b * P:(b + 1) * P], ident)
                        last.then_inc(turned, 1)
                    j = m - 3
                    if 0 <= j < N:
                        h, i = divmod(j, QT)
                        e = 64 * (h % 2)
                        pe.wait_ge(t_low, j + 1)
                        if high_tiles(j):
                            pe.wait_ge(t_high, high_tiles(j))
                        if j:
                            pe.wait_ge(y_done, j)
                        nb = i + 1 - first(i)
                        for b in range(nb):
                            last = pe.matmul(psO[e:e + HD, 0:P], v_of(kv_of(h), first(i) + b), pT[:, j % 2, b, :],
                                             start=(b == 0), stop=(b == nb - 1))
                        last.then_inc(mixed, 1)

            @block.scalar
            def _(act):
                def high_part(h, g):
                    dst, _, t0 = prep(h, g)
                    act.wait_ge(x_done, 4 * h + g + 1)
                    act.activation(dst[0][0:kdim, h % 2, t0 * P:(t0 + 4) * P],
                                   psX[0:kdim, :, :].rearrange("p t n -> p (t n)"), ACT.Copy).then_inc(x_hi, 1)

                if kdim < 96:
                    act.wait_ge(cleared, 4)
                for g in range(4):
                    high_part(0, g)
                for m in range(N + 3):
                    if m < N:
                        i = m % QT
                        w = (i + 1 - first(i)) * P
                        act.wait_ge(maxed, m + 1)
                        if m >= NPR:
                            act.wait_ge(turned, m - NPR + 1)
                        act.activation(pr[:, m % NPR, 0:w], psS[:, m % 2, 0:w], ACT.Exp, bias=nmax[:, m:m + 1],
                                       accum_out=tot[:, m:m + 1]).then_inc(expd, 1)
                        if swa:
                            act.activation(sk[:, m:m + 1], nmax[:, m:m + 1], ACT.Exp,
                                           bias=k.row[:, R_SINK + m // QT:R_SINK + m // QT + 1]).then_inc(sunk, 1)
                        for g in groups(m):
                            high_part(*g)
                    j = m - 2
                    if 0 <= j < N:
                        i = j % QT
                        nb = min(4, i + 1 - first(i))
                        act.wait_ge(turned, j + 1)
                        if j >= 2:
                            act.wait_ge(mixed, j - 1)
                        act.activation(pT[:, j % 2, 0:nb, :], psT[:, 0:nb, :], ACT.Copy).then_inc(t_low, 1)
                    j = m - 3
                    if 0 <= j < N:
                        h, i = divmod(j, QT)
                        e = 64 * (h % 2)
                        act.wait_ge(mixed, j + 1)
                        act.activation(yT[e:e + HD, yc + h // 2, i * P:(i + 1) * P], psO[e:e + HD, 0:P], ACT.Copy)\
                           .then_inc(y_done, 1)

            @block.vector
            def _(dve):
                own = Steps(dve, dve_steps)

                def low_part(h, g):
                    dst, _, t0 = prep(h, g)
                    dve.wait_ge(x_hi, 4 * h + g + 1)
                    at = slice(t0 * P, (t0 + 4) * P)
                    dve.tensor_tensor(dst[1][0:kdim, h % 2, at], psX[0:kdim, :, :].rearrange("p t n -> p (t n)"),
                                      dst[0][0:kdim, h % 2, at].bitcast(F32), ALU.subtract).then_inc(x_lo, 1)

                if kdim < 96:
                    dve.wait_ge(cleared, 4)
                for g in range(4):
                    low_part(0, g)
                for m in range(N + 2):
                    if m < N:
                        h, i = divmod(m, QT)
                        w = (i + 1 - first(i)) * P
                        dve.wait_ge(scored, m + 1)
                        scores = psS[:, m % 2, 0:w]
                        if swa:
                            own.after(dve.scalar_tensor_tensor(
                                scores, k.const[:, C_DIST + 2 * P - w:C_DIST + 2 * P],
                                k.const[:, C_SLOPE + h:C_SLOPE + h + 1], scores, ALU.mult, ALU.add))
                            own.after(dve.reduce_max(zero[:, m:m + 1], scores, AX))
                            dve.tensor_scalar(nmax[:, m:m + 1], zero[:, m:m + 1],
                                              k.row[:, R_SINK + h:R_SINK + h + 1], -1.0, ALU.max, ALU.mult)\
                               .then_inc(maxed, 1)
                        else:
                            dve.tensor_reduce(nmax[:, m:m + 1], scores, AX, ALU.max, negate=True).then_inc(maxed, 1)
                        for g in groups(m):
                            low_part(*g)
                    j = m - 1
                    if 0 <= j < N:
                        i = j % QT
                        w = (i + 1 - first(i)) * P
                        dve.wait_ge(expd, j + 1)
                        if swa:
                            dve.wait_ge(sunk, j + 1)
                            own.after(dve.tensor_tensor(tot[:, j:j + 1], tot[:, j:j + 1], sk[:, j:j + 1], ALU.add))
                        own.after(dve.reciprocal(rtot[:, j:j + 1], tot[:, j:j + 1]))
                        dve.tensor_scalar(pr[:, j % NPR, 0:w], pr[:, j % NPR, 0:w], rtot[:, j:j + 1], None,
                                          ALU.mult).then_inc(normed, 1)
                    j = m - 2
                    if 0 <= j < N and j % QT - first(j % QT) >= 4:
                        nb = j % QT + 1
                        dve.wait_ge(turned, j + 1)
                        if j >= 2:
                            dve.wait_ge(mixed, j - 1)
                        dve.tensor_copy(pT[:, j % 2, 4:nb, :], psT[:, 4:nb, :]).then_inc(t_high, 1)
    restart(nc, k.lists["att"])


def attend_sample(nc, k, kind, heads, q_new, kunits, kdim, row_of, tiles, loads, yT, yc, fs=None):
    mla, fox = kind == "mla", kind == "fox"
    keys = sum(t[0] for t in tiles)
    offs = [sum(t[0] for t in tiles[:n]) for n in range(len(tiles))]
    pw = keys if keys <= 512 else keys // 3
    NPC = keys // pw
    G = (heads + 3) // 4
    pairs = heads // 2
    qunits = heads if mla else pairs
    jobs = [(u, list(range(a, min(a + 4, len(tiles))))) for u in range(kunits) for a in range(0, len(tiles), 4)]
    if fox:
        jobs += [("f", list(range(a, min(a + 4, len(tiles))))) for a in range(0, len(tiles), 4)]
    pjobs = [(g, list(range(a, min(a + 4, len(tiles))))) for g in range(G) for a in range(0, len(tiles), 4)]
    J, PJ = len(jobs), len(pjobs) // G
    rows = [32 * min(4, heads - 4 * g) for g in range(G)]
    with ExitStack() as s:
        T = lambda n, shape: s.enter_context(nc.sbuf_tensor(n + "_s" + kind, shape, F32))
        kT = T("kT", [P, kunits, keys])
        qz = T("qz", [P, qunits, DEC if mla else 2 * DEC])
        pr = T("pr", [P, G, keys])
        pT = T("pT", [P, G, len(tiles), P])
        st = T("st", [P, 4, G])
        mx, tot, rtot, sk = (st[:, n] for n in range(4))
        sink = T("sink", [P, 2])
        if fox:
            rb, lb, fq = T("rb", [64, keys]), T("lb", [64, G * P]), T("fq", [64, DEC])
        psS = s.enter_context(nc.psum_tensor("psS_s" + kind, [P, NPC, 512], F32))
        psX = s.enter_context(nc.psum_tensor("psX_s" + kind, [P, 2, 4, P], F32))
        psQ = s.enter_context(nc.psum_tensor("psQ_s" + kind, [P, 4, P], F32))
        psO = s.enter_context(nc.psum_tensor("psO_s" + kind, [P, 2, 512], F32))
        sem = k.sems["smp"]
        (cache_in, zeroed, q_turned, q_done, x_done, x_out, k_ready, scored, dve_steps, maxed, expd, normed,
         t_done, t_out, mixed, y_done) = (sem[n] for n in ("in", "z", "qt", "qd", "x", "xo", "k", "s", "d", "m",
                                                           "e", "n", "t", "to", "o", "y"))
        ident = k.const[:, C_ID:C_ID + P]

        engines = (nc.scalar, nc.vector)

        def unload(eng, b):
            for j in range(b, J, 2):
                u, ts = jobs[j]
                c0, w = offs[ts[0]], sum(tiles[t][0] for t in ts)
                eng.wait_ge(x_done, j + 1)
                n = FOXH if u == "f" else (kdim if mla else P)
                full = [t for t in ts if tiles[t][0] == P]
                parts = ([(0, len(full))] if full else []) + [(ts.index(t), 0) for t in ts if tiles[t][0] < P]
                for m, (i, cnt) in enumerate(parts):
                    o = offs[ts[i]]
                    if cnt:
                        src = psX[0:n, b, i:i + cnt, :].rearrange("p t n -> p (t n)")
                        ww = cnt * P
                    else:
                        ww = tiles[ts[i]][0]
                        src = psX[0:n, b, i, 0:ww]
                    dst = rb[0:n, o:o + ww] if u == "f" else kT[0:n, u, o:o + ww]
                    sc = -1.0 if u == "f" else 1.0
                    if u == "f" and len(tiles) - 1 in ts and not cnt:
                        copy(eng, fq[32:32 + FOXH, :], src, 1.0)
                    last = copy(eng, dst, src, sc)
                last.then_inc(x_out[b], 1)

        def copy(eng, dst, src, scale):
            if eng is engines[0]:
                return eng.activation(dst, src, ACT.Copy, scale=scale)
            return eng.tensor_scalar(dst, src, scale, None, ALU.mult)

        def unload_p(eng, j):
            g, ts = pjobs[j]
            eng.wait_ge(t_done, j + 1)
            full = [t for t in ts if tiles[t][0] == P]
            if full:
                last = copy(eng, pT[:, g, full[0]:full[-1] + 1, 0:rows[g]],
                            psX[:, j % 2, 0:len(full), 0:rows[g]], 1.0)
            for t in ts:
                if tiles[t][0] < P:
                    r = tiles[t][0]
                    last = copy(eng, pT[0:r, g, t, 0:rows[g]],
                                psX[0:r, j % 2, ts.index(t), 0:rows[g]], 1.0)
            last.then_inc(t_out[j % 2], 1)

        with nc.Block() as block:

            @block.sync
            def _(sp):
                for dst, src in loads:
                    sp.dma_start(dst, src).then_inc(cache_in, 16)

            @block.gpsimd
            def _(pool):
                pool.memset(qz[:, :, :], 0.0).then_inc(zeroed, 1)
                if fox:
                    for n, (rows, value) in enumerate(((rb[0:32, :], 0.0), (rb[32:64, :], 1.0), (fq[32:64, :], 0.0))):
                        pool.wait_ge(zeroed, n + 1)
                        pool.memset(rows, value).then_inc(zeroed, 1)

            @block.tensor
            def _(pe):
                for u in range(qunits):
                    n = kdim if mla else P
                    last = pe.transpose(psQ[0:n, u, 0:DEC], q_new(u), ident[0:DEC, 0:DEC])
                last.then_inc(q_turned, 1)
                pe.wait_ge(cache_in, 16 * len(loads))
                for j, (u, ts) in enumerate(jobs):
                    if j >= 2:
                        pe.wait_ge(x_out[j % 2], j // 2)
                    for n, t in enumerate(ts):
                        r = tiles[t][0]
                        src = fs[0:r, t, :] if u == "f" else tiles[t][1](u)
                        c = FOXH if u == "f" else (kdim if mla else P)
                        last = pe.transpose(psX[0:c, j % 2, n, 0:r], src, ident[0:r, 0:r])
                    last.then_inc(x_done, 1)
                pe.wait_ge(x_out[0], (J + 1) // 2)
                pe.wait_ge(x_out[1], J // 2)
                pe.wait_ge(q_done, 1)
                for g in range(G):
                    if g:
                        pe.wait_ge(expd, g)
                    for a in range(NPC):
                        at = slice(a * pw, (a + 1) * pw)
                        if fox:
                            pe.matmul(psS[0:rows[g], a, 0:pw], lb[:, g * P:g * P + rows[g]], rb[:, at],
                                      start=True, stop=False, skip_group_check=True)
                        if mla:
                            for h in range(4):
                                last = pe.matmul(psS[32 * h:32 * h + DEC, a, 0:pw], qz[0:kdim, h, :],
                                                 kT[0:kdim, h, at], start=True, stop=True)
                        else:
                            for p in range(2 * g, min(2 * g + 2, pairs)):
                                e = 64 * (p % 2)
                                last = pe.matmul(psS[e:e + 64, a, 0:pw], qz[:, p, :], kT[:, p if fox else 0, at],
                                                 start=not fox, stop=True, skip_group_check=True)
                    last.then_inc(scored, 1)
                for j, (g, ts) in enumerate(pjobs):
                    pe.wait_ge(normed, g + 1)
                    if j >= 2:
                        pe.wait_ge(t_out[j % 2], j // 2)
                    for n, t in enumerate(ts):
                        r = tiles[t][0]
                        last = pe.transpose(psX[0:r, j % 2, n, 0:rows[g]], pr[0:rows[g], g, offs[t]:offs[t] + r],
                                            ident[0:rows[g], 0:rows[g]])
                    last.then_inc(t_done, 1)
                pe.wait_ge(t_out[0], (len(pjobs) + 1) // 2)
                pe.wait_ge(t_out[1], len(pjobs) // 2)
                for p in range(pairs):
                    g, e = p // 2, 64 * (p % 2)
                    if p >= 2:
                        pe.wait_ge(y_done, 2 * (p - 1))
                    for t, (r, _, v) in enumerate(tiles):
                        last = pe.matmul(psO[:, p % 2, 0:2 * DEC], v(p), pT[0:r, g, t, e:e + 64],
                                         start=(t == 0), stop=(t == len(tiles) - 1))
                    last.then_inc(mixed, 1)

            @block.scalar
            def _(act):
                if fox:
                    act.wait_ge(zeroed, 4)
                unload(engines[0], 0)
                for g in range(G):
                    act.wait_ge(maxed, g + 1)
                    last = act.activation(pr[0:rows[g], g, :].rearrange("p (a n) -> p a n", a=NPC),
                                          psS[0:rows[g], :, 0:pw], ACT.Exp, bias=mx[0:rows[g], g:g + 1],
                                          accum_out=tot[0:rows[g], g:g + 1])
                    if kind == "swa":
                        last = act.activation(sk[0:rows[g], g:g + 1], mx[0:rows[g], g:g + 1], ACT.Exp,
                                              bias=sink[0:rows[g], g:g + 1])
                    last.then_inc(expd, 1)
                for j in range(0, len(pjobs), 2):
                    unload_p(engines[0], j)

            @block.vector
            def _(dve):
                own = Steps(dve, dve_steps)
                dve.wait_ge(q_turned, 1)
                dve.wait_ge(zeroed, 1)
                if mla:
                    last = dve.tensor_copy(qz[0:kdim, :, :], psQ[0:kdim, 0:4, 0:DEC])
                else:
                    for h in range(heads):
                        e, r = 64 * (h % 2), row_of(h)
                        last = dve.tensor_copy(qz[r:r + HD, h // 2, DEC * (h % 2):DEC * (h % 2 + 1)],
                                               psQ[e:e + HD, h // 2, 0:DEC])
                if not fox:
                    last.then_inc(q_done, 1)
                if kind == "swa":
                    for g in range(G):
                        for h in range(4 * g, min(4 * g + 4, heads)):
                            e = 32 * (h % 4)
                            last = dve.tensor_copy(sink[e:e + 32, g:g + 1], k.row[e:e + 32, R_SINK + h:R_SINK + h + 1])
                    own.after(last)
                if fox:
                    dve.wait_ge(zeroed, 4)
                unload(engines[1], 1)
                if fox:
                    dve.wait_ge(x_out[0], (J + 1) // 2)
                    dve.wait_ge(x_out[1], J // 2)
                    dve.tensor_copy(lb[0:32, :], k.const[0:32, C_SEL:C_SEL + G * P])
                    dve.tensor_tensor(lb[32:64, :].rearrange("p (a n) -> p a n", n=DEC),
                                      k.const[32:64, C_SEL:C_SEL + G * P].rearrange("p (a n) -> p a n", n=DEC),
                                      bcast(fq[32:64, :], [32, G * 4, DEC], 1), ALU.mult).then_inc(q_done, 1)
                for g in range(G):
                    R = rows[g]
                    dve.wait_ge(scored, g + 1)
                    if fox:
                        new = psS[0:R, NPC - 1, pw - DEC:pw]
                        own.after(dve.tensor_tensor(new, new, k.const[0:R, C_MNEW:C_MNEW + DEC], ALU.add))
                    if kind == "swa":
                        b = k.const[0:R, C_BSW + g * SKEYS:C_BSW + (g + 1) * SKEYS]
                        own.after(dve.tensor_tensor(psS[0:R, 0, 0:pw], psS[0:R, 0, 0:pw], b, ALU.add))
                    own.after(dve.reduce_max(mx[0:R, g:g + 1], psS[0:R, :, 0:pw], mybir.AxisListType.XY))
                    if kind == "swa":
                        own.after(dve.tensor_tensor(mx[0:R, g:g + 1], mx[0:R, g:g + 1], sink[0:R, g:g + 1], ALU.max))
                    dve.tensor_scalar(mx[0:R, g:g + 1], mx[0:R, g:g + 1], -1.0, None, ALU.mult).then_inc(maxed, 1)
                for g in range(G):
                    R = rows[g]
                    dve.wait_ge(expd, g + 1)
                    if kind == "swa":
                        own.after(dve.tensor_tensor(tot[0:R, g:g + 1], tot[0:R, g:g + 1], sk[0:R, g:g + 1], ALU.add))
                    own.after(dve.reciprocal(rtot[0:R, g:g + 1], tot[0:R, g:g + 1]))
                    dve.tensor_scalar(pr[0:R, g, :], pr[0:R, g, :], rtot[0:R, g:g + 1], None, ALU.mult)\
                       .then_inc(normed, 1)
                for j in range(1, len(pjobs), 2):
                    unload_p(engines[1], j)
                for p in range(pairs):
                    dve.wait_ge(mixed, p + 1)
                    for h in (2 * p, 2 * p + 1):
                        e, r, c = 64 * (h % 2), row_of(h), DEC * (h % 2)
                        dve.tensor_copy(yT[e:e + HD, yc + p, SEQ:TOK], psO[r:r + HD, p % 2, c:c + DEC])\
                           .then_inc(y_done, 1)
    restart(nc, k.lists["smp"])


def swa_prepare(nc, k, lay, proj):
    NH = SWAH + SWAKV
    with ExitStack() as s:
        sq = s.enter_context(nc.sbuf_tensor("ssq", [P, TT, NH, HD], F32))
        ss = s.enter_context(nc.sbuf_tensor("sss", [P, TT, NH], F32))
        sem = k.sems["swa"]
        stored, squared, summed, act_steps, dve_steps = (sem[n] for n in ("st", "sq", "sum", "act", "dve"))
        qk = proj[:, :, O_SQ:O_SV].rearrange("p t (h d) -> p t h d", d=HD)
        with nc.Block() as block:

            @block.sync
            def _(sp):
                def out(dst, src):
                    sp.dma_start(dst, src).then_inc(stored, 16)
                for new, cache, o in ((k.swa_k_s, k.cache_swa_k, O_SK), (k.swa_v_s, k.cache_swa_v, O_SV)):
                    out(new[lay, 0, 0:WIN - DEC], cache[lay, 0, DEC:WIN])
                kv = lambda r, t, o: proj[0:r, t, o:o + SWAKV * HD]
                out(k.swa_v_s[lay, 0, WIN - DEC:WIN].rearrange("t h d -> t (h d)"), kv(DEC, QT, O_SV))
                out(k.swa_v_p[lay, 0].rearrange("t h d -> t (h d)"), kv(P, QT - 1, O_SV))
                sp.wait_ge(dve_steps, 2)
                out(k.swa_k_s[lay, 0, WIN - DEC:WIN].rearrange("t h d -> t (h d)"), kv(DEC, QT, O_SK))
                out(k.swa_k_p[lay, 0].rearrange("t h d -> t (h d)"), kv(P, QT - 1, O_SK))
                sp.wait_ge(stored, 16 * 6)

            @block.scalar
            def _(act):
                for t in range(TT):
                    act.activation(sq[:, t], qk[:, t], ACT.Square).then_inc(squared, 1)
                own = Steps(act, act_steps)
                act.wait_ge(summed, TT)
                own.after(act.activation(ss[:, :, :], ss[:, :, :], ACT.Ln, scale=1.0 / HD,
                                         bias=k.const[:, C_EPS:C_EPS + 1]))
                own.after(act.activation(ss[:, :, :], ss[:, :, :], ACT.Exp, scale=-0.5))

            @block.vector
            def _(dve):
                own = Steps(dve, dve_steps)
                for t in range(TT):
                    dve.wait_ge(squared, t + 1)
                    dve.tensor_reduce(ss[:, t, :], sq[:, t], AX, ALU.add).then_inc(summed, 1)
                dve.wait_ge(act_steps, 2)
                for a, n, row in ((SWAH, SWAKV, R_SK), (0, SWAH, R_SQ)):
                    v = qk[:, :, a:a + n]
                    own.after(dve.tensor_tensor(v, v, bcast(ss[:, :, a:a + n], [P, TT, n, HD], 3), ALU.mult))
                    own.after(dve.tensor_tensor(v, v, bcast(k.row[:, row:row + HD], [P, TT, n, HD], 1, 1), ALU.mult))


def mla_prepare(nc, k, lay, proj, qm, km, vm):
    KT = 2 * QT + 1
    half = ROPE // 2
    with ExitStack() as s:
        T = lambda n, shape: s.enter_context(nc.sbuf_tensor("m" + n, shape, F32))
        ckc, krc = T("ckc", [P, QT, KVLORA]), T("krc", [P, QT, ROPE])
        wuq, wukv = T("wuq", [P, 2, MLAH * MQK]), T("wukv", [P, 512])
        lat = km[:, 0:TT].rearrange("p t h e -> p t (h e)")
        ss = T("ss", [P, 2, TT])
        cT = T("cT", [P, 2, 3, P])
        rot = T("rot", [P, 2, TT, MLAH, half])
        sq = T("sq", [P, 2, MLAH, MQK])
        hs = T("hs", [P, 2, KT, MLAH])
        psX = s.enter_context(nc.psum_tensor("mpsX", [P, 2, 512], F32))
        psQ = s.enter_context(nc.psum_tensor("mpsQ", [P, 2, 512], F32))
        psK = s.enter_context(nc.psum_tensor("mpsK", [P, 2, 512], F32))
        sem = k.sems["mla"]
        (w_in, c_in, stored, squared, act_steps, d, turned, x_out, q_done, k_done, q_out, k_out, h_sq, h_sum, a2) = (
            sem[n] for n in ("w", "c", "st", "sq", "act", "dve", "t", "xo", "q", "k", "qo", "ko", "hsq", "hsum", "a2"))
        ident = k.const[:, C_ID:C_ID + P]
        cos = k.const[:, C_COS:C_SIN].rearrange("p (t n) -> p t n", n=half)
        sin = k.const[:, C_SIN:C_SLOPE].rearrange("p (t n) -> p t n", n=half)
        cq, ckv, kr = (proj[:, :, a:b] for a, b in ((O_CQ, O_CKV), (O_CKV, O_KR), (O_KR, IN_W)))

        def latents(j):
            if j < QT:
                return P, j
            return (P, None) if j < 2 * QT else (DEC, QT)

        with nc.Block() as block:

            @block.sync
            def _(sp):
                sp.dma_start(wuq[:, :, :], k.w_mla_uq[lay].rearrange("(c p) n -> p c n", p=P)).then_inc(w_in, 16)
                sp.dma_start(wukv[:, :], k.w_mla_ukv[lay]).then_inc(w_in, 16)
                sp.dma_start(ckc[:, :, :], k.cache_mla_ckv[lay, 0].rearrange("(t p) n -> p t n", p=P)).then_inc(c_in, 16)
                sp.dma_start(krc[:, :, :], k.cache_mla_krope[lay, 0].rearrange("(t p) n -> p t n", p=P)).then_inc(c_in, 16)
                sp.wait_ge(d, 12)
                for dst, dst_s, src in ((k.mla_ckv_p, k.mla_ckv_s, ckv), (k.mla_krope_p, k.mla_krope_s, kr)):
                    sp.dma_start(dst[lay, 0].rearrange("(t p) n -> p t n", p=P), src[:, 0:QT]).then_inc(stored, 16)
                    sp.dma_start(dst_s[lay, 0], src[0:DEC, QT]).then_inc(stored, 16)
                sp.wait_ge(stored, 64)

            @block.scalar
            def _(act):
                own = Steps(act, act_steps)
                eps = k.const[:, C_EPS:C_EPS + 1]
                own.after(act.activation(lat[:, :, 0:2 * P], cq, ACT.Square))
                own.after(act.activation(lat[:, :, 2 * P:3 * P], ckv, ACT.Square))
                act.wait_ge(d, 2)
                own.after(act.activation(ss[:, 0], ss[:, 0], ACT.Ln, scale=1.0 / QLORA, bias=eps))
                own.after(act.activation(ss[:, 1], ss[:, 1], ACT.Ln, scale=1.0 / KVLORA, bias=eps))
                own.after(act.activation(ss[:, :, :], ss[:, :, :], ACT.Exp, scale=-0.5))
                for j in range(KT):
                    n, t = latents(j)
                    act.wait_ge(turned, j + 1)
                    if j >= 2:
                        act.wait_ge(k_done, j - 1)
                    c0 = 0 if t is not None else 2
                    act.activation(cT[:, j % 2, c0:3, 0:n],
                                   psX[:, j % 2, 0:3 * P].rearrange("p (c n) -> p c n", n=P)[:, c0:3, 0:n],
                                   ACT.Copy).then_inc(x_out, 1)
                    act.wait_ge(k_done, j + 1)
                    kv = psK[0:n, j % 2, :].rearrange("p (h e) -> p h e", e=NOPE + HD)
                    act.activation(km[0:n, j, :, 0:NOPE], kv[:, :, 0:NOPE], ACT.Copy)
                    act.activation(vm[0:n, j, :, :], kv[:, :, NOPE:], ACT.Copy).then_inc(k_out, 1)
                act.wait_ge(k_out, KT)
                for x, cnt, sel in ((km, KT, 1), (qm, TT, 0)):
                    if sel == 0:
                        act.wait_ge(d, 24)
                    else:
                        act.wait_ge(d, 17)
                    for t in range(cnt):
                        i = t + (KT if sel == 0 else 0)
                        if i >= 2:
                            act.wait_ge(h_sum, i - 1)
                        act.activation(sq[:, i % 2], x[:, t], ACT.Square).then_inc(h_sq, 1)
                act.wait_ge(h_sum, KT + TT)
                o2 = Steps(act, a2)
                act.activation(hs[:, 0, 0:TT], hs[:, 0, 0:TT], ACT.Ln, scale=1.0 / MQK, bias=eps)
                o2.after(act.activation(hs[:, 1], hs[:, 1], ACT.Ln, scale=1.0 / MQK, bias=eps))
                act.activation(hs[:, 0, 0:TT], hs[:, 0, 0:TT], ACT.Exp, scale=-0.5)
                o2.after(act.activation(hs[:, 1], hs[:, 1], ACT.Exp, scale=-0.5))

            @block.vector
            def _(dve):
                own = Steps(dve, d)
                dve.wait_ge(act_steps, 2)
                own.after(dve.tensor_reduce(ss[:, 0], lat[:, :, 0:2 * P], AX, ALU.add))
                own.after(dve.tensor_reduce(ss[:, 1], lat[:, :, 2 * P:3 * P], AX, ALU.add))
                x1, x2 = kr[:, :, 0:half], kr[:, :, half:]
                r = [rot[:, a, :, b, :] for a in range(2) for b in range(2)]
                own.after(dve.tensor_tensor(r[0], x1, cos, ALU.mult))
                own.after(dve.tensor_tensor(r[1], x2, sin, ALU.mult))
                own.after(dve.tensor_tensor(r[2], x1, sin, ALU.mult))
                own.after(dve.tensor_tensor(r[3], x2, cos, ALU.mult))
                own.after(dve.tensor_tensor(x1, r[0], r[1], ALU.subtract))
                own.after(dve.tensor_tensor(x2, r[2], r[3], ALU.add))
                dve.wait_ge(act_steps, 5)
                for n, (x, a, row) in enumerate(((cq, QLORA, R_CQ), (ckv, KVLORA, R_CKV))):
                    own.after(dve.tensor_tensor(x, x, bcast(ss[:, n], [P, TT, a], 2), ALU.mult))
                    own.after(dve.tensor_tensor(x, x, bcast(k.row[:, row:row + a], [P, TT, a], 1), ALU.mult))
                dve.wait_ge(c_in, 32)
                own.after(dve.tensor_copy(km[:, 0:QT, :, NOPE:], bcast(kr[:, 0:QT], [P, QT, MLAH, ROPE], 2)))
                own.after(dve.tensor_copy(km[:, QT:2 * QT, :, NOPE:], bcast(krc[:, :, :], [P, QT, MLAH, ROPE], 2)))
                own.after(dve.memset(km[32:64, 2 * QT, :, :], 0.0))
                own.after(dve.memset(km[64:128, 2 * QT, :, :], 0.0))
                dve.tensor_copy(km[0:DEC, 2 * QT, :, NOPE:], bcast(kr[0:DEC, QT], [DEC, MLAH, ROPE], 1))
                dve.memset(qm[32:64, QT, :, :], 0.0)
                own.after(dve.memset(qm[64:128, QT, :, :], 0.0))
                for t in range(TT):
                    n = P if t < QT else DEC
                    dve.wait_ge(q_done, t + 1)
                    last = dve.tensor_copy(qm[0:n, t].rearrange("p h e -> p (h e)"), psQ[0:n, t % 2, 0:MLAH * MQK])
                    last.then_inc(q_out, 1)
                dve.wait_ge(k_out, KT)
                dve.wait_ge(q_out, TT)
                x1, x2 = qm[:, :, :, NOPE:NOPE + half], qm[:, :, :, NOPE + half:]
                cb, sb = (bcast(a, [P, TT, MLAH, half], 2) for a in (cos, sin))
                own.after(dve.tensor_tensor(rot[:, 0], x1, cb, ALU.mult))
                own.after(dve.tensor_tensor(rot[:, 1], x2, sb, ALU.mult))
                own.after(dve.tensor_tensor(rot[:, 0], rot[:, 0], rot[:, 1], ALU.subtract))
                own.after(dve.tensor_tensor(rot[:, 1], x1, sb, ALU.mult))
                own.after(dve.tensor_copy(x1, rot[:, 0]))
                own.after(dve.tensor_tensor(rot[:, 0], x2, cb, ALU.mult))
                own.after(dve.tensor_tensor(x2, rot[:, 0], rot[:, 1], ALU.add))
                for t in range(KT + TT):
                    dve.wait_ge(h_sq, t + 1)
                    dst = hs[:, 1, t] if t < KT else hs[:, 0, t - KT]
                    dve.tensor_reduce(dst, sq[:, t % 2], AX, ALU.add).then_inc(h_sum, 1)
                dve.wait_ge(a2, 2)
                for x, n, cnt, row in ((qm, 0, TT, R_MQ), (km, 1, KT, R_MK)):
                    own.after(dve.tensor_tensor(x[:, :, :, :], x[:, :, :, :], bcast(hs[:, n, 0:cnt], [P, cnt, MLAH, MQK], 3), ALU.mult))
                    own.after(dve.tensor_tensor(x[:, :, :, :], x[:, :, :, :], bcast(k.row[:, row:row + MQK], [P, cnt, MLAH, MQK], 1, 1), ALU.mult))

            @block.tensor
            def _(pe):
                pe.wait_ge(c_in, 32)
                pe.wait_ge(w_in, 32)
                pe.wait_ge(d, 12)

                def turn(j):
                    n, t = latents(j)
                    if j >= 2:
                        pe.wait_ge(x_out, j - 1)
                    for c in range(3):
                        if t is None and c < 2:
                            continue
                        src = (ckc[:, j - QT, :] if t is None else
                               (cq[0:n, t, c * P:(c + 1) * P] if c < 2 else ckv[0:n, t, :]))
                        last = pe.transpose(psX[:, j % 2, c * P:c * P + n], src, ident[0:n, 0:n])
                    last.then_inc(turned, 1)

                turn(0)
                nq = 0
                for j in range(KT):
                    if j + 1 < KT:
                        turn(j + 1)
                    n, t = latents(j)
                    pe.wait_ge(x_out, j + 1)
                    if t is not None:
                        if nq >= 2:
                            pe.wait_ge(q_out, nq - 1)
                        for c in range(2):
                            last = pe.matmul(psQ[0:n, nq % 2, 0:MLAH * MQK], cT[:, j % 2, c, 0:n], wuq[:, c, :],
                                             start=(c == 0), stop=(c == 1))
                        last.then_inc(q_done, 1)
                        nq += 1
                    if j >= 2:
                        pe.wait_ge(k_out, j - 1)
                    pe.matmul(psK[0:n, j % 2, :], cT[:, j % 2, 2, 0:n], wukv[:, :], start=True, stop=True)\
                      .then_inc(k_done, 1)


def project_out(nc, k, lay, hi, lo, xT):
    with ExitStack() as s:
        raw = s.enter_context(nc.sbuf_tensor("oraw", [P, 2, DC, P], F32))
        whi = s.enter_context(nc.sbuf_tensor("ohi", [P, 2, DC, P], F32R))
        wlo = s.enter_context(nc.sbuf_tensor("olo", [P, 2, DC, P], F32R))
        ps = s.enter_context(nc.psum_tensor("ops", [P, 2, NT, 512], F32))
        sem = k.sems["wout"]
        raw_in, hi_done, lo_done, x_in, tile_done, added = (sem[n] for n in ("raw", "hi", "lo", "x", "done", "add"))
        w_dram = k.w_out[lay].rearrange("(c p) n -> p c n", p=P)

        def steps(eng, body):
            with eng.Fori(0, DC // 2) as i:
                for b in range(2):
                    body(i, b)

        with nc.Block() as block:

            @block.sync
            def _(sp):
                sp.dma_start(xT[:, :, :], k.x_dram).then_inc(x_in, 16)

                def body(i, b):
                    sp.wait_ge(lo_done[b], i)
                    sp.dma_start(raw[:, b], w_dram[:, :, bass.ds((2 * i + b) * P, P)]).then_inc(raw_in[b], 16)
                steps(sp, body)

            @block.scalar
            def _(act):
                def body(i, b):
                    act.wait_ge(raw_in[b], 16 * i + 16)
                    act.wait_ge(tile_done[b], i * NT)
                    act.activation(whi[:, b], raw[:, b], ACT.Copy).then_inc(hi_done[b], 1)
                steps(act, body)

            @block.gpsimd
            def _(pool):
                def body(i, b):
                    pool.wait_ge(hi_done[b], i + 1)
                    pool.wait_ge(lo_done[1 - b], i + b)
                    pool.tensor_tensor(wlo[:, b], raw[:, b], whi[:, b].bitcast(F32), ALU.subtract)\
                        .then_inc(lo_done[b], 1)
                steps(pool, body)

            @block.tensor
            def _(pe):
                def body(i, b):
                    pe.wait_ge(lo_done[b], i + 1)
                    for t in range(NT):
                        pe.wait_ge(added[b], i * NT + t)
                        at = slice(t * TN, (t + 1) * TN)
                        for c in range(DC):
                            for m, (w, a) in enumerate(((whi, hi), (wlo, hi), (whi, lo))):
                                last = pe.matmul(ps[:, b, t, 0:TN], w[:, b, c, :], a[:, c, at],
                                                 start=(c == 0 and m == 0), stop=(c == DC - 1 and m == 2))
                        last.then_inc(tile_done[b], 1)
                steps(pe, body)

            @block.vector
            def _(dve):
                dve.wait_ge(x_in, 16)

                def body(i, b):
                    for t in range(NT):
                        dve.wait_ge(tile_done[b], i * NT + (t + 1))
                        x = xT[:, bass.ds(2 * i + b, 1), t * TN:(t + 1) * TN]
                        dve.tensor_tensor(x, x, ps[:, b, t:t + 1, 0:TN], ALU.add).then_inc(added[b], 1)
                steps(dve, body)


def conv_ffn(nc, k, lay, hi, lo, xT):
    PAIRS = FC // 2
    EXT = CW - 1
    RW = TOK + 2 * EXT
    CL = RW - EXT
    SB = SEQ + EXT
    A0, B0, D0, D1, A1, B1 = range(6)
    with ExitStack() as s:
        T = lambda n, shape, dt=F32: s.enter_context(nc.sbuf_tensor("f" + n, shape, dt))
        raw = T("raw", [P, 2, DC, P])
        whi, wlo = T("whi", [P, 6, DC, P], F32R), T("wlo", [P, 6, DC, P], F32R)
        ax = T("ax", [P, 2, RW])
        cb = T("cb", [P, 2, CL])
        uhi, ulo = T("uhi", [P, 2, TOK], F32R), T("ulo", [P, 2, TOK], F32R)
        tail = T("tail", [P, 2 * EXT, FC])
        tl = T("tl", [2 * EXT * FC, P])
        psA = s.enter_context(nc.psum_tensor("fpsA", [P, NT, 512], F32))
        psB = s.enter_context(nc.psum_tensor("fpsB", [P, NT, 512], F32))
        psD = s.enter_context(nc.psum_tensor("fpsD", [P, 2, 512], F32))
        sem = k.sems["ffn"]
        (cleared, raw_in, hi_done, split, a_done, a_out, row_done, conv_steps, conv_done, gelu_done,
         b_done, b_out, u_hi, u_lo, p_done, p_out, t_done, t_out, stored) = (sem[n] for n in (
             "clr", "raw", "hi", "split", "a", "ao", "row", "cs", "conv", "gelu", "b", "bo", "uh", "ul",
             "p", "po", "t", "to", "st"))
        up = k.w_ffn_up[lay].rearrange("(c p) n -> p c n", p=P)
        down = k.w_ffn_down[lay].rearrange("(j p) (m n) -> j p m n", p=P, n=P)
        vcw = k.vec[:, V_CW:V_CB].rearrange("p (w c) -> p w c", c=FC)
        vst = k.vec[:, V_ST:V_N].rearrange("p (t c) -> p t c", c=FC)

        def before(g):
            return 6 * g - 2

        def each_round(eng, body):
            body(0, (A0, B0, A1, B1), 0)
            with eng.Fori(1, PAIRS) as g:
                body(g, (A0, B0, D0, D1, A1, B1), before(g))
            body(PAIRS, (D0, D1), before(PAIRS))

        with nc.Block() as block:

            @block.sync
            def _(sp):
                def body(g, roles, n0):
                    for o, r in enumerate(roles):
                        if r in (D0, D1):
                            src = down[bass.ds(2 * (g - 1) + (r - D0), 1)].rearrange("j p m n -> p (j m) n")
                        else:
                            col = (2 * g + (r >= A1)) * P + (DFF if r in (B0, B1) else 0)
                            src = up[:, :, bass.ds(col, P)]
                        if not (isinstance(g, int) and n0 + o < 2):
                            sp.wait_ge(split, n0 + (o - 1))
                        sp.dma_start(raw[:, o % 2], src).then_inc(raw_in[o % 2], 16)
                each_round(sp, body)
                sp.wait_ge(t_out, 1)
                row = lambda d: d[lay, 0].rearrange("t (c p) -> (t c) p", p=P)
                sp.dma_start(row(k.ffn_conv_p), tl[0:EXT * FC, :]).then_inc(stored, 16)
                sp.dma_start(row(k.ffn_conv_s), tl[EXT * FC:2 * EXT * FC, :]).then_inc(stored, 16)
                sp.wait_ge(p_out[0], 12 * PAIRS)
                sp.wait_ge(p_out[1], 12 * PAIRS)
                sp.dma_start(k.x_dram, xT[:, :, :]).then_inc(stored, 16)
                sp.wait_ge(stored, 48)

            @block.gpsimd
            def _(pool):
                for b in range(2):
                    pool.memset(ax[:, b, 0:EXT], 0.0).then_inc(cleared, 1)
                    pool.wait_ge(cleared, b + 1)

                def body(g, roles, n0):
                    for o, r in enumerate(roles):
                        if not (isinstance(g, int) and n0 + o == 0):
                            pool.wait_ge(split, n0 + o)
                        pool.wait_ge(hi_done, n0 + (o + 1))
                        pool.tensor_tensor(wlo[:, r], raw[:, o % 2], whi[:, r].bitcast(F32), ALU.subtract)\
                            .then_inc(split, 1)
                each_round(pool, body)

            @block.tensor
            def _(pe):
                three = lambda a, b: ((a[0], b[0]), (a[1], b[0]), (a[0], b[1]))

                def up_chunk(g, e, n):
                    first = isinstance(g, int) and g == 0 and e == 0
                    for ps, role, done, out in ((psA, (A0, A1)[e], a_done, a_out), (psB, (B0, B1)[e], b_done, b_out)):
                        pe.wait_ge(split, n + 1 if ps is psA else n + 2)
                        for t in range(NT):
                            if not first:
                                pe.wait_ge(out, 6 * g + (3 * e + t - 2))
                            at = slice(t * TN, (t + 1) * TN)
                            for c in range(DC):
                                for m, (w, x) in enumerate(three((whi, wlo), (hi, lo))):
                                    last = pe.matmul(ps[:, t, 0:TN], w[:, role, c, :], x[:, c, at],
                                                     start=(c == 0 and m == 0), stop=(c == DC - 1 and m == 2))
                            last.then_inc(done, 1)

                def down_pair(g, n):
                    pe.wait_ge(split, n + 2)
                    pe.wait_ge(u_lo, 2 * g)
                    for m in range(DC):
                        for t in range(NT):
                            o = m * NT + t
                            pe.wait_ge(p_out[o % 2], 12 * (g - 1) + o // 2)
                            at = slice(t * TN, (t + 1) * TN)
                            for e in range(2):
                                for i, (w, x) in enumerate(three((whi, wlo), (uhi, ulo))):
                                    last = pe.matmul(psD[:, o % 2, 0:TN], w[:, D0 + e, m, :], x[:, e, at],
                                                     start=(e == 0 and i == 0), stop=(e == 1 and i == 2))
                            last.then_inc(p_done[o % 2], 1)

                def body(g, roles, n0):
                    o = 0
                    if A0 in roles:
                        up_chunk(g, 0, n0)
                        o += 2
                    if D0 in roles:
                        down_pair(g, n0 + o)
                        o += 2
                    if A1 in roles:
                        up_chunk(g, 1, n0 + o)
                each_round(pe, body)
                pe.wait_ge(row_done, FC)
                pe.transpose(psA[0:2 * EXT * FC, 0, 0:P], tail[:, :, :].rearrange("p t c -> p (t c)"),
                             k.const[:, C_ID:C_ID + P]).then_inc(t_done, 1)

            @block.scalar
            def _(act):
                act.wait_ge(cleared, 2)
                rest = SEQ - 2 * TN

                def high_weights(g, roles, o):
                    peeled = isinstance(g, int)
                    for r in roles:
                        at = (6 * g - 2 if peeled and g else 0 if peeled else before(g)) + o
                        half_at = o // 2 if peeled and g == 0 else 3 * g + (o // 2 - 1)
                        act.wait_ge(raw_in[o % 2], 16 * half_at + 16)
                        if not (peeled and g == 0):
                            if r in (A0, B0):
                                act.wait_ge(b_done, 6 * g - 3)
                            elif r in (A1, B1):
                                act.wait_ge(b_done, 6 * g)
                            elif not (peeled and g == 1):
                                act.wait_ge(p_done[1], 12 * g - 12)
                        act.activation(whi[:, r], raw[:, o % 2], ACT.Copy).then_inc(hi_done, 1)
                        o += 1

                def rows_of(g, e):
                    ch = 2 * g + e
                    if not (isinstance(g, int) and g == 0):
                        act.wait_ge(conv_done, 2 * g + (e - 1))
                    act.activation(ax[:, e, SB:SB + EXT], vst[:, :, bass.ds(ch, 1)].rearrange("p t c -> p (t c)"), ACT.Copy)
                    for t in range(NT):
                        act.wait_ge(a_done, 6 * g + (3 * e + t + 1))
                        if t < NT - 1:
                            act.activation(ax[:, e, EXT + t * TN:EXT + (t + 1) * TN], psA[:, t, 0:TN], ACT.Copy)\
                               .then_inc(a_out, 1)
                        else:
                            act.activation(ax[:, e, EXT + t * TN:EXT + SEQ], psA[:, t, 0:rest], ACT.Copy)
                            act.activation(ax[:, e, SB + EXT:RW], psA[:, t, rest:TN], ACT.Copy).then_inc(a_out, 1)
                    act.wait_ge(a_out, 6 * g + (3 * e + NT))
                    tl_v = lambda a: tail[:, a:a + EXT, bass.ds(ch, 1)].rearrange("p t c -> p (t c)")
                    act.activation(tl_v(0), ax[:, e, SEQ:SEQ + EXT], ACT.Copy)
                    act.activation(tl_v(EXT), ax[:, e, RW - EXT:RW], ACT.Copy).then_inc(row_done, 1)
                    act.wait_ge(conv_done, 2 * g + (e + 1))
                    act.activation(cb[:, e, :], cb[:, e, :], ACT.Gelu_apprx_tanh).then_inc(gelu_done, 1)

                def high_of(g, e):
                    act.wait_ge(b_out, 6 * g + (3 * e + NT))
                    if not (isinstance(g, int) and g == 0):
                        act.wait_ge(p_done[1], 12 * g)
                    act.activation(uhi[:, e, 0:SEQ], cb[:, e, 0:SEQ], ACT.Copy)
                    act.activation(uhi[:, e, SEQ:TOK], cb[:, e, SB:CL], ACT.Copy).then_inc(u_hi, 1)

                def body(g, last=False):
                    zero = isinstance(g, int) and g == 0
                    if not zero:
                        high_weights(g, (D0, D1), 2)
                    rows_of(g, 0)
                    high_weights(g, (A1, B1), 2 if zero else 4)
                    high_of(g, 0)
                    if not last:
                        high_weights(g + 1, (A0, B0), 0)
                    rows_of(g, 1)
                    if last:
                        high_weights(PAIRS, (D0, D1), 0)
                    high_of(g, 1)

                high_weights(0, (A0, B0), 0)
                body(0)
                with act.Fori(1, PAIRS - 1) as g:
                    body(g)
                body(PAIRS - 1, last=True)
                act.wait_ge(t_done, 1)
                act.activation(tl[:, :], psA[0:2 * EXT * FC, 0, 0:P], ACT.Copy).then_inc(t_out, 1)

            @block.vector
            def _(dve):
                rest = SEQ - 2 * TN

                def conv_of(g, e):
                    ch = 2 * g + e
                    own = Steps(dve, conv_steps, 4 * g + 2 * e)
                    dve.wait_ge(row_done, 2 * g + (e + 1))
                    if not (isinstance(g, int) and g == 0):
                        dve.wait_ge(u_hi, 2 * g + (e - 1))
                    w = lambda j: vcw[:, j, bass.ds(ch, 1)]
                    c = cb[:, e, :]
                    own.after(dve.tensor_scalar(c, ax[:, e, 0:CL], w(0), k.vec[:, bass.ds(V_CB + ch, 1)], ALU.mult, ALU.add))
                    own.after(dve.scalar_tensor_tensor(c, ax[:, e, 1:1 + CL], w(1), c, ALU.mult, ALU.add))
                    dve.scalar_tensor_tensor(c, ax[:, e, 2:2 + CL], w(2), c, ALU.mult, ALU.add).then_inc(conv_done, 1)

                def gate_of(g, e):
                    dve.wait_ge(gelu_done, 2 * g + (e + 1))
                    for t in range(NT):
                        dve.wait_ge(b_done, 6 * g + (3 * e + t + 1))
                        if t < NT - 1:
                            v = cb[:, e, t * TN:(t + 1) * TN]
                            dve.tensor_tensor(v, v, psB[:, t, 0:TN], ALU.mult).then_inc(b_out, 1)
                        else:
                            v = cb[:, e, t * TN:SEQ]
                            dve.tensor_tensor(v, v, psB[:, t, 0:rest], ALU.mult)
                            v = cb[:, e, SB:CL]
                            dve.tensor_tensor(v, v, psB[:, t, rest:TN], ALU.mult).then_inc(b_out, 1)

                def low_of(g, e):
                    dve.wait_ge(u_hi, 2 * g + (e + 1))
                    dve.tensor_tensor(ulo[:, e, 0:SEQ], cb[:, e, 0:SEQ], uhi[:, e, 0:SEQ].bitcast(F32), ALU.subtract)
                    dve.tensor_tensor(ulo[:, e, SEQ:TOK], cb[:, e, SB:CL], uhi[:, e, SEQ:TOK].bitcast(F32), ALU.subtract)\
                       .then_inc(u_lo, 1)

                def add_pair(g):
                    for m in range(DC):
                        for t in range(NT):
                            o = m * NT + t
                            dve.wait_ge(p_done[o % 2], 12 * (g - 1) + (o // 2 + 1))
                            x = xT[:, m, t * TN:(t + 1) * TN]
                            last = dve.tensor_tensor(x, x, psD[:, o % 2, 0:TN], ALU.add)
                            last.then_inc(p_out[o % 2], 1)

                def body(g, roles, n0):
                    if A0 in roles:
                        conv_of(g, 0)
                        gate_of(g, 0)
                    if D0 in roles:
                        add_pair(g)
                    if A0 in roles:
                        low_of(g, 0)
                        conv_of(g, 1)
                        gate_of(g, 1)
                        low_of(g, 1)
                each_round(dve, body)


def restart(nc, sems):
    with nc.Block() as block:

        @block.gpsimd
        def _(pool):
            for x in sems:
                pool.sem_clear(x)


def program(nc, k):
    alloc = lambda n: nc.alloc_semaphore(n)
    many = lambda n, m: [alloc(f"{n}{i}") for i in range(m)]
    k.sems = {
        "tok": dict(const=alloc("tok_const"), stored=alloc("tok_stored"), a=many("tok_rows", 2),
                    b=many("tok_turned", 2), c=many("tok_copied", 2)),
        "out": dict(x=alloc("out_x"), b=many("out_turned", 2), c=many("out_copied", 2), s=many("out_stored", 2)),
    }
    layer, k.lists = [], {}

    def group(name, singles, several=()):
        d = {n: alloc(f"{name}_{n}") for n in singles.split()}
        for n, m in several:
            d[n] = many(f"{name}_{n}", m)
        for v in d.values():
            layer.extend(v if isinstance(v, list) else [v])
        k.sems[name] = d
        k.lists[name] = [x for v in d.values() for x in (v if isinstance(v, list) else [v])]

    group("vec", "l t r d")
    group("norm", "sq sum ln rs hf hi lo", [("x", DC)])
    group("win", "", [("raw", 2), ("hi", 2), ("lo", 2), ("done", 3), ("tf", 3)])
    group("fox", "cl st sq act dve sum f")
    group("swa", "st sq sum act dve")
    group("mla", "w c st sq act dve t xo q k qo ko hsq hsum a2")
    group("att", "clr x xh xl s m e n t tl th o y d sk")
    group("smp", "in z qt qd x k s d m e n t o y", [("xo", 2), ("to", 2)])
    group("wout", "x", [("raw", 2), ("hi", 2), ("lo", 2), ("done", 2), ("add", 2)])
    group("ffn", "clr hi split a ao row cs conv gelu b bo uh ul t to st", [("raw", 2), ("p", 2), ("po", 2)])

    with ExitStack() as s:
        T = lambda n, shape, dt=F32: s.enter_context(nc.sbuf_tensor(n, shape, dt))
        k.const = T("const", [P, C_N])
        k.identr, k.mfoxr, k.mmlar = (T(n, [P, P], F32R) for n in ("identr", "mfoxr", "mmlar"))
        k.vec, k.row = T("vec", [P, V_N]), T("row", [P, R_N])
        load_tokens(nc, k)
        with nc.Fori(0, DEPTH) as lay:
            one_layer(nc, k, lay)
            restart(nc, layer)
        store_tokens(nc, k)


def one_layer(nc, k, lay):
    left, right = ExitStack(), ExitStack()

    def lt(n, shape, dt=F32, where=left):
        return where.enter_context(nc.sbuf_tensor(n, shape, dt))

    load_vectors(nc, k, lay)
    hi, lo = lt("h_hi", [P, DC, TOK], F32R), lt("h_lo", [P, DC, TOK], F32R)
    with nc.sbuf_tensor("xT1", [P, DC, TOK], F32) as xT:
        norm(nc, k, xT, hi, lo, V_G1, "1", [(0, DC)], load=True)
    proj = right.enter_context(nc.sbuf_tensor("proj", [P, TT, IN_W], F32, side="right"))
    project_in(nc, k, lay, hi, lo, proj)
    left.close()

    yT = lt("yT", [P, DC, TOK])
    with ExitStack() as f:
        fs = f.enter_context(nc.sbuf_tensor("fs", [P, TT, FOXH], F32))
        qk_new = f.enter_context(nc.sbuf_tensor("qk_new", [DEC, 2 * FOXH, HD], F32))
        a = ExitStack()
        aug = a.enter_context(nc.sbuf_tensor("aug", [P, TT, 2 * FOXH, HD + 2], F32))
        fox_prepare(nc, k, lay, proj, aug, fs, qk_new)
        v_of = lambda h, t: proj[:, t, O_FV + HD * h:O_FV + HD * (h + 1)]
        attend_prompt(nc, k, "fox", "fox", FOXH, HD + 2, lambda h: aug[:, :, h, :],
                      lambda h: aug[:, :, FOXH + h, :], v_of, lambda h: h, yT, 0)
        a.close()
        kc = f.enter_context(nc.sbuf_tensor("fkc", [P, QT, FOXH * HD], F32))
        vc = f.enter_context(nc.sbuf_tensor("fvc", [P, QT, FOXH * HD], F32))
        loads = [(dst[:, :, :], src[lay, 0].rearrange("(t p) h d -> p t (h d)", p=P))
                 for dst, src in ((kc, k.cache_fox_k), (vc, k.cache_fox_v))]
        tiles = [(P, lambda u, t=t: kc[:, t, P * u:P * (u + 1)], lambda p, t=t: vc[:, t, P * p:P * (p + 1)])
                 for t in range(QT)]
        tiles.append((DEC, lambda u: qk_new[:, FOXH + 2 * u:FOXH + 2 * u + 2, :].rearrange("p h d -> p (h d)"),
                      lambda p: proj[0:DEC, QT, O_FV + P * p:O_FV + P * (p + 1)]))
        attend_sample(nc, k, "fox", FOXH, lambda u: qk_new[:, 2 * u:2 * u + 2, :].rearrange("p h d -> p (h d)"), FOXH // 2, P,
                      lambda h: HD * (h % 2), tiles, loads, yT, 0, fs)

    swa_prepare(nc, k, lay, proj)
    attend_prompt(nc, k, "swa", "swa", SWAH, HD, lambda h: proj[:, :, O_SQ + HD * h:O_SQ + HD * (h + 1)],
                  lambda g: proj[:, :, O_SK + HD * g:O_SK + HD * (g + 1)],
                  lambda g, t: proj[:, t, O_SV + HD * g:O_SV + HD * (g + 1)], lambda h: h // (SWAH // SWAKV), yT, 3)
    with ExitStack() as f:
        old = WIN - CHUNK
        kc = f.enter_context(nc.sbuf_tensor("skc", [old, P], F32))
        vc = f.enter_context(nc.sbuf_tensor("svc", [old, P], F32))
        loads = [(dst[:, :], src[lay, 0, CHUNK:WIN].rearrange("t h d -> t (h d)"))
                 for dst, src in ((kc, k.cache_swa_k), (vc, k.cache_swa_v))]
        tiles = [(old, lambda u: kc[:, :], lambda p: vc[:, :]),
                 (DEC, lambda u: proj[0:DEC, QT, O_SK:O_SV], lambda p: proj[0:DEC, QT, O_SV:O_CQ])]
        attend_sample(nc, k, "swa", SWAH, lambda u: proj[0:DEC, QT, O_SQ + P * u:O_SQ + P * (u + 1)], 1, P,
                      lambda h: HD * (h // (SWAH // SWAKV)), tiles, loads, yT, 3)

    with ExitStack() as f:
        qm = f.enter_context(nc.sbuf_tensor("qm", [P, TT, MLAH, MQK], F32))
        km = f.enter_context(nc.sbuf_tensor("km", [P, 2 * QT + 1, MLAH, MQK], F32))
        vm = f.enter_context(nc.sbuf_tensor("vm", [P, 2 * QT + 1, MLAH, HD], F32))
        mla_prepare(nc, k, lay, proj, qm, km, vm)
        right.close()
        attend_prompt(nc, k, "mla", "mla", MLAH, MQK, lambda h: qm[:, :, h, :], lambda h: km[:, :, h, :],
                      lambda h, t: vm[:, t, h, :], lambda h: h, yT, 6)
        tiles = [(P if j < QT else DEC, lambda u, j=j: km[0:P if j < QT else DEC, QT + j, u, :],
                  lambda p, j=j: vm[0:P if j < QT else DEC, QT + j, 2 * p:2 * p + 2, :].rearrange("p h d -> p (h d)"))
                 for j in range(TT)]
        attend_sample(nc, k, "mla", MLAH, lambda h: qm[0:DEC, QT, h, :], MLAH, MQK, lambda h: HD * (h % 2), tiles,
                      [], yT, 6)

    with ExitStack() as f:
        hi, lo = (f.enter_context(nc.sbuf_tensor(n, [P, DC, TOK], F32R, side="right")) for n in ("y_hi", "y_lo"))
        norm(nc, k, yT, hi, lo, V_GM, "2", [(0, 3), (3, 6), (6, 8)])
        left.close()
        xT = lt("xT2", [P, DC, TOK])
        project_out(nc, k, lay, hi, lo, xT)
    with ExitStack() as f:
        hi, lo = (f.enter_context(nc.sbuf_tensor(n, [P, DC, TOK], F32R, side="right")) for n in ("g_hi", "g_lo"))
        norm(nc, k, xT, hi, lo, V_G2, "3", [(0, DC)])
        conv_ffn(nc, k, lay, hi, lo, xT)
    left.close()


_INS = ['x_prompt', 'x_sample', 'cache_fox_k', 'cache_fox_v', 'cache_fox_logf', 'cache_swa_k', 'cache_swa_v',
        'cache_mla_ckv', 'cache_mla_krope', 'state_ffn_conv', 'g_norm1', 'w_in', 'b_fox_f', 'g_fox_q', 'g_fox_k',
        'g_swa_q', 'g_swa_k', 'swa_sinks', 'g_mla_cq', 'g_mla_ckv', 'w_mla_uq', 'w_mla_ukv', 'g_mla_q', 'g_mla_k',
        'g_mix_out', 'w_out', 'g_norm2', 'w_ffn_up', 'w_ffn_conv', 'b_ffn_conv', 'w_ffn_down']
_STREAM = lambda T, win: [(DEPTH, 1, T, FOXH, HD), (DEPTH, 1, T, FOXH, HD), (DEPTH, 1, T, FOXH),
                          (DEPTH, 1, win, SWAKV, HD), (DEPTH, 1, win, SWAKV, HD), (DEPTH, 1, T, KVLORA),
                          (DEPTH, 1, T, ROPE), (DEPTH, 1, CW - 1, DFF)]
_PARTS = ['fox_k', 'fox_v', 'fox_logf', 'swa_k', 'swa_v', 'mla_ckv', 'mla_krope', 'ffn_conv']
_OUTS = [('y_prompt', (1, SEQ, D)), ('y_sample', (1, DEC, D))] + \
    [(n + '_p', s) for n, s in zip(_PARTS, _STREAM(SEQ, WIN))] + \
    [(n + '_s', s) for n, s in zip(_PARTS, _STREAM(DEC, WIN))]


def kernel(**inputs):
    import concourse.bacc as _bacc
    from concourse.bass_utils import run_bass_kernel_spmd as _run

    nc = _bacc.Bacc("TRN2", target_bir_lowering=False, num_devices=1)
    arrays = {f"in_{name}": np.ascontiguousarray(inputs[name]) for name in _INS}
    arrays["in_const"] = const_table()
    k = Chip()
    for name in _INS:
        a = arrays[f"in_{name}"]
        ap = nc.dram_tensor(f"in_{name}", a.shape, F32, kind="ExternalInput").ap()
        k.__dict__[name] = ap[0] if name.startswith("x_") else ap
    k.consts = nc.dram_tensor("in_const", (P, C_N), F32, kind="ExternalInput").ap()
    for name, shape in _OUTS:
        ap = nc.dram_tensor(f"out_{name}", shape, F32, kind="ExternalOutput").ap()
        k.__dict__[name] = ap[0] if name.startswith("y_") else ap
    k.x_dram = nc.dram_tensor("x_between", (P, DC, TOK), F32, kind="Internal").ap()
    program(nc, k)
    r = _run(nc, [arrays], core_ids=[0])
    return tuple(r.results[0][f"out_{name}"] for name, _ in _OUTS)
```

```python
import math
from contextlib import ExitStack, contextmanager

import numpy as np
import concourse.bass as bass
from concourse import mybir

F32 = mybir.dt.float32
F32R = mybir.dt.float32r
ACT = mybir.ActivationFunctionType
ALU = mybir.AluOpType
AX = mybir.AxisListType.X

P = 128
D = 1024
SEQ = 1024
DEC = 32
PAST = 1024
DEPTH = 2
TOK = SEQ + DEC
DC = D // P
QT = SEQ // P
TT = QT + 1
NT = 3
TN = TOK // NT
HD = 64
FOXH, SWAH, SWAKV, MLAH = 6, 6, 2, 4
CHUNK = 64
WIN = 128
QLORA, KVLORA, NOPE, ROPE = 256, 128, 64, 32
MQK = NOPE + ROPE
DFF = 2816
FC = DFF // P
CW = 3
EPS = 1e-6
BIG = -1e30
O_FQ, O_FK, O_FV, O_G = 0, 384, 768, 1152
O_SQ, O_SK, O_SV = 1158, 1542, 1670
O_CQ, O_CKV, O_KR = 1798, 2054, 2182
IN_W = 2214
WN = 246
WSTEPS = IN_W // WN
V_G1, V_G2, V_GM, V_CW, V_CB, V_ST = 0, 8, 16, 24, 24 + CW * FC, 24 + (CW + 1) * FC
V_N = V_ST + 2 * FC
R_FQ, R_FK, R_SQ, R_SK = 0, 64, 128, 192
R_CQ, R_CKV, R_MQ, R_MK, R_BF, R_SINK = 256, 512, 640, 736, 832, 838
R_N = 844
SLOPES = [2.0 ** (-8.0 * (h + 1) / SWAH) for h in range(SWAH)]


class Steps:

    def __init__(self, eng, sem, base=0):
        self.eng, self.sem, self.base, self.n = eng, sem, base, 0

    def mark(self, ins):
        ins.then_inc(self.sem, 1)
        self.n += 1
        return self.n

    def wait(self, n):
        self.eng.wait_ge(self.sem, self.base + n)

    def after(self, ins):
        self.wait(self.mark(ins))


def is_first(i):
    return isinstance(i, int) and i == 0


def bcast(ap, shape, *axes):
    for a in axes:
        ap = ap.unsqueeze(a)
    return ap.broadcast_to(shape)


C_ID, C_TRI, C_ONE, C_MFOX, C_MMLA, C_COS = 0, 128, 256, 384, 512, 640
C_SIN = C_COS + TT * ROPE // 2
C_MNEW = C_SIN + TT * ROPE // 2
C_SEL = C_MNEW + DEC
C_BSW = C_SEL + 2 * P
SKEYS = WIN - CHUNK + DEC
C_EPS = C_BSW + 2 * SKEYS
C_N = C_EPS + 1


def const_table():
    c = np.zeros((P, C_N), np.float32)
    p = np.arange(P)
    c[:, C_ID:C_ID + P] = np.eye(P)
    c[:, C_TRI:C_TRI + P] = p[:, None] <= p[None, :]
    c[:, C_ONE:C_ONE + P] = 1
    c[:, C_MFOX:C_MFOX + P] = np.where(p[None, :] <= p[:, None], 0, BIG)
    c[:, C_MMLA:C_MMLA + P] = np.where(p[None, :] // CHUNK <= p[:, None] // CHUNK, 0, BIG)
    half = ROPE // 2
    inv = (np.float32(10000.0) ** (-np.arange(half, dtype=np.float32) / np.float32(half))).astype(np.float32)
    for t in range(TT):
        ang = (np.float32(P * t) + p.astype(np.float32))[:, None] * inv[None, :]
        c[:, C_COS + t * half:C_COS + (t + 1) * half] = np.cos(ang.astype(np.float64))
        c[:, C_SIN + t * half:C_SIN + (t + 1) * half] = np.sin(ang.astype(np.float64))
    q = p % DEC
    c[:, C_MNEW:C_MNEW + DEC] = np.where(np.arange(DEC)[None, :] <= q[:, None], 0, BIG)
    qpos = PAST + q[:, None]
    kpos = PAST - (WIN - CHUNK) + np.arange(SKEYS)[None, :]
    for g in range(2):
        for r in range(P):
            h = 4 * g + r // DEC
            if h < FOXH:
                c[h, C_SEL + g * P + r] = c[32 + h, C_SEL + g * P + r] = 1
                c[r, C_BSW + g * SKEYS:C_BSW + (g + 1) * SKEYS] = -SLOPES[h] * np.abs(qpos[r] - kpos[0])
    c[:, C_EPS] = EPS
    return c


def alibi_table():
    p, j = np.arange(P)[:, None], np.arange(2 * P)[None, :]
    qc, kc = (P + p) // CHUNK, j // CHUNK
    ok = (kc <= qc) & (kc > qc - WIN // CHUNK)
    return np.stack([np.where(ok, -s * np.abs(P + p - j), BIG) for s in SLOPES], 1).astype(np.float32)


class Chip:
    pass


@contextmanager
def x_home(nc, k, name):
    with nc.sbuf_tensor(name, [P, DC, TOK], F32) as place:
        if name == "xT":
            k.xT = place
        yield k.xT


def load_tokens(nc, k):
    with ExitStack() as s:
        xT = s.enter_context(x_home(nc, k, "xT"))
        xin = s.enter_context(nc.sbuf_tensor("xin", [P, 2, D], F32))
        ps = s.enter_context(nc.psum_tensor("xps", [P, 2, DC, P], F32))
        ident = k.const[:, C_ID:C_ID + P]
        sem = k.sems["tok"]
        const_in = sem["const"]
        rows_in, turned, copied = sem["a"], sem["b"], sem["c"]
        with nc.Block() as block:

            @block.sync
            def _(sp):
                sp.dma_start(k.const[:, :], k.consts).then_inc(const_in, 16)
                for t in range(TT):
                    if t >= 2:
                        sp.wait_ge(turned[t % 2], t // 2)
                    n = P if t < QT else DEC
                    src = k.x_prompt[t * P:t * P + n] if t < QT else k.x_sample
                    sp.dma_start(xin[0:n, t % 2, :], src).then_inc(rows_in[t % 2], 16)

            @block.tensor
            def _(pe):
                pe.wait_ge(const_in, 16)
                for t in range(TT):
                    n = P if t < QT else DEC
                    pe.wait_ge(rows_in[t % 2], 16 * (t // 2 + 1))
                    if t >= 2:
                        pe.wait_ge(copied[t % 2], t // 2)
                    for c in range(DC):
                        last = pe.transpose(ps[:, t % 2, c, 0:n], xin[0:n, t % 2, c * P:(c + 1) * P],
                                            ident[0:n, 0:n])
                    last.then_inc(turned[t % 2], 1)

            @block.scalar
            def _(act):
                act.wait_ge(const_in, 16)
                act.activation(k.identr[:, :], k.const[:, C_ID:C_ID + P], ACT.Copy)
                act.activation(k.mfoxr[:, :], k.const[:, C_MFOX:C_MFOX + P], ACT.Copy)
                act.activation(k.mmlar[:, :], k.const[:, C_MMLA:C_MMLA + P], ACT.Copy)
                for t in range(TT):
                    n = P if t < QT else DEC
                    act.wait_ge(turned[t % 2], t // 2 + 1)
                    act.activation(xT[:, :, t * P:t * P + n], ps[:, t % 2, :, 0:n], ACT.Copy)\
                       .then_inc(copied[t % 2], 1)


def store_tokens(nc, k):
    with ExitStack() as s:
        xT = s.enter_context(x_home(nc, k, "xT9"))
        xout = s.enter_context(nc.sbuf_tensor("xout", [P, 2, D], F32))
        ps = s.enter_context(nc.psum_tensor("yps", [P, 2, DC, P], F32))
        ident = k.const[:, C_ID:C_ID + P]
        sem = k.sems["out"]
        turned, copied, stored = sem["b"], sem["c"], sem["s"]
        with nc.Block() as block:

            @block.sync
            def _(sp):
                for t in range(TT):
                    n = P if t < QT else DEC
                    sp.wait_ge(copied[t % 2], t // 2 + 1)
                    dst = k.y_prompt[t * P:t * P + n] if t < QT else k.y_sample
                    sp.dma_start(dst, xout[0:n, t % 2, :]).then_inc(stored[t % 2], 16)
                sp.wait_ge(stored[0], 16 * (TT // 2 + 1))
                sp.wait_ge(stored[1], 16 * (TT // 2))

            @block.tensor
            def _(pe):
                for t in range(TT):
                    n = P if t < QT else DEC
                    if t >= 2:
                        pe.wait_ge(copied[t % 2], t // 2)
                    for c in range(DC):
                        last = pe.transpose(ps[0:n, t % 2, c, :], xT[:, c, t * P:t * P + n], ident)
                    last.then_inc(turned[t % 2], 1)

            @block.scalar
            def _(act):
                for t in range(TT):
                    n = P if t < QT else DEC
                    act.wait_ge(turned[t % 2], t // 2 + 1)
                    if t >= 2:
                        act.wait_ge(stored[t % 2], 16 * (t // 2))
                    act.activation(xout[0:n, t % 2, :], ps[0:n, t % 2, :, :].rearrange("p c n -> p (c n)"),
                                   ACT.Copy).then_inc(copied[t % 2], 1)


class Vectors:

    def __init__(self, nc, k, lay, s):
        self.k, self.lay = k, lay
        self.st = s.enter_context(nc.sbuf_tensor("vstage", [P, 2, P], F32))
        self.ps = s.enter_context(nc.psum_tensor("vps", [P, 2, P], F32))
        sem = k.sems["vec"]
        self.loaded, self.turned, self.rows_in, self.ready, self.scaled = (sem[n] for n in "ltrvd")
        self.rest = V_N - P
        self.feat = [(V_G1, k.g_norm1[lay].rearrange("(c p) -> c p", p=P)),
                     (V_G2, k.g_norm2[lay].rearrange("(c p) -> c p", p=P)),
                     (V_GM, k.g_mix_out[lay].rearrange("(c p) -> c p", p=P)),
                     (V_CW, k.w_ffn_conv[lay].rearrange("w (c p) -> (w c) p", p=P)),
                     (V_CB, k.b_ffn_conv[lay].rearrange("(c p) -> c p", p=P))]
        self.free = [(R_FQ, k.g_fox_q), (R_FK, k.g_fox_k), (R_SQ, k.g_swa_q), (R_SK, k.g_swa_k),
                     (R_CQ, k.g_mla_cq), (R_CKV, k.g_mla_ckv), (R_MQ, k.g_mla_q), (R_MK, k.g_mla_k),
                     (R_BF, k.b_fox_f), (R_SINK, k.swa_sinks)]

    def load(self, sp):
        k, lay, st = self.k, self.lay, self.st
        for at, src in self.feat:
            sp.dma_start(st[at:at + src.shape[0], 0, :], src).then_inc(self.loaded, 16)
        state = k.state_ffn_conv[lay, 0].rearrange("t (c p) -> (t c) p", p=P)
        split = P - V_ST
        sp.dma_start(st[V_ST:P, 0, :], state[0:split]).then_inc(self.loaded, 16)
        sp.dma_start(st[0:self.rest, 1, :], state[split:2 * FC]).then_inc(self.loaded, 16)
        for at, src in self.free:
            sp.dma_start(k.row[:, at:at + src.shape[1]], src[lay].partition_broadcast(P)).then_inc(self.rows_in, 16)

    def turn(self, pe):
        ident, rest = self.k.const[:, C_ID:C_ID + P], self.rest
        pe.wait_ge(self.loaded, 16 * (len(self.feat) + 2))
        pe.transpose(self.ps[:, 0, :], self.st[:, 0, :], ident)
        pe.transpose(self.ps[:, 1, 0:rest], self.st[0:rest, 1, :], ident[0:rest, 0:rest]).then_inc(self.turned, 1)

    def copy(self, act):
        act.wait_ge(self.turned, 1)
        act.activation(self.k.vec[:, 0:P], self.ps[:, 0, :], ACT.Copy)
        act.activation(self.k.vec[:, P:V_N], self.ps[:, 1, 0:self.rest], ACT.Copy).then_inc(self.ready, 1)

    def scale(self, dve):
        row = self.k.row
        dve.wait_ge(self.rows_in, 16 * len(self.free))
        for at, n, d in ((R_FQ, HD, HD), (R_SQ, HD, HD), (R_MQ, MQK, MQK)):
            last = dve.tensor_scalar(row[:, at:at + n], row[:, at:at + n], float(d) ** -0.5, None, ALU.mult)
        last.then_inc(self.scaled, 1)
        dve.wait_ge(self.scaled, 1)


def norm(nc, k, xT, hi, lo, gain, tag, groups, also=None, vectors=None):
    with ExitStack() as s:
        G, HC = len(groups), DC // 2
        T = lambda n, shape: s.enter_context(nc.sbuf_tensor(n + tag, shape, F32))
        sq, hf, rs = T("nsq", [P, 2, DC, TN]), T("nhf", [P, 2, DC, TN]), T("nrs", [P, 2, G, TN])
        ps = s.enter_context(nc.psum_tensor("nps" + tag, [P, 2, G, 512], F32))
        sem = k.sems["norm"]
        squared, summed, logged, inverted, normed, hi_done, low, pool_low = (sem[n] for n in
                                                         ("sq", "sum", "ln", "rs", "hf", "hi", "lo", "lp"))
        ones = k.const[:, C_ONE:C_ONE + P]
        group_of = [g for g, (a, b) in enumerate(groups) for c in range(a, b)]
        cols = lambda t: slice(t * TN, (t + 1) * TN)
        half = lambda h: slice(h * HC, (h + 1) * HC)
        with nc.Block() as block:

            @block.sync
            def _(sp):
                if vectors:
                    vectors.load(sp)
                also(sp)

            @block.scalar
            def _(act):
                def square(t):
                    if t >= 2:
                        act.wait_ge(summed, t - 1)
                    for h in range(2):
                        act.activation(sq[:, t % 2, half(h)], xT[:, half(h), cols(t)], ACT.Square)\
                           .then_inc(squared, 1)

                def inverse_root(t):
                    act.wait_ge(summed, t + 1)
                    if t >= 2:
                        act.wait_ge(normed, DC * (t - 1))
                    for g, (a, b) in enumerate(groups):
                        act.activation(rs[:, t % 2, g, :], ps[:, t % 2, g, 0:TN], ACT.Ln, scale=1.0 / (P * (b - a)),
                                       bias=k.const[:, C_EPS:C_EPS + 1]).then_inc(logged, 1)
                    act.wait_ge(logged, G * (t + 1))
                    act.activation(rs[:, t % 2], rs[:, t % 2], ACT.Exp, scale=-0.5).then_inc(inverted, 1)

                square(0)
                square(1)
                inverse_root(0)
                if vectors:
                    vectors.copy(act)
                for t in range(NT):
                    if t + 2 < NT:
                        square(t + 2)
                    if t + 1 < NT:
                        inverse_root(t + 1)
                    for h in range(2):
                        act.wait_ge(normed, DC * t + HC * (h + 1))
                        act.activation(hi[:, half(h), cols(t)], hf[:, t % 2, half(h)], ACT.Copy).then_inc(hi_done, 1)

            @block.tensor
            def _(pe):
                for t in range(NT):
                    if t >= 2:
                        pe.wait_ge(logged, G * (t - 1))
                    for c in range(DC):
                        if c % HC == 0:
                            pe.wait_ge(squared, 2 * t + c // HC + 1)
                        g = group_of[c]
                        last = pe.matmul(ps[:, t % 2, g, 0:TN], ones, sq[:, t % 2, c, :],
                                         start=(c == groups[g][0]), stop=(c == groups[g][1] - 1))
                    last.then_inc(summed, 1)
                    if vectors and t == 0:
                        vectors.turn(pe)

            @block.vector
            def _(dve):
                def low_half(t):
                    dve.wait_ge(hi_done, 2 * t + 1)
                    dve.tensor_tensor(lo[:, half(0), cols(t)], hf[:, t % 2, half(0)],
                                      hi[:, half(0), cols(t)].bitcast(F32), ALU.subtract).then_inc(low, 1)

                for t in range(NT):
                    dve.wait_ge(inverted, t + 1)
                    if vectors and t == 0:
                        dve.wait_ge(vectors.ready, 1)
                    if t >= 2:
                        dve.wait_ge(low, t - 1)
                        dve.wait_ge(pool_low, t - 1)
                    for c in range(DC):
                        dve.scalar_tensor_tensor(hf[:, t % 2, c, :], xT[:, c, cols(t)],
                                                 k.vec[:, gain + c:gain + c + 1], rs[:, t % 2, group_of[c], :],
                                                 ALU.mult, ALU.mult).then_inc(normed, 1)
                    if t >= 1:
                        low_half(t - 1)
                low_half(NT - 1)
                if vectors:
                    vectors.scale(dve)

            @block.gpsimd
            def _(pool):
                for t in range(NT):
                    pool.wait_ge(hi_done, 2 * t + 2)
                    if t:
                        pool.wait_ge(pool_low, t)
                    pool.tensor_tensor(lo[:, half(1), cols(t)], hf[:, t % 2, half(1)],
                                       hi[:, half(1), cols(t)].bitcast(F32), ALU.subtract).then_inc(pool_low, 1)
    restart(nc, k.lists["norm"])


def w_in_block(k, lay, step):
    return k.w_in[lay].rearrange("(c p) n -> p c n", p=P)[:, :, bass.ds(step * WN, WN)]


def project_in(nc, k, lay, hi, lo, proj, raw, beside):
    with ExitStack() as s:
        whi = s.enter_context(nc.sbuf_tensor("whi", [P, 2, DC, WN], F32R))
        wlo = s.enter_context(nc.sbuf_tensor("wlo", [P, 2, DC, WN], F32R))
        NB = 3
        ps = s.enter_context(nc.psum_tensor("wps", [P, NB, 512], F32))
        sem = k.sems["win"]
        raw_in, hi_done, lo_done, tile_done, tile_free = (sem[n] for n in ("raw", "hi", "lo", "done", "tf"))
        per = TT // NB

        def steps(eng, body):
            for b in range(2):
                body(0, b, b)
            with eng.Fori(1, WSTEPS // 2) as i:
                for b in range(2):
                    body(i, b, 2 * i + b)
            body(WSTEPS // 2, 0, WSTEPS - 1)

        def columns_ready(eng, upto):
            for b in range(NB):
                eng.wait_ge(tile_free[b], per * -(-upto // WN))

        with nc.Block() as block:

            @block.sync
            def _(sp):
                def body(i, b, step):
                    if is_first(i):
                        return
                    sp.wait_ge(lo_done[b], i)
                    sp.dma_start(raw[:, b], w_in_block(k, lay, step)).then_inc(raw_in[b], 16)
                steps(sp, body)
                beside.load_store(sp, columns_ready)

            @block.vector
            def _(dve):
                beside.vector(dve, columns_ready)

            @block.gpsimd
            def _(pool):
                def body(i, b, step):
                    pool.wait_ge(hi_done[b], i + 1)
                    if not (is_first(i) and b == 0):
                        pool.wait_ge(lo_done[1 - b], i + b)
                    pool.tensor_tensor(wlo[:, b], raw[:, b], whi[:, b].bitcast(F32), ALU.subtract)\
                        .then_inc(lo_done[b], 1)
                steps(pool, body)

            @block.scalar
            def _(act):
                def split(i, b):
                    act.wait_ge(raw_in[b], 16 * i + 16)
                    act.activation(whi[:, b], raw[:, b], ACT.Copy).then_inc(hi_done[b], 1)

                def drain(i, b, step, tiles=range(TT)):
                    for t in tiles:
                        n = P if t < QT else DEC
                        act.wait_ge(tile_done[t % NB], step * per + (t // NB + 1))
                        act.activation(proj[0:n, t, bass.ds(step * WN, WN)], ps[0:n, t % NB, 0:WN],
                                       ACT.Copy).then_inc(tile_free[t % NB], 1)
                def both(i):
                    split(i, 1)
                    drain(i, 0, 2 * i)
                    split(i + 1, 0)
                    drain(i, 1, 2 * i + 1)
                split(0, 0)
                both(0)
                with act.Fori(1, WSTEPS // 2 - 1) as i:
                    both(i)
                last = WSTEPS // 2
                split(last - 1, 1)
                split_at = 2 * NB
                drain(last - 1, 0, WSTEPS - 3)
                split(last, 0)
                beside.scalar_fox(act)
                drain(last - 1, 1, WSTEPS - 2)
                drain(last, 0, WSTEPS - 1, range(split_at))
                beside.scalar_swa(act)
                drain(last, 0, WSTEPS - 1, range(split_at, TT))

            @block.tensor
            def _(pe):
                def body(i, b, step):
                    pe.wait_ge(lo_done[b], i + 1)
                    for t in range(TT):
                        n = P if t < QT else DEC
                        if not (is_first(step) and t < NB):
                            pe.wait_ge(tile_free[t % NB], step * per + t // NB)
                        at = slice(t * P, t * P + n)
                        for c in range(DC):
                            for m, (a, w) in enumerate(((hi, whi), (hi, wlo), (lo, whi))):
                                last = pe.matmul(ps[0:n, t % NB, 0:WN], a[:, c, at], w[:, b, c, :],
                                                 start=(c == 0 and m == 0), stop=(c == DC - 1 and m == 2))
                        last.then_inc(tile_done[t % NB], 1)
                steps(pe, body)


class Prepare:
    HF, HS = 2 * FOXH, SWAH + SWAKV
    ABS = 3
    FOX_SUMS = ABS + 2 * TT
    ONE_PLUS = FOX_SUMS + 1
    LOGF = ONE_PLUS + 5
    STARTS = LOGF + TT
    FOX_K, FOX_Q = STARTS + 2, STARTS + 4
    SWA_SUMS = FOX_Q + 2 * TT
    SWA_K, SWA_Q = SWA_SUMS + 2, SWA_SUMS + 4

    def __init__(self, nc, k, lay, s, proj):
        self.k, self.lay, self.proj = k, lay, proj
        T = lambda n, shape: s.enter_context(nc.sbuf_tensor(n, shape, F32))
        self.fs = T("fs", [P, TT, FOXH])
        self.g = T("fgate", [P, 6, TT, FOXH])
        self.cl = T("fcl", [P, TT, FOXH])
        self.fp = T("ffp", [P, QT, FOXH])
        self.pre = T("fpre", [P, 2, TT, FOXH])
        self.sq = T("fsq", [P, self.HF, HD])
        self.ssf, self.sss = T("ssf", [P, TT, self.HF]), T("sss", [P, TT, self.HS])
        sem = k.sems["fox"]
        self.cached, self.stored, self.act_steps, self.dve_steps = (sem[n] for n in ("cl", "st", "act", "dve"))
        self.fox = proj[:, :, O_FQ:O_FV].rearrange("p t (h d) -> p t h d", d=HD)
        self.swa = proj[:, :, O_SQ:O_SV].rearrange("p t (h d) -> p t h d", d=HD)
        self.STORES = 12

    def load_store(self, sp, columns_ready):
        k, lay, proj, lf = self.k, self.lay, self.proj, self.g[:, 5]
        sp.dma_start(self.cl[:, 0:QT, :], k.cache_fox_logf[lay, 0].rearrange("(t p) h -> p t h", p=P))\
          .then_inc(self.cached, 16)

        def out(dst, src):
            sp.dma_start(dst, src).then_inc(self.stored, 16)

        def out_fox(dst, dst_s, src):
            out(dst[lay, 0].rearrange("(t p) h d -> p t (h d)", p=P), src[:, 0:QT])
            out(dst_s[lay, 0].rearrange("t h d -> t (h d)"), src[0:DEC, QT])
        for new, cache in ((k.swa_k_s, k.cache_swa_k), (k.swa_v_s, k.cache_swa_v)):
            out(new[lay, 0, 0:WIN - DEC], cache[lay, 0, DEC:WIN])
        columns_ready(sp, O_G)
        out_fox(k.fox_v_p, k.fox_v_s, proj[:, :, O_FV:O_G])
        sp.wait_ge(self.dve_steps, self.LOGF)
        out(k.fox_logf_p[lay, 0].rearrange("(t p) h -> p t h", p=P), lf[:, 0:QT])
        out(k.fox_logf_s[lay, 0], lf[0:DEC, QT])
        sp.wait_ge(self.dve_steps, self.FOX_K)
        out_fox(k.fox_k_p, k.fox_k_s, proj[:, :, O_FK:O_FV])
        kv = lambda r, t, o: proj[0:r, t, o:o + SWAKV * HD]
        columns_ready(sp, O_CQ)
        sp.wait_ge(self.dve_steps, self.SWA_K)
        for new, last, o in ((k.swa_v_s, k.swa_v_p, O_SV), (k.swa_k_s, k.swa_k_p, O_SK)):
            out(new[lay, 0, WIN - DEC:WIN].rearrange("t h d -> t (h d)"), kv(DEC, QT, o))
            out(last[lay, 0].rearrange("t h d -> t (h d)"), kv(P, QT - 1, o))

    def scalar_fox(self, act):
        x, ax, e, u, r, lf = (self.g[:, n] for n in range(6))
        own = Steps(act, self.act_steps)
        act.wait_ge(self.dve_steps, self.FOX_SUMS)
        own.after(act.activation(e, ax, ACT.Exp, scale=-1.0))
        act.wait_ge(self.dve_steps, self.ONE_PLUS)
        own.after(act.activation(ax, u, ACT.Ln))
        self.inverse_root(act, own, self.ssf)

    def scalar_swa(self, act):
        act.wait_ge(self.dve_steps, self.SWA_SUMS)
        self.inverse_root(act, Steps(act, self.act_steps, 4), self.sss)

    def inverse_root(self, act, own, ss):
        own.after(act.activation(ss[:, :, :], ss[:, :, :], ACT.Ln, scale=1.0 / HD,
                                 bias=self.k.const[:, C_EPS:C_EPS + 1]))
        own.after(act.activation(ss[:, :, :], ss[:, :, :], ACT.Exp, scale=-0.5))

    def vector(self, dve, columns_ready):
        k, proj, cl, pre = self.k, self.proj, self.cl, self.pre
        x, ax, e, u, r, lf = (self.g[:, n] for n in range(6))
        own = Steps(dve, self.dve_steps)

        def sums(heads, ss, n):
            for t in range(TT):
                own.after(dve.tensor_tensor(self.sq[:, 0:n], heads[:, t], heads[:, t], ALU.mult))
                own.after(dve.tensor_reduce(ss[:, t], self.sq[:, 0:n], AX, ALU.add))

        def scaled(heads, ss, a, n, row):
            v = heads[:, :, a:a + n]
            own.after(dve.tensor_tensor(v, v, bcast(ss[:, :, a:a + n], [P, TT, n, HD], 3), ALU.mult))
            own.after(dve.tensor_tensor(v, v, bcast(k.row[:, row:row + HD], [P, TT, n, HD], 1, 1), ALU.mult))

        dve.memset(proj[32:64, QT, :], 0.0)
        own.after(dve.memset(proj[64:128, QT, :], 0.0))
        columns_ready(dve, O_G + FOXH)
        own.after(dve.tensor_tensor(x, proj[:, :, O_G:O_G + FOXH], bcast(k.row[:, R_BF:R_BF + FOXH], [P, TT, FOXH], 1),
                                    ALU.add))
        own.after(dve.scalar_tensor_tensor(ax, x, -1.0, x, ALU.mult, ALU.max))
        assert own.n == self.ABS
        sums(self.fox, self.ssf, self.HF)
        dve.wait_ge(self.act_steps, 1)
        own.after(dve.tensor_scalar(u, e, 1.0, None, ALU.add))
        assert own.n == self.ONE_PLUS
        own.after(dve.tensor_scalar(r, u, -1.0, None, ALU.add))
        own.after(dve.tensor_tensor(r, e, r, ALU.subtract))
        own.after(dve.tensor_scalar(x, x, 0.0, None, ALU.min))
        dve.wait_ge(self.act_steps, 2)
        own.after(dve.tensor_tensor(r, ax, r, ALU.add))
        own.after(dve.tensor_tensor(lf, x, r, ALU.subtract))
        assert own.n == self.LOGF
        dve.wait_ge(self.cached, 16)
        dve.memset(cl[32:64, QT, :], 0.0)
        dve.memset(cl[64:128, QT, :], 0.0)
        dve.tensor_copy(cl[0:DEC, QT, :], lf[0:DEC, QT, :])
        own.after(dve.memset(pre[:, :, 0, :], 0.0))
        for t in range(1, TT):
            if t < QT:
                dve.tensor_tensor(pre[:, 0, t], pre[:, 0, t - 1], lf[:, t - 1], ALU.add)
            own.after(dve.tensor_tensor(pre[:, 1, t], pre[:, 1, t - 1], cl[:, t - 1], ALU.add))
        assert own.n == self.STARTS
        dve.wait_ge(self.act_steps, 4)
        scaled(self.fox, self.ssf, FOXH, FOXH, R_FK)
        scaled(self.fox, self.ssf, 0, FOXH, R_FQ)
        assert own.n == self.FOX_Q
        columns_ready(dve, O_SV)
        sums(self.swa, self.sss, self.HS)
        assert own.n == self.SWA_SUMS
        dve.wait_ge(self.act_steps, 6)
        scaled(self.swa, self.sss, SWAH, SWAKV, R_SK)
        scaled(self.swa, self.sss, 0, SWAH, R_SQ)


def fox_rows(nc, k, prep, frow):
    with ExitStack() as s:
        ps = s.enter_context(nc.psum_tensor("fps", [P, 2, 512], F32))
        psF = s.enter_context(nc.psum_tensor("fpsF", [P, QT, P], F32))
        sem = k.sems["fox"]
        f_done, copied, f_turned, row_hi = (sem[n] for n in ("f", "fc", "ft", "rh"))
        tri, ones = k.const[:, C_TRI:C_TRI + P], k.const[:, C_ONE:C_ONE + P]
        lf, cl, pre, fp, fs = prep.g[:, 5], prep.cl, prep.pre, prep.fp, prep.fs
        with nc.Block() as block:

            @block.sync
            def _(sp):
                sp.wait_ge(prep.stored, 16 * prep.STORES)

            @block.tensor
            def _(pe):
                pe.matmul(ps[:, 0, 0:QT * FOXH], tri, lf[:, 0:QT, :], start=True, stop=False)
                pe.matmul(ps[:, 0, 0:QT * FOXH], ones, pre[:, 0, 0:QT, :], start=False, stop=True)
                pe.matmul(ps[:, 1, 0:TT * FOXH], tri, cl[:, :, :], start=True, stop=False)
                pe.matmul(ps[:, 1, 0:TT * FOXH], ones, pre[:, 1], start=False, stop=True).then_inc(f_done, 1)
                pe.wait_ge(copied, 1)
                for t in range(QT):
                    last = pe.transpose(psF[0:FOXH, t, :], fp[:, t, :], k.const[:, C_ID:C_ID + P])
                last.then_inc(f_turned, 1)

            @block.scalar
            def _(act):
                act.wait_ge(f_turned, 1)
                act.activation(frow[0][:, :], psF[0:FOXH, :, :].rearrange("p t n -> p (t n)"), ACT.Copy,
                               scale=-1.0).then_inc(row_hi, 1)

            @block.vector
            def _(dve):
                dve.wait_ge(f_done, 1)
                dve.tensor_copy(fp[:, :, :], ps[:, 0, 0:QT * FOXH].rearrange("p (t h) -> p t h", h=FOXH))\
                   .then_inc(copied, 1)
                dve.tensor_copy(fs[:, :, :], ps[:, 1, 0:TT * FOXH].rearrange("p (t h) -> p t h", h=FOXH))
                dve.wait_ge(row_hi, 1)
                dve.scalar_tensor_tensor(frow[1][:, :], psF[0:FOXH, :, :].rearrange("p t n -> p (t n)"), -1.0,
                                         frow[0][:, :].bitcast(F32), ALU.mult, ALU.subtract)


def attend_prompt(nc, k, kind, heads, kdim, q_of, k_of, v_of, kv_of, yT, yc, frow=None, alibi=None):
    swa, fox = kind == "swa", kind == "fox"
    pairs = heads // 2
    R = pairs * QT
    AHEAD, RQ = 3, 4

    def first(i):
        return max(i - 1, 0) if swa else 0

    units = []
    for r in range(R):
        i = r % QT
        if i + 1 - first(i) <= 4:
            units.append((r, (0, 1), True))
        else:
            units += [(r, (0,), False), (r, (1,), True)]
    NU = len(units)
    sink = 1 if swa else 0
    with ExitStack() as s:
        T = lambda n, shape, dt=F32: s.enter_context(nc.sbuf_tensor(n + kind, shape, dt))
        qT = [T("qT" + n, [96, RQ, 2, P], F32R) for n in ("hi", "lo")]
        kT = [T("kT" + n, [96, 2, 2, SEQ], F32R) for n in ("hi", "lo")]
        NPR = 3
        pr = T("pr", [P, NPR, 2, 512])
        pT = T("pT", [P, 2, 2, 2 if swa else QT, P])
        st = T("st", [P, 3, NU, 2])
        nmax, tot, rtot = (st[:, n] for n in range(3))
        if swa:
            bias = T("bias", [P, SWAH, 2 * P])
        psS = s.enter_context(nc.psum_tensor("psS" + kind, [P, 2, 2, 512], F32))
        psX = s.enter_context(nc.psum_tensor("psX" + kind, [P, 2, 2, P], F32))
        psT = s.enter_context(nc.psum_tensor("psT" + kind, [P, 8, P], F32))
        psO = s.enter_context(nc.psum_tensor("psO" + kind, [P, 512], F32))
        sem = k.sems["att"]
        (cleared, loaded, row_in, x_done, x_hi, x_lo, scored, maxed, expd, normed, turned, t_low, t_high, mixed,
         y_done, dve_steps, inverted, pool_normed) = (sem[n] for n in ("clr", "ld", "row", "x", "xh", "xl", "s", "m", "e", "n", "t", "tl",
                                                "th", "o", "y", "d", "iv", "pn"))
        ident = k.const[:, C_ID:C_ID + P]

        def width(r):
            i = r % QT
            return (i + 1 - first(i)) * P

        shared = [(j, width(r)) for j, (r, es, _) in enumerate(units) if len(es) == 2]

        def shared_to(j):
            return sum(1 for n, _ in shared if n <= j)

        def next_tile(m):
            if 1 <= m <= NU and units[m - 1][2] and units[m - 1][0] + AHEAD < R:
                return units[m - 1][0] + AHEAD

        def units_to(r):
            return sum(1 for u in units if u[0] <= r)

        with nc.Block() as block:

            @block.sync
            def _(sp):
                if swa:
                    sp.dma_start(bias[:, :, :], alibi).then_inc(loaded, 16)
                if fox:
                    sp.wait_ge(cleared, 6)
                    for p in range(pairs):
                        if p >= 2:
                            sp.wait_ge(scored, units_to((p - 1) * QT - 1))
                        for n in range(2):
                            for e in range(2):
                                h = 2 * p + e
                                sp.dma_start(kT[n][64:65, p % 2, e, :].bitcast(F32), frow[n][h:h + 1, :].bitcast(F32))\
                                  .then_inc(row_in[p % 2], 16)

            @block.gpsimd
            def _(pool):
                if kdim < 96:
                    jobs = [(t[64:96], 0.0) for t in (*qT, *kT)] + [(qT[0][64:65], 1.0)] * 2 * fox
                    for n, (rows, value) in enumerate(jobs):
                        pool.memset(rows.bitcast(F32), value).then_inc(cleared, 1)
                        pool.wait_ge(cleared, n + 1)
                for n, (j, w) in enumerate(shared):
                    pool.wait_ge(inverted, n + 1)
                    if n:
                        pool.wait_ge(pool_normed, n)
                    v = pr[:, j % NPR, :, 0:w]
                    pool.tensor_tensor(v, v, bcast(rtot[:, j, :], [P, 2, w], 2), ALU.mult).then_inc(pool_normed, 1)

            @block.tensor
            def _(pe):
                def turn_tile(r):
                    p, i = divmod(r, QT)
                    if r:
                        pe.wait_ge(x_lo, r)
                    for e in range(2):
                        h = 2 * p + e
                        pe.transpose(psX[0:kdim, 0, e, :], q_of(h)[:, i, :], ident)
                        last = pe.transpose(psX[0:kdim, 1, e, :], k_of(kv_of(h))[:, i, :], ident)
                    last.then_inc(x_done, 1)

                for r in range(AHEAD):
                    turn_tile(r)
                for m in range(NU + 3):
                    if m < NU:
                        r, es, ends = units[m]
                        p, i = divmod(r, QT)
                        pe.wait_ge(x_lo, r + 1)
                        if fox:
                            pe.wait_ge(row_in[p % 2], 64 * (p // 2 + 1))
                        if m >= 2:
                            pe.wait_ge(expd, m - 1)
                        f, w = first(i) * P, width(r)
                        for e in es:
                            both = len(es) == 2
                            for a in range(0, w, 512):
                                n = min(512, w - a)
                                diag = not swa and a + n == w
                                bank = psS[:, m % 2, e if both else a // 512, :]
                                for j, (x, y) in enumerate(((0, 0), (0, 1), (1, 0))):
                                    last = pe.matmul(bank[:, 0:n], qT[x][:, r % RQ, e, :],
                                                     kT[y][:, p % 2, e, f + a:f + a + n],
                                                     start=(j == 0), stop=(j == 2 and not diag))
                                if diag:
                                    last = pe.matmul(bank[:, n - P:n], k.identr[:, :],
                                                     (k.mfoxr if fox else k.mmlar)[:, :], start=False, stop=True)
                        last.then_inc(scored, 1)
                    if next_tile(m):
                        turn_tile(next_tile(m))
                    j = m - 2
                    if 0 <= j < NU:
                        r, es, _ = units[j]
                        nb = width(r) // P
                        if len(es) == 2:
                            pe.wait_ge(pool_normed, shared_to(j))
                        else:
                            pe.wait_ge(normed, j + 1 - shared_to(j))
                        if j:
                            pe.wait_ge(t_low, j)
                            pe.wait_ge(t_high, j)
                        for n, e in enumerate(es):
                            flat = pr[:, j % NPR, n, :] if len(es) == 2 else \
                                pr[:, j % NPR].rearrange("p e n -> p (e n)")
                            for b in range(nb):
                                last = pe.transpose(psT[:, 4 * n + b, :], flat[:, b * P:(b + 1) * P], ident)
                        last.then_inc(turned, 1)
                    j = m - 3
                    if 0 <= j < NU and units[j][2]:
                        r = units[j][0]
                        p, i = divmod(r, QT)
                        pe.wait_ge(t_low, j + 1)
                        pe.wait_ge(t_high, j + 1)
                        if r:
                            pe.wait_ge(y_done, r)
                        nb = width(r) // P
                        for b in range(nb):
                            for e in range(2):
                                last = pe.matmul(psO[64 * e:64 * e + HD, 0:P],
                                                 v_of(kv_of(2 * p + e), first(i) + b), pT[:, r % 2, e, b, :],
                                                 start=(b == 0), stop=(b == nb - 1))
                        last.then_inc(mixed, 1)

            @block.scalar
            def _(act):
                def high_part(r):
                    p, i = divmod(r, QT)
                    act.wait_ge(x_done, r + 1)
                    act.activation(qT[0][0:kdim, r % RQ, :, :], psX[0:kdim, 0], ACT.Copy)
                    act.activation(kT[0][0:kdim, p % 2, :, i * P:(i + 1) * P], psX[0:kdim, 1], ACT.Copy)\
                       .then_inc(x_hi, 1)

                if kdim < 96:
                    act.wait_ge(cleared, 6 if fox else 4)
                for r in range(AHEAD):
                    high_part(r)
                for m in range(NU + 3):
                    if next_tile(m):
                        high_part(next_tile(m))
                    if m < NU:
                        r, es, _ = units[m]
                        w = width(r) + sink
                        act.wait_ge(maxed, m + 1)
                        if m >= NPR:
                            act.wait_ge(turned, m - NPR + 1)
                        for n, e in enumerate(es):
                            src, dst = psS[:, m % 2], pr[:, m % NPR]
                            if len(es) == 2:
                                src, dst = src[:, n, :], dst[:, n, :]
                            else:
                                src, dst = (v.rearrange("p e n -> p (e n)") for v in (src, dst))
                            last = act.activation(dst[:, 0:w], src[:, 0:w], ACT.Exp, bias=nmax[:, m, n:n + 1],
                                                  accum_out=tot[:, m, n:n + 1])
                        last.then_inc(expd, 1)
                    j = m - 2
                    if 0 <= j < NU:
                        r, es, _ = units[j]
                        nb = min(4, width(r) // P)
                        act.wait_ge(turned, j + 1)
                        if r >= 2:
                            act.wait_ge(mixed, r - 1)
                        act.activation(pT[:, r % 2, es[0], 0:nb, :], psT[:, 0:nb, :], ACT.Copy).then_inc(t_low, 1)
                    j = m - 3
                    if 0 <= j < NU and units[j][2]:
                        r = units[j][0]
                        p, i = divmod(r, QT)
                        act.wait_ge(mixed, r + 1)
                        act.activation(yT[:, yc + p, i * P:(i + 1) * P], psO[:, 0:P], ACT.Copy).then_inc(y_done, 1)

            @block.vector
            def _(dve):
                own = Steps(dve, dve_steps)

                def low_part(r):
                    p, i = divmod(r, QT)
                    dve.wait_ge(x_hi, r + 1)
                    dve.tensor_tensor(qT[1][0:kdim, r % RQ, :, :], psX[0:kdim, 0],
                                      qT[0][0:kdim, r % RQ, :, :].bitcast(F32), ALU.subtract)
                    at = slice(i * P, (i + 1) * P)
                    dve.tensor_tensor(kT[1][0:kdim, p % 2, :, at], psX[0:kdim, 1],
                                      kT[0][0:kdim, p % 2, :, at].bitcast(F32), ALU.subtract).then_inc(x_lo, 1)

                if kdim < 96:
                    dve.wait_ge(cleared, 6 if fox else 4)
                for r in range(AHEAD):
                    low_part(r)
                if swa:
                    dve.wait_ge(loaded, 16)
                for m in range(NU + 2):
                    if m < NU:
                        r, es, _ = units[m]
                        w, h = width(r), 2 * (r // QT)
                        ne = len(es)
                        dve.wait_ge(scored, m + 1)
                        if swa:
                            v = psS[:, m % 2, :, 0:w]
                            dve.tensor_tensor(v, v, bias[:, h:h + 2, 2 * P - w:2 * P], ALU.add)
                            own.after(dve.tensor_copy(psS[:, m % 2, :, w], k.row[:, R_SINK + h:R_SINK + h + 2]))
                        v = psS[:, m % 2, :, 0:w + sink] if ne == 2 else \
                            psS[:, m % 2].rearrange("p e n -> p (e n)")[:, 0:w]
                        dve.tensor_reduce(nmax[:, m, 0:ne], v, AX, ALU.max, negate=True).then_inc(maxed, 1)
                    j = m - 1
                    if 0 <= j < NU:
                        r, es, _ = units[j]
                        w = width(r)
                        dve.wait_ge(expd, j + 1)
                        inverse = dve.reciprocal(rtot[:, j, 0:len(es)], tot[:, j, 0:len(es)])
                        if len(es) == 2:
                            inverse.then_inc(inverted, 1)
                        else:
                            own.after(inverse)
                            v = pr[:, j % NPR].rearrange("p e n -> p (e n)")[:, 0:w]
                            dve.tensor_scalar(v, v, rtot[:, j, 0:1], None, ALU.mult).then_inc(normed, 1)
                    j = m - 2
                    if 0 <= j < NU:
                        r, es, _ = units[j]
                        nb = width(r) // P
                        dve.wait_ge(turned, j + 1)
                        if r >= 2:
                            dve.wait_ge(mixed, r - 1)
                        if len(es) == 2:
                            dve.tensor_copy(pT[:, r % 2, 1, 0:nb, :], psT[:, 4:4 + nb, :]).then_inc(t_high, 1)
                        else:
                            dve.tensor_copy(pT[:, r % 2, es[0], 4:nb, :], psT[:, 4:nb, :]).then_inc(t_high, 1)
                    if next_tile(m):
                        low_part(next_tile(m))
    restart(nc, k.lists["att"])


def attend_sample(nc, k, kind, heads, q_new, kunits, kdim, row_of, tiles, loads, yT, yc, fs=None):
    mla, fox = kind == "mla", kind == "fox"
    keys = sum(t[0] for t in tiles)
    offs = [sum(t[0] for t in tiles[:n]) for n in range(len(tiles))]
    pw = keys if keys <= 512 else keys // 3
    NPC = keys // pw
    G = (heads + 3) // 4
    pairs = heads // 2
    qunits = heads if mla else pairs
    jobs = [(u, list(range(a, min(a + 4, len(tiles))))) for u in range(kunits) for a in range(0, len(tiles), 4)]
    if fox:
        jobs += [("f", list(range(a, min(a + 4, len(tiles))))) for a in range(0, len(tiles), 4)]
    pjobs = [(g, list(range(a, min(a + 4, len(tiles))))) for g in range(G) for a in range(0, len(tiles), 4)]
    J, PJ = len(jobs), len(pjobs) // G
    rows = [32 * min(4, heads - 4 * g) for g in range(G)]
    with ExitStack() as s:
        T = lambda n, shape: s.enter_context(nc.sbuf_tensor(n + "_s" + kind, shape, F32))
        kT = T("kT", [P, kunits, keys])
        qz = T("qz", [P, qunits, DEC if mla else 2 * DEC])
        pr = T("pr", [P, G, keys])
        pT = T("pT", [P, G, len(tiles), P])
        st = T("st", [P, 4, G])
        mx, tot, rtot, sk = (st[:, n] for n in range(4))
        sink = T("sink", [P, 2])
        if fox:
            rb, lb, fq = T("rb", [64, keys]), T("lb", [64, G * P]), T("fq", [64, DEC])
        psS = s.enter_context(nc.psum_tensor("psS_s" + kind, [P, NPC, 512], F32))
        psX = s.enter_context(nc.psum_tensor("psX_s" + kind, [P, 2, 4, P], F32))
        psQ = s.enter_context(nc.psum_tensor("psQ_s" + kind, [P, 4, P], F32))
        psO = s.enter_context(nc.psum_tensor("psO_s" + kind, [P, 2, 512], F32))
        sem = k.sems["smp"]
        (cache_in, zeroed, q_turned, q_done, x_done, x_out, k_ready, scored, dve_steps, maxed, expd, normed,
         t_done, t_out, mixed, y_done) = (sem[n] for n in ("in", "z", "qt", "qd", "x", "xo", "k", "s", "d", "m",
                                                           "e", "n", "t", "to", "o", "y"))
        ident = k.const[:, C_ID:C_ID + P]

        engines = (nc.scalar, nc.vector)

        def unload(eng, b):
            for j in range(b, J, 2):
                u, ts = jobs[j]
                c0, w = offs[ts[0]], sum(tiles[t][0] for t in ts)
                eng.wait_ge(x_done, j + 1)
                n = FOXH if u == "f" else (kdim if mla else P)
                full = [t for t in ts if tiles[t][0] == P]
                parts = ([(0, len(full))] if full else []) + [(ts.index(t), 0) for t in ts if tiles[t][0] < P]
                for m, (i, cnt) in enumerate(parts):
                    o = offs[ts[i]]
                    if cnt:
                        src = psX[0:n, b, i:i + cnt, :].rearrange("p t n -> p (t n)")
                        ww = cnt * P
                    else:
                        ww = tiles[ts[i]][0]
                        src = psX[0:n, b, i, 0:ww]
                    dst = rb[0:n, o:o + ww] if u == "f" else kT[0:n, u, o:o + ww]
                    sc = -1.0 if u == "f" else 1.0
                    if u == "f" and len(tiles) - 1 in ts and not cnt:
                        copy(eng, fq[32:32 + FOXH, :], src, 1.0)
                    last = copy(eng, dst, src, sc)
                last.then_inc(x_out[b], 1)

        def copy(eng, dst, src, scale):
            if eng is engines[0]:
                return eng.activation(dst, src, ACT.Copy, scale=scale)
            return eng.tensor_scalar(dst, src, scale, None, ALU.mult)

        def unload_p(eng, j):
            g, ts = pjobs[j]
            eng.wait_ge(t_done, j + 1)
            full = [t for t in ts if tiles[t][0] == P]
            if full:
                last = copy(eng, pT[:, g, full[0]:full[-1] + 1, 0:rows[g]],
                            psX[:, j % 2, 0:len(full), 0:rows[g]], 1.0)
            for t in ts:
                if tiles[t][0] < P:
                    r = tiles[t][0]
                    last = copy(eng, pT[0:r, g, t, 0:rows[g]],
                                psX[0:r, j % 2, ts.index(t), 0:rows[g]], 1.0)
            last.then_inc(t_out[j % 2], 1)

        with nc.Block() as block:

            @block.sync
            def _(sp):
                for dst, src in loads:
                    sp.dma_start(dst, src).then_inc(cache_in, 16)

            @block.gpsimd
            def _(pool):
                pool.memset(qz[:, :, :], 0.0).then_inc(zeroed, 1)
                if fox:
                    for n, (rows, value) in enumerate(((rb[0:32, :], 0.0), (rb[32:64, :], 1.0), (fq[32:64, :], 0.0))):
                        pool.wait_ge(zeroed, n + 1)
                        pool.memset(rows, value).then_inc(zeroed, 1)

            @block.tensor
            def _(pe):
                for u in range(qunits):
                    n = kdim if mla else P
                    last = pe.transpose(psQ[0:n, u, 0:DEC], q_new(u), ident[0:DEC, 0:DEC])
                last.then_inc(q_turned, 1)
                pe.wait_ge(cache_in, 16 * len(loads))
                for j, (u, ts) in enumerate(jobs):
                    if j >= 2:
                        pe.wait_ge(x_out[j % 2], j // 2)
                    for n, t in enumerate(ts):
                        r = tiles[t][0]
                        src = fs[0:r, t, :] if u == "f" else tiles[t][1](u)
                        c = FOXH if u == "f" else (kdim if mla else P)
                        last = pe.transpose(psX[0:c, j % 2, n, 0:r], src, ident[0:r, 0:r])
                    last.then_inc(x_done, 1)
                pe.wait_ge(x_out[0], (J + 1) // 2)
                pe.wait_ge(x_out[1], J // 2)
                pe.wait_ge(q_done, 1)
                for g in range(G):
                    if g:
                        pe.wait_ge(expd, g)
                    for a in range(NPC):
                        at = slice(a * pw, (a + 1) * pw)
                        if fox:
                            pe.matmul(psS[0:rows[g], a, 0:pw], lb[:, g * P:g * P + rows[g]], rb[:, at],
                                      start=True, stop=False, skip_group_check=True)
                        if mla:
                            for h in range(4):
                                last = pe.matmul(psS[32 * h:32 * h + DEC, a, 0:pw], qz[0:kdim, h, :],
                                                 kT[0:kdim, h, at], start=True, stop=True)
                        else:
                            for p in range(2 * g, min(2 * g + 2, pairs)):
                                e = 64 * (p % 2)
                                last = pe.matmul(psS[e:e + 64, a, 0:pw], qz[:, p, :], kT[:, p if fox else 0, at],
                                                 start=not fox, stop=True, skip_group_check=True)
                    last.then_inc(scored, 1)
                for j, (g, ts) in enumerate(pjobs):
                    pe.wait_ge(normed, g + 1)
                    if j >= 2:
                        pe.wait_ge(t_out[j % 2], j // 2)
                    for n, t in enumerate(ts):
                        r = tiles[t][0]
                        last = pe.transpose(psX[0:r, j % 2, n, 0:rows[g]], pr[0:rows[g], g, offs[t]:offs[t] + r],
                                            ident[0:rows[g], 0:rows[g]])
                    last.then_inc(t_done, 1)
                pe.wait_ge(t_out[0], (len(pjobs) + 1) // 2)
                pe.wait_ge(t_out[1], len(pjobs) // 2)
                for p in range(pairs):
                    g, e = p // 2, 64 * (p % 2)
                    if p >= 2:
                        pe.wait_ge(y_done, 2 * (p - 1))
                    for t, (r, _, v) in enumerate(tiles):
                        last = pe.matmul(psO[:, p % 2, 0:2 * DEC], v(p), pT[0:r, g, t, e:e + 64],
                                         start=(t == 0), stop=(t == len(tiles) - 1))
                    last.then_inc(mixed, 1)

            @block.scalar
            def _(act):
                if fox:
                    act.wait_ge(zeroed, 4)
                unload(engines[0], 0)
                for g in range(G):
                    act.wait_ge(maxed, g + 1)
                    last = act.activation(pr[0:rows[g], g, :].rearrange("p (a n) -> p a n", a=NPC),
                                          psS[0:rows[g], :, 0:pw], ACT.Exp, bias=mx[0:rows[g], g:g + 1],
                                          accum_out=tot[0:rows[g], g:g + 1])
                    if kind == "swa":
                        last = act.activation(sk[0:rows[g], g:g + 1], mx[0:rows[g], g:g + 1], ACT.Exp,
                                              bias=sink[0:rows[g], g:g + 1])
                    last.then_inc(expd, 1)
                for j in range(0, len(pjobs), 2):
                    unload_p(engines[0], j)

            @block.vector
            def _(dve):
                own = Steps(dve, dve_steps)
                dve.wait_ge(q_turned, 1)
                dve.wait_ge(zeroed, 1)
                if mla:
                    last = dve.tensor_copy(qz[0:kdim, :, :], psQ[0:kdim, 0:4, 0:DEC])
                else:
                    for h in range(heads):
                        e, r = 64 * (h % 2), row_of(h)
                        last = dve.tensor_copy(qz[r:r + HD, h // 2, DEC * (h % 2):DEC * (h % 2 + 1)],
                                               psQ[e:e + HD, h // 2, 0:DEC])
                if not fox:
                    last.then_inc(q_done, 1)
                if kind == "swa":
                    for g in range(G):
                        for h in range(4 * g, min(4 * g + 4, heads)):
                            e = 32 * (h % 4)
                            last = dve.tensor_copy(sink[e:e + 32, g:g + 1], k.row[e:e + 32, R_SINK + h:R_SINK + h + 1])
                    own.after(last)
                if fox:
                    dve.wait_ge(zeroed, 4)
                unload(engines[1], 1)
                if fox:
                    dve.wait_ge(x_out[0], (J + 1) // 2)
                    dve.wait_ge(x_out[1], J // 2)
                    dve.tensor_copy(lb[0:32, :], k.const[0:32, C_SEL:C_SEL + G * P])
                    dve.tensor_tensor(lb[32:64, :].rearrange("p (a n) -> p a n", n=DEC),
                                      k.const[32:64, C_SEL:C_SEL + G * P].rearrange("p (a n) -> p a n", n=DEC),
                                      bcast(fq[32:64, :], [32, G * 4, DEC], 1), ALU.mult).then_inc(q_done, 1)
                for g in range(G):
                    R = rows[g]
                    dve.wait_ge(scored, g + 1)
                    if fox:
                        new = psS[0:R, NPC - 1, pw - DEC:pw]
                        own.after(dve.tensor_tensor(new, new, k.const[0:R, C_MNEW:C_MNEW + DEC], ALU.add))
                    if kind == "swa":
                        b = k.const[0:R, C_BSW + g * SKEYS:C_BSW + (g + 1) * SKEYS]
                        own.after(dve.tensor_tensor(psS[0:R, 0, 0:pw], psS[0:R, 0, 0:pw], b, ALU.add))
                    own.after(dve.reduce_max(mx[0:R, g:g + 1], psS[0:R, :, 0:pw], mybir.AxisListType.XY))
                    if kind == "swa":
                        own.after(dve.tensor_tensor(mx[0:R, g:g + 1], mx[0:R, g:g + 1], sink[0:R, g:g + 1], ALU.max))
                    dve.tensor_scalar(mx[0:R, g:g + 1], mx[0:R, g:g + 1], -1.0, None, ALU.mult).then_inc(maxed, 1)
                for g in range(G):
                    R = rows[g]
                    dve.wait_ge(expd, g + 1)
                    if kind == "swa":
                        own.after(dve.tensor_tensor(tot[0:R, g:g + 1], tot[0:R, g:g + 1], sk[0:R, g:g + 1], ALU.add))
                    own.after(dve.reciprocal(rtot[0:R, g:g + 1], tot[0:R, g:g + 1]))
                    dve.tensor_scalar(pr[0:R, g, :], pr[0:R, g, :], rtot[0:R, g:g + 1], None, ALU.mult)\
                       .then_inc(normed, 1)
                for j in range(1, len(pjobs), 2):
                    unload_p(engines[1], j)
                for p in range(pairs):
                    dve.wait_ge(mixed, p + 1)
                    for h in (2 * p, 2 * p + 1):
                        e, r, c = 64 * (h % 2), row_of(h), DEC * (h % 2)
                        dve.tensor_copy(yT[e:e + HD, yc + p, SEQ:TOK], psO[r:r + HD, p % 2, c:c + DEC])\
                           .then_inc(y_done, 1)
    restart(nc, k.lists["smp"])


def mla_prepare(nc, k, lay, proj, qm, km, vm):
    KT = 2 * QT + 1
    half = ROPE // 2
    with ExitStack() as s:
        T = lambda n, shape: s.enter_context(nc.sbuf_tensor("m" + n, shape, F32))
        ckc, krc = T("ckc", [P, QT, KVLORA]), T("krc", [P, QT, ROPE])
        wuq, wukv = T("wuq", [P, 2, MLAH * MQK]), T("wukv", [P, 512])
        lat = km[:, 0:TT].rearrange("p t h e -> p t (h e)")
        ss = T("ss", [P, 2, TT])
        cT = T("cT", [P, 2, 3, P])
        rot = T("rot", [P, 2, TT, MLAH, half])
        sq = T("sq", [P, 2, MLAH, MQK])
        hs = T("hs", [P, 2, KT, MLAH])
        psX = s.enter_context(nc.psum_tensor("mpsX", [P, 2, 512], F32))
        psQ = s.enter_context(nc.psum_tensor("mpsQ", [P, 2, 512], F32))
        psK = s.enter_context(nc.psum_tensor("mpsK", [P, 2, 512], F32))
        sem = k.sems["mla"]
        (w_in, c_in, stored, squared, act_steps, d, turned, x_out, q_done, k_done, q_out, k_out, h_sq, h_sum, a2) = (
            sem[n] for n in ("w", "c", "st", "sq", "act", "dve", "t", "xo", "q", "k", "qo", "ko", "hsq", "hsum", "a2"))
        ident = k.const[:, C_ID:C_ID + P]
        cos = k.const[:, C_COS:C_SIN].rearrange("p (t n) -> p t n", n=half)
        sin = k.const[:, C_SIN:C_MNEW].rearrange("p (t n) -> p t n", n=half)
        cq, ckv, kr = (proj[:, :, a:b] for a, b in ((O_CQ, O_CKV), (O_CKV, O_KR), (O_KR, IN_W)))

        def latents(j):
            if j < QT:
                return P, j
            return (P, None) if j < 2 * QT else (DEC, QT)

        with nc.Block() as block:

            @block.sync
            def _(sp):
                sp.dma_start(wuq[:, :, :], k.w_mla_uq[lay].rearrange("(c p) n -> p c n", p=P)).then_inc(w_in, 16)
                sp.dma_start(wukv[:, :], k.w_mla_ukv[lay]).then_inc(w_in, 16)
                sp.dma_start(ckc[:, :, :], k.cache_mla_ckv[lay, 0].rearrange("(t p) n -> p t n", p=P)).then_inc(c_in, 16)
                sp.dma_start(krc[:, :, :], k.cache_mla_krope[lay, 0].rearrange("(t p) n -> p t n", p=P)).then_inc(c_in, 16)
                sp.wait_ge(d, 12)
                for dst, dst_s, src in ((k.mla_ckv_p, k.mla_ckv_s, ckv), (k.mla_krope_p, k.mla_krope_s, kr)):
                    sp.dma_start(dst[lay, 0].rearrange("(t p) n -> p t n", p=P), src[:, 0:QT]).then_inc(stored, 16)
                    sp.dma_start(dst_s[lay, 0], src[0:DEC, QT]).then_inc(stored, 16)
                sp.wait_ge(stored, 64)

            @block.scalar
            def _(act):
                own = Steps(act, act_steps)
                eps = k.const[:, C_EPS:C_EPS + 1]
                own.after(act.activation(lat[:, :, 0:2 * P], cq, ACT.Square))
                own.after(act.activation(lat[:, :, 2 * P:3 * P], ckv, ACT.Square))
                act.wait_ge(d, 2)
                own.after(act.activation(ss[:, 0], ss[:, 0], ACT.Ln, scale=1.0 / QLORA, bias=eps))
                own.after(act.activation(ss[:, 1], ss[:, 1], ACT.Ln, scale=1.0 / KVLORA, bias=eps))
                own.after(act.activation(ss[:, :, :], ss[:, :, :], ACT.Exp, scale=-0.5))
                for j in range(KT):
                    n, t = latents(j)
                    act.wait_ge(turned, j + 1)
                    if j >= 2:
                        act.wait_ge(k_done, j - 1)
                    c0 = 0 if t is not None else 2
                    act.activation(cT[:, j % 2, c0:3, 0:n],
                                   psX[:, j % 2, 0:3 * P].rearrange("p (c n) -> p c n", n=P)[:, c0:3, 0:n],
                                   ACT.Copy).then_inc(x_out, 1)
                    act.wait_ge(k_done, j + 1)
                    kv = psK[0:n, j % 2, :].rearrange("p (h e) -> p h e", e=NOPE + HD)
                    act.activation(km[0:n, j, :, 0:NOPE], kv[:, :, 0:NOPE], ACT.Copy)
                    act.activation(vm[0:n, j, :, :], kv[:, :, NOPE:], ACT.Copy).then_inc(k_out, 1)
                act.wait_ge(k_out, KT)
                for x, cnt, sel in ((km, KT, 1), (qm, TT, 0)):
                    if sel == 0:
                        act.wait_ge(d, 24)
                    else:
                        act.wait_ge(d, 17)
                    for t in range(cnt):
                        i = t + (KT if sel == 0 else 0)
                        if i >= 2:
                            act.wait_ge(h_sum, i - 1)
                        act.activation(sq[:, i % 2], x[:, t], ACT.Square).then_inc(h_sq, 1)
                act.wait_ge(h_sum, KT + TT)
                o2 = Steps(act, a2)
                act.activation(hs[:, 0, 0:TT], hs[:, 0, 0:TT], ACT.Ln, scale=1.0 / MQK, bias=eps)
                o2.after(act.activation(hs[:, 1], hs[:, 1], ACT.Ln, scale=1.0 / MQK, bias=eps))
                act.activation(hs[:, 0, 0:TT], hs[:, 0, 0:TT], ACT.Exp, scale=-0.5)
                o2.after(act.activation(hs[:, 1], hs[:, 1], ACT.Exp, scale=-0.5))

            @block.vector
            def _(dve):
                own = Steps(dve, d)
                dve.wait_ge(act_steps, 2)
                own.after(dve.tensor_reduce(ss[:, 0], lat[:, :, 0:2 * P], AX, ALU.add))
                own.after(dve.tensor_reduce(ss[:, 1], lat[:, :, 2 * P:3 * P], AX, ALU.add))
                x1, x2 = kr[:, :, 0:half], kr[:, :, half:]
                r = [rot[:, a, :, b, :] for a in range(2) for b in range(2)]
                own.after(dve.tensor_tensor(r[0], x1, cos, ALU.mult))
                own.after(dve.tensor_tensor(r[1], x2, sin, ALU.mult))
                own.after(dve.tensor_tensor(r[2], x1, sin, ALU.mult))
                own.after(dve.tensor_tensor(r[3], x2, cos, ALU.mult))
                own.after(dve.tensor_tensor(x1, r[0], r[1], ALU.subtract))
                own.after(dve.tensor_tensor(x2, r[2], r[3], ALU.add))
                dve.wait_ge(act_steps, 5)
                for n, (x, a, row) in enumerate(((cq, QLORA, R_CQ), (ckv, KVLORA, R_CKV))):
                    own.after(dve.tensor_tensor(x, x, bcast(ss[:, n], [P, TT, a], 2), ALU.mult))
                    own.after(dve.tensor_tensor(x, x, bcast(k.row[:, row:row + a], [P, TT, a], 1), ALU.mult))
                dve.wait_ge(c_in, 32)
                own.after(dve.tensor_copy(km[:, 0:QT, :, NOPE:], bcast(kr[:, 0:QT], [P, QT, MLAH, ROPE], 2)))
                own.after(dve.tensor_copy(km[:, QT:2 * QT, :, NOPE:], bcast(krc[:, :, :], [P, QT, MLAH, ROPE], 2)))
                own.after(dve.memset(km[32:64, 2 * QT, :, :], 0.0))
                own.after(dve.memset(km[64:128, 2 * QT, :, :], 0.0))
                dve.tensor_copy(km[0:DEC, 2 * QT, :, NOPE:], bcast(kr[0:DEC, QT], [DEC, MLAH, ROPE], 1))
                dve.memset(qm[32:64, QT, :, :], 0.0)
                own.after(dve.memset(qm[64:128, QT, :, :], 0.0))
                for t in range(TT):
                    n = P if t < QT else DEC
                    dve.wait_ge(q_done, t + 1)
                    last = dve.tensor_copy(qm[0:n, t].rearrange("p h e -> p (h e)"), psQ[0:n, t % 2, 0:MLAH * MQK])
                    last.then_inc(q_out, 1)
                dve.wait_ge(k_out, KT)
                dve.wait_ge(q_out, TT)
                x1, x2 = qm[:, :, :, NOPE:NOPE + half], qm[:, :, :, NOPE + half:]
                cb, sb = (bcast(a, [P, TT, MLAH, half], 2) for a in (cos, sin))
                own.after(dve.tensor_tensor(rot[:, 0], x1, cb, ALU.mult))
                own.after(dve.tensor_tensor(rot[:, 1], x2, sb, ALU.mult))
                own.after(dve.tensor_tensor(rot[:, 0], rot[:, 0], rot[:, 1], ALU.subtract))
                own.after(dve.tensor_tensor(rot[:, 1], x1, sb, ALU.mult))
                own.after(dve.tensor_copy(x1, rot[:, 0]))
                own.after(dve.tensor_tensor(rot[:, 0], x2, cb, ALU.mult))
                own.after(dve.tensor_tensor(x2, rot[:, 0], rot[:, 1], ALU.add))
                for t in range(KT + TT):
                    dve.wait_ge(h_sq, t + 1)
                    dst = hs[:, 1, t] if t < KT else hs[:, 0, t - KT]
                    dve.tensor_reduce(dst, sq[:, t % 2], AX, ALU.add).then_inc(h_sum, 1)
                dve.wait_ge(a2, 2)
                for x, n, cnt, row in ((qm, 0, TT, R_MQ), (km, 1, KT, R_MK)):
                    own.after(dve.tensor_tensor(x[:, :, :, :], x[:, :, :, :], bcast(hs[:, n, 0:cnt], [P, cnt, MLAH, MQK], 3), ALU.mult))
                    own.after(dve.tensor_tensor(x[:, :, :, :], x[:, :, :, :], bcast(k.row[:, row:row + MQK], [P, cnt, MLAH, MQK], 1, 1), ALU.mult))

            @block.tensor
            def _(pe):
                pe.wait_ge(c_in, 32)
                pe.wait_ge(w_in, 32)
                pe.wait_ge(d, 12)

                def turn(j):
                    n, t = latents(j)
                    if j >= 2:
                        pe.wait_ge(x_out, j - 1)
                    for c in range(3):
                        if t is None and c < 2:
                            continue
                        src = (ckc[:, j - QT, :] if t is None else
                               (cq[0:n, t, c * P:(c + 1) * P] if c < 2 else ckv[0:n, t, :]))
                        last = pe.transpose(psX[:, j % 2, c * P:c * P + n], src, ident[0:n, 0:n])
                    last.then_inc(turned, 1)

                turn(0)
                nq = 0
                for j in range(KT):
                    if j + 1 < KT:
                        turn(j + 1)
                    n, t = latents(j)
                    pe.wait_ge(x_out, j + 1)
                    if t is not None:
                        if nq >= 2:
                            pe.wait_ge(q_out, nq - 1)
                        for c in range(2):
                            last = pe.matmul(psQ[0:n, nq % 2, 0:MLAH * MQK], cT[:, j % 2, c, 0:n], wuq[:, c, :],
                                             start=(c == 0), stop=(c == 1))
                        last.then_inc(q_done, 1)
                        nq += 1
                    if j >= 2:
                        pe.wait_ge(k_out, j - 1)
                    pe.matmul(psK[0:n, j % 2, :], cT[:, j % 2, 2, 0:n], wukv[:, :], start=True, stop=True)\
                      .then_inc(k_done, 1)


def w_out_block(k, lay, step):
    return k.w_out[lay].rearrange("(c p) n -> p c n", p=P)[:, :, bass.ds(step * P, P)]


def project_out(nc, k, lay, hi, lo, xT, raw):
    with ExitStack() as s:
        whi = s.enter_context(nc.sbuf_tensor("ohi", [P, 2, DC, P], F32R))
        wlo = s.enter_context(nc.sbuf_tensor("olo", [P, 2, DC, P], F32R))
        ps = s.enter_context(nc.psum_tensor("ops", [P, 2, NT, 512], F32))
        sem = k.sems["wout"]
        raw_in, hi_done, lo_done, x_in, tile_done, added = (sem[n] for n in ("raw", "hi", "lo", "x", "done", "add"))

        def steps(eng, body):
            for b in range(2):
                body(0, b)
            with eng.Fori(1, DC // 2) as i:
                for b in range(2):
                    body(i, b)

        with nc.Block() as block:

            @block.sync
            def _(sp):
                def body(i, b):
                    if is_first(i):
                        return
                    sp.wait_ge(lo_done[b], i)
                    sp.dma_start(raw[:, b], w_out_block(k, lay, 2 * i + b)).then_inc(raw_in[b], 16)
                steps(sp, body)

            @block.scalar
            def _(act):
                def body(i, b):
                    act.wait_ge(raw_in[b], 16 * i + 16)
                    if not is_first(i):
                        act.wait_ge(tile_done[b], i * NT)
                    act.activation(whi[:, b], raw[:, b], ACT.Copy).then_inc(hi_done[b], 1)
                steps(act, body)

            @block.gpsimd
            def _(pool):
                def body(i, b):
                    pool.wait_ge(hi_done[b], i + 1)
                    if not (is_first(i) and b == 0):
                        pool.wait_ge(lo_done[1 - b], i + b)
                    pool.tensor_tensor(wlo[:, b], raw[:, b], whi[:, b].bitcast(F32), ALU.subtract)\
                        .then_inc(lo_done[b], 1)
                steps(pool, body)

            @block.tensor
            def _(pe):
                def body(i, b):
                    pe.wait_ge(lo_done[b], i + 1)
                    for t in range(NT):
                        if not is_first(i):
                            pe.wait_ge(added[b], (i - 1) * NT + (t + 1))
                        at = slice(t * TN, (t + 1) * TN)
                        for c in range(DC):
                            for m, (w, a) in enumerate(((whi, hi), (wlo, hi), (whi, lo))):
                                last = pe.matmul(ps[:, b, t, 0:TN], w[:, b, c, :], a[:, c, at],
                                                 start=(c == 0 and m == 0), stop=(c == DC - 1 and m == 2))
                        last.then_inc(tile_done[b], 1)
                steps(pe, body)

            @block.vector
            def _(dve):
                dve.wait_ge(x_in, 16)

                def body(i, b):
                    for t in range(NT):
                        dve.wait_ge(tile_done[b], i * NT + (t + 1))
                        x = xT[:, bass.ds(2 * i + b, 1), t * TN:(t + 1) * TN]
                        dve.tensor_tensor(x, x, ps[:, b, t:t + 1, 0:TN], ALU.add).then_inc(added[b], 1)
                steps(dve, body)


def up_block(k, lay, col):
    return k.w_ffn_up[lay].rearrange("(c p) n -> p c n", p=P)[:, :, bass.ds(col, P)]


def conv_ffn(nc, k, lay, hi, lo, xT, raw):
    PAIRS = FC // 2
    EXT = CW - 1
    RW = TOK + 2 * EXT
    CL = RW - EXT
    SB = SEQ + EXT
    A0, B0, D0, D1, A1, B1 = range(6)
    with ExitStack() as s:
        T = lambda n, shape, dt=F32: s.enter_context(nc.sbuf_tensor("f" + n, shape, dt))
        whi, wlo = T("whi", [P, 6, DC, P], F32R), T("wlo", [P, 6, DC, P], F32R)
        ax = T("ax", [P, 2, RW])
        cb = T("cb", [P, 2, CL])
        uhi, ulo = T("uhi", [P, 2, TOK], F32R), T("ulo", [P, 2, TOK], F32R)
        tail = T("tail", [P, 2 * EXT, FC])
        tl = T("tl", [2 * EXT * FC, P])
        psA = s.enter_context(nc.psum_tensor("fpsA", [P, NT, 512], F32))
        psB = s.enter_context(nc.psum_tensor("fpsB", [P, NT, 512], F32))
        psD = s.enter_context(nc.psum_tensor("fpsD", [P, 2, 512], F32))
        sem = k.sems["ffn"]
        (cleared, raw_in, hi_done, split, a_done, a_out, row_done, conv_steps, conv_done, gelu_done,
         b_done, b_out, u_hi, u_lo, p_done, p_out, t_done, t_out, stored) = (sem[n] for n in (
             "clr", "raw", "hi", "split", "a", "ao", "row", "cs", "conv", "gelu", "b", "bo", "uh", "ul",
             "p", "po", "t", "to", "st"))
        down = k.w_ffn_down[lay].rearrange("(j p) (m n) -> j p m n", p=P, n=P)
        vcw = k.vec[:, V_CW:V_CB].rearrange("p (w c) -> p w c", c=FC)
        vst = k.vec[:, V_ST:V_N].rearrange("p (t c) -> p t c", c=FC)

        def before(g):
            return 6 * g - 2

        def each_round(eng, body):
            body(0, (A0, B0, A1, B1), 0)
            with eng.Fori(1, PAIRS) as g:
                body(g, (A0, B0, D0, D1, A1, B1), before(g))
            body(PAIRS, (D0, D1), before(PAIRS))

        with nc.Block() as block:

            @block.sync
            def _(sp):
                def body(g, roles, n0):
                    for o, r in enumerate(roles):
                        if is_first(g) and o < 2:
                            continue
                        if r in (D0, D1):
                            src = down[bass.ds(2 * (g - 1) + (r - D0), 1)].rearrange("j p m n -> p (j m) n")
                        else:
                            col = (2 * g + (r >= A1)) * P + (DFF if r in (B0, B1) else 0)
                            src = up_block(k, lay, col)
                        sp.wait_ge(split, n0 + (o - 1))
                        sp.dma_start(raw[:, o % 2], src).then_inc(raw_in[o % 2], 16)
                each_round(sp, body)
                sp.wait_ge(t_out, 1)
                row = lambda d: d[lay, 0].rearrange("t (c p) -> (t c) p", p=P)
                sp.dma_start(row(k.ffn_conv_p), tl[0:EXT * FC, :]).then_inc(stored, 16)
                sp.dma_start(row(k.ffn_conv_s), tl[EXT * FC:2 * EXT * FC, :]).then_inc(stored, 16)
                sp.wait_ge(stored, 32)

            @block.gpsimd
            def _(pool):
                for b in range(2):
                    pool.memset(ax[:, b, 0:EXT], 0.0).then_inc(cleared, 1)
                    pool.wait_ge(cleared, b + 1)

                def body(g, roles, n0):
                    for o, r in enumerate(roles):
                        if not (isinstance(g, int) and n0 + o == 0):
                            pool.wait_ge(split, n0 + o)
                        pool.wait_ge(hi_done, n0 + (o + 1))
                        pool.tensor_tensor(wlo[:, r], raw[:, o % 2], whi[:, r].bitcast(F32), ALU.subtract)\
                            .then_inc(split, 1)
                each_round(pool, body)

            @block.tensor
            def _(pe):
                three = lambda a, b: ((a[0], b[0]), (a[1], b[0]), (a[0], b[1]))

                def up_chunk(g, e, n):
                    first = isinstance(g, int) and g == 0 and e == 0
                    for ps, role, done, out in ((psA, (A0, A1)[e], a_done, a_out), (psB, (B0, B1)[e], b_done, b_out)):
                        pe.wait_ge(split, n + 1 if ps is psA else n + 2)
                        for t in range(NT):
                            if not first:
                                pe.wait_ge(out, 6 * g + (3 * e + t - 2))
                            at = slice(t * TN, (t + 1) * TN)
                            for c in range(DC):
                                for m, (w, x) in enumerate(three((whi, wlo), (hi, lo))):
                                    last = pe.matmul(ps[:, t, 0:TN], w[:, role, c, :], x[:, c, at],
                                                     start=(c == 0 and m == 0), stop=(c == DC - 1 and m == 2))
                            last.then_inc(done, 1)

                def down_pair(g, n):
                    pe.wait_ge(split, n + 2)
                    pe.wait_ge(u_lo, 2 * g)
                    for m in range(DC):
                        for t in range(NT):
                            o = m * NT + t
                            pe.wait_ge(p_out[o % 2], 12 * (g - 1) + (o // 2 + 1))
                            at = slice(t * TN, (t + 1) * TN)
                            for e in range(2):
                                for i, (w, x) in enumerate(three((whi, wlo), (uhi, ulo))):
                                    last = pe.matmul(psD[:, o % 2, 0:TN], w[:, D0 + e, m, :], x[:, e, at],
                                                     start=(e == 0 and i == 0), stop=(e == 1 and i == 2))
                            last.then_inc(p_done[o % 2], 1)

                def body(g, roles, n0):
                    o = 0
                    if A0 in roles:
                        up_chunk(g, 0, n0)
                        o += 2
                    if D0 in roles:
                        down_pair(g, n0 + o)
                        o += 2
                    if A1 in roles:
                        up_chunk(g, 1, n0 + o)
                each_round(pe, body)
                pe.wait_ge(row_done, FC)
                pe.transpose(psA[0:2 * EXT * FC, 0, 0:P], tail[:, :, :].rearrange("p t c -> p (t c)"),
                             k.const[:, C_ID:C_ID + P]).then_inc(t_done, 1)

            @block.scalar
            def _(act):
                act.wait_ge(cleared, 2)
                rest = SEQ - 2 * TN

                def high_weights(g, roles, o):
                    peeled = isinstance(g, int)
                    for r in roles:
                        at = (6 * g - 2 if peeled and g else 0 if peeled else before(g)) + o
                        half_at = o // 2 if peeled and g == 0 else 3 * g + (o // 2 - 1)
                        act.wait_ge(raw_in[o % 2], 16 * half_at + 16)
                        if not (peeled and g == 0):
                            if r in (A0, B0):
                                act.wait_ge(b_done, 6 * g - 3)
                            elif r in (A1, B1):
                                act.wait_ge(b_done, 6 * g)
                            else:
                                act.wait_ge(p_out[1], 12 * g - 11)
                        act.activation(whi[:, r], raw[:, o % 2], ACT.Copy).then_inc(hi_done, 1)
                        o += 1

                def rows_of(g, e):
                    ch = 2 * g + e
                    if not (isinstance(g, int) and g == 0):
                        act.wait_ge(conv_done, 2 * g + (e - 1))
                    act.activation(ax[:, e, SB:SB + EXT], vst[:, :, bass.ds(ch, 1)].rearrange("p t c -> p (t c)"), ACT.Copy)
                    for t in range(NT):
                        act.wait_ge(a_done, 6 * g + (3 * e + t + 1))
                        if t < NT - 1:
                            act.activation(ax[:, e, EXT + t * TN:EXT + (t + 1) * TN], psA[:, t, 0:TN], ACT.Copy)\
                               .then_inc(a_out, 1)
                        else:
                            act.activation(ax[:, e, EXT + t * TN:EXT + SEQ], psA[:, t, 0:rest], ACT.Copy)
                            act.activation(ax[:, e, SB + EXT:RW], psA[:, t, rest:TN], ACT.Copy).then_inc(a_out, 1)
                    act.wait_ge(a_out, 6 * g + (3 * e + NT))
                    tl_v = lambda a: tail[:, a:a + EXT, bass.ds(ch, 1)].rearrange("p t c -> p (t c)")
                    act.activation(tl_v(0), ax[:, e, SEQ:SEQ + EXT], ACT.Copy)
                    act.activation(tl_v(EXT), ax[:, e, RW - EXT:RW], ACT.Copy).then_inc(row_done, 1)
                    act.wait_ge(conv_done, 2 * g + (e + 1))
                    act.activation(cb[:, e, :], cb[:, e, :], ACT.Gelu_apprx_tanh).then_inc(gelu_done, 1)

                def high_of(g, e):
                    act.wait_ge(b_out, 6 * g + (3 * e + NT))
                    if not (isinstance(g, int) and g == 0):
                        act.wait_ge(p_done[1], 12 * g)
                    act.activation(uhi[:, e, 0:SEQ], cb[:, e, 0:SEQ], ACT.Copy)
                    act.activation(uhi[:, e, SEQ:TOK], cb[:, e, SB:CL], ACT.Copy).then_inc(u_hi, 1)

                def body(g, last=False):
                    zero = isinstance(g, int) and g == 0
                    if not zero:
                        high_weights(g, (D0, D1), 2)
                    rows_of(g, 0)
                    high_weights(g, (A1, B1), 2 if zero else 4)
                    high_of(g, 0)
                    if not last:
                        high_weights(g + 1, (A0, B0), 0)
                    rows_of(g, 1)
                    if last:
                        high_weights(PAIRS, (D0, D1), 0)
                    high_of(g, 1)

                high_weights(0, (A0, B0), 0)
                body(0)
                with act.Fori(1, PAIRS - 1) as g:
                    body(g)
                body(PAIRS - 1, last=True)
                act.wait_ge(t_done, 1)
                act.activation(tl[:, :], psA[0:2 * EXT * FC, 0, 0:P], ACT.Copy).then_inc(t_out, 1)

            @block.vector
            def _(dve):
                rest = SEQ - 2 * TN
                for b in range(2):
                    dve.memset(cb[:, b, 0:1], 0.0).then_inc(p_out[b], 1)
                    dve.wait_ge(p_out[b], 1)

                def conv_of(g, e):
                    ch = 2 * g + e
                    own = Steps(dve, conv_steps, 4 * g + 2 * e)
                    dve.wait_ge(row_done, 2 * g + (e + 1))
                    if not (isinstance(g, int) and g == 0):
                        dve.wait_ge(u_hi, 2 * g + (e - 1))
                    w = lambda j: vcw[:, j, bass.ds(ch, 1)]
                    c = cb[:, e, :]
                    own.after(dve.tensor_scalar(c, ax[:, e, 0:CL], w(0), k.vec[:, bass.ds(V_CB + ch, 1)], ALU.mult, ALU.add))
                    own.after(dve.scalar_tensor_tensor(c, ax[:, e, 1:1 + CL], w(1), c, ALU.mult, ALU.add))
                    dve.scalar_tensor_tensor(c, ax[:, e, 2:2 + CL], w(2), c, ALU.mult, ALU.add).then_inc(conv_done, 1)

                def gate_of(g, e):
                    dve.wait_ge(gelu_done, 2 * g + (e + 1))
                    for t in range(NT):
                        dve.wait_ge(b_done, 6 * g + (3 * e + t + 1))
                        if t < NT - 1:
                            v = cb[:, e, t * TN:(t + 1) * TN]
                            dve.tensor_tensor(v, v, psB[:, t, 0:TN], ALU.mult).then_inc(b_out, 1)
                        else:
                            v = cb[:, e, t * TN:SEQ]
                            dve.tensor_tensor(v, v, psB[:, t, 0:rest], ALU.mult)
                            v = cb[:, e, SB:CL]
                            dve.tensor_tensor(v, v, psB[:, t, rest:TN], ALU.mult).then_inc(b_out, 1)

                def low_of(g, e):
                    dve.wait_ge(u_hi, 2 * g + (e + 1))
                    dve.tensor_tensor(ulo[:, e, 0:SEQ], cb[:, e, 0:SEQ], uhi[:, e, 0:SEQ].bitcast(F32), ALU.subtract)
                    dve.tensor_tensor(ulo[:, e, SEQ:TOK], cb[:, e, SB:CL], uhi[:, e, SEQ:TOK].bitcast(F32), ALU.subtract)\
                       .then_inc(u_lo, 1)

                def add_pair(g):
                    for m in range(DC):
                        for t in range(NT):
                            o = m * NT + t
                            dve.wait_ge(p_done[o % 2], 12 * (g - 1) + (o // 2 + 1))
                            x = xT[:, m, t * TN:(t + 1) * TN]
                            last = dve.tensor_tensor(x, x, psD[:, o % 2, 0:TN], ALU.add)
                            last.then_inc(p_out[o % 2], 1)

                def body(g, roles, n0):
                    if A0 in roles:
                        conv_of(g, 0)
                        gate_of(g, 0)
                    if D0 in roles:
                        add_pair(g)
                    if A0 in roles:
                        low_of(g, 0)
                        conv_of(g, 1)
                        gate_of(g, 1)
                        low_of(g, 1)
                each_round(dve, body)


def restart(nc, sems):
    with nc.Block() as block:

        @block.gpsimd
        def _(pool):
            for x in sems:
                pool.sem_clear(x)


def program(nc, k):
    alloc = lambda n: nc.alloc_semaphore(n)
    many = lambda n, m: [alloc(f"{n}{i}") for i in range(m)]
    k.sems = {
        "tok": dict(const=alloc("tok_const"), a=many("tok_rows", 2),
                    b=many("tok_turned", 2), c=many("tok_copied", 2)),
        "out": dict(b=many("out_turned", 2), c=many("out_copied", 2), s=many("out_stored", 2)),
    }
    layer, k.lists = [], {}

    def group(name, singles, several=()):
        d = {n: alloc(f"{name}_{n}") for n in singles.split()}
        for n, m in several:
            d[n] = many(f"{name}_{n}", m)
        for v in d.values():
            layer.extend(v if isinstance(v, list) else [v])
        k.sems[name] = d
        k.lists[name] = [x for v in d.values() for x in (v if isinstance(v, list) else [v])]

    group("vec", "l t r v d")
    group("norm", "sq sum ln rs hf hi lo lp")
    group("x", "st")
    group("win", "", [("raw", 2), ("hi", 2), ("lo", 2), ("done", 3), ("tf", 3)])
    group("fox", "cl st act dve f fc ft rh")
    group("mla", "w c st sq act dve t xo q k qo ko hsq hsum a2")
    group("att", "clr ld x xh xl s m e n t tl th o y d iv pn", [("row", 2)])
    group("smp", "in z qt qd x k s d m e n t o y", [("xo", 2), ("to", 2)])
    group("wout", "x", [("raw", 2), ("hi", 2), ("lo", 2), ("done", 2), ("add", 2)])
    group("ffn", "clr hi split a ao row cs conv gelu b bo uh ul t to st", [("raw", 2), ("p", 2), ("po", 2)])

    with ExitStack() as s:
        T = lambda n, shape, dt=F32: s.enter_context(nc.sbuf_tensor(n, shape, dt))
        k.const = T("const", [P, C_N])
        k.identr, k.mfoxr, k.mmlar = (T(n, [P, P], F32R) for n in ("identr", "mfoxr", "mmlar"))
        k.vec, k.row = T("vec", [P, V_N]), T("row", [P, R_N])
        load_tokens(nc, k)
        with nc.Fori(0, DEPTH) as lay:
            one_layer(nc, k, lay)
            restart(nc, layer)
        store_tokens(nc, k)


def one_layer(nc, k, lay):
    left, right = ExitStack(), ExitStack()

    def lt(n, shape, dt=F32):
        return left.enter_context(nc.sbuf_tensor(n, shape, dt))

    def rt(n, shape, dt=F32, where=right):
        return where.enter_context(nc.sbuf_tensor(n, shape, dt, side="right"))

    def first_blocks(sp, raw, sems, block):
        for b in range(2):
            sp.dma_start(raw[:, b], block(b)).then_inc(sems[b], 16)

    hi, lo = rt("h_hi", [P, DC, TOK], F32R), rt("h_lo", [P, DC, TOK], F32R)
    wraw = rt("wraw", [P, 2, DC, WN])
    with ExitStack() as f:
        xT = f.enter_context(x_home(nc, k, "xT1"))
        x_stored = k.sems["x"]["st"]

        def also(sp):
            sp.dma_start(k.x_dram, xT[:, :, :]).then_inc(x_stored, 16)
            first_blocks(sp, wraw, k.sems["win"]["raw"], lambda b: w_in_block(k, lay, b))
            sp.wait_ge(x_stored, 16)

        norm(nc, k, xT, hi, lo, V_G1, "1", [(0, DC)], also, Vectors(nc, k, lay, f))
    proj = lt("proj", [P, TT, IN_W])
    prepared = ExitStack()
    prep = Prepare(nc, k, lay, prepared, proj)
    project_in(nc, k, lay, hi, lo, proj, wraw, prep)
    right.close()

    yT = rt("yT", [P, DC, TOK])
    with prepared as f:
        fs = prep.fs
        with ExitStack() as f2:
            frow = [f2.enter_context(nc.sbuf_tensor("frow" + n, [FOXH, SEQ], F32R)) for n in ("hi", "lo")]
            fox_rows(nc, k, prep, frow)
            cols = lambda o: (lambda h: proj[:, :, o + HD * h:o + HD * (h + 1)])
            attend_prompt(nc, k, "fox", FOXH, HD, cols(O_FQ), cols(O_FK),
                          lambda h, t: proj[:, t, O_FV + HD * h:O_FV + HD * (h + 1)], lambda h: h, yT, 0, frow=frow)
        kc = f.enter_context(nc.sbuf_tensor("fkc", [P, QT, FOXH * HD], F32))
        vc = f.enter_context(nc.sbuf_tensor("fvc", [P, QT, FOXH * HD], F32))
        loads = [(dst[:, :, :], src[lay, 0].rearrange("(t p) h d -> p t (h d)", p=P))
                 for dst, src in ((kc, k.cache_fox_k), (vc, k.cache_fox_v))]
        tiles = [(P, lambda u, t=t: kc[:, t, P * u:P * (u + 1)], lambda p, t=t: vc[:, t, P * p:P * (p + 1)])
                 for t in range(QT)]
        tiles.append((DEC, lambda u: proj[0:DEC, QT, O_FK + P * u:O_FK + P * (u + 1)],
                      lambda p: proj[0:DEC, QT, O_FV + P * p:O_FV + P * (p + 1)]))
        attend_sample(nc, k, "fox", FOXH, lambda u: proj[0:DEC, QT, O_FQ + P * u:O_FQ + P * (u + 1)], FOXH // 2, P,
                      lambda h: HD * (h % 2), tiles, loads, yT, 0, fs)

    attend_prompt(nc, k, "swa", SWAH, HD, cols(O_SQ), cols(O_SK),
                  lambda g, t: proj[:, t, O_SV + HD * g:O_SV + HD * (g + 1)], lambda h: h // (SWAH // SWAKV), yT, 3,
                  alibi=k.alibi)
    with ExitStack() as f:
        old = WIN - CHUNK
        kc = f.enter_context(nc.sbuf_tensor("skc", [old, P], F32))
        vc = f.enter_context(nc.sbuf_tensor("svc", [old, P], F32))
        loads = [(dst[:, :], src[lay, 0, CHUNK:WIN].rearrange("t h d -> t (h d)"))
                 for dst, src in ((kc, k.cache_swa_k), (vc, k.cache_swa_v))]
        tiles = [(old, lambda u: kc[:, :], lambda p: vc[:, :]),
                 (DEC, lambda u: proj[0:DEC, QT, O_SK:O_SV], lambda p: proj[0:DEC, QT, O_SV:O_CQ])]
        attend_sample(nc, k, "swa", SWAH, lambda u: proj[0:DEC, QT, O_SQ + P * u:O_SQ + P * (u + 1)], 1, P,
                      lambda h: HD * (h // (SWAH // SWAKV)), tiles, loads, yT, 3)

    with ExitStack() as f:
        qm = rt("qm", [P, TT, MLAH, MQK], where=f)
        km = rt("km", [P, 2 * QT + 1, MLAH, MQK], where=f)
        vm = rt("vm", [P, 2 * QT + 1, MLAH, HD], where=f)
        mla_prepare(nc, k, lay, proj, qm, km, vm)
        left.close()
        attend_prompt(nc, k, "mla", MLAH, MQK, lambda h: qm[:, :, h, :], lambda h: km[:, :, h, :],
                      lambda h, t: vm[:, t, h, :], lambda h: h, yT, 6)
        tiles = [(P if j < QT else DEC, lambda u, j=j: km[0:P if j < QT else DEC, QT + j, u, :],
                  lambda p, j=j: vm[0:P if j < QT else DEC, QT + j, 2 * p:2 * p + 2, :].rearrange("p h d -> p (h d)"))
                 for j in range(TT)]
        attend_sample(nc, k, "mla", MLAH, lambda h: qm[0:DEC, QT, h, :], MLAH, MQK, lambda h: HD * (h % 2), tiles,
                      [], yT, 6)

    xT = left.enter_context(x_home(nc, k, "xT2"))
    with ExitStack() as f:
        T = lambda n, shape, dt=F32: f.enter_context(nc.sbuf_tensor(n, shape, dt))
        hi, lo, raw = T("y_hi", [P, DC, TOK], F32R), T("y_lo", [P, DC, TOK], F32R), T("oraw", [P, 2, DC, P])

        def also(sp):
            first_blocks(sp, raw, k.sems["wout"]["raw"], lambda b: w_out_block(k, lay, b))
            sp.dma_start(xT[:, :, :], k.x_dram).then_inc(k.sems["wout"]["x"], 16)

        norm(nc, k, yT, hi, lo, V_GM, "2", [(0, 3), (3, 6), (6, 8)], also)
        right.close()
        project_out(nc, k, lay, hi, lo, xT, raw)
    with ExitStack() as f:
        T = lambda n, shape, dt=F32: f.enter_context(nc.sbuf_tensor(n, shape, dt))
        hi, lo, raw = T("g_hi", [P, DC, TOK], F32R), T("g_lo", [P, DC, TOK], F32R), T("fraw", [P, 2, DC, P])

        def also(sp):
            first_blocks(sp, raw, k.sems["ffn"]["raw"], lambda b: up_block(k, lay, b * DFF))

        norm(nc, k, xT, hi, lo, V_G2, "3", [(0, DC)], also)
        conv_ffn(nc, k, lay, hi, lo, xT, raw)
    left.close()


_INS = ['x_prompt', 'x_sample', 'cache_fox_k', 'cache_fox_v', 'cache_fox_logf', 'cache_swa_k', 'cache_swa_v',
        'cache_mla_ckv', 'cache_mla_krope', 'state_ffn_conv', 'g_norm1', 'w_in', 'b_fox_f', 'g_fox_q', 'g_fox_k',
        'g_swa_q', 'g_swa_k', 'swa_sinks', 'g_mla_cq', 'g_mla_ckv', 'w_mla_uq', 'w_mla_ukv', 'g_mla_q', 'g_mla_k',
        'g_mix_out', 'w_out', 'g_norm2', 'w_ffn_up', 'w_ffn_conv', 'b_ffn_conv', 'w_ffn_down']
_STREAM = lambda T, win: [(DEPTH, 1, T, FOXH, HD), (DEPTH, 1, T, FOXH, HD), (DEPTH, 1, T, FOXH),
                          (DEPTH, 1, win, SWAKV, HD), (DEPTH, 1, win, SWAKV, HD), (DEPTH, 1, T, KVLORA),
                          (DEPTH, 1, T, ROPE), (DEPTH, 1, CW - 1, DFF)]
_PARTS = ['fox_k', 'fox_v', 'fox_logf', 'swa_k', 'swa_v', 'mla_ckv', 'mla_krope', 'ffn_conv']
_OUTS = [('y_prompt', (1, SEQ, D)), ('y_sample', (1, DEC, D))] + \
    [(n + '_p', s) for n, s in zip(_PARTS, _STREAM(SEQ, WIN))] + \
    [(n + '_s', s) for n, s in zip(_PARTS, _STREAM(DEC, WIN))]


def kernel(**inputs):
    import concourse.bacc as _bacc
    from concourse.bass_utils import run_bass_kernel_spmd as _run

    nc = _bacc.Bacc("TRN2", target_bir_lowering=False, num_devices=1)
    arrays = {f"in_{name}": np.ascontiguousarray(inputs[name]) for name in _INS}
    arrays["in_const"], arrays["in_alibi"] = const_table(), alibi_table()
    k = Chip()
    for name in _INS:
        a = arrays[f"in_{name}"]
        ap = nc.dram_tensor(f"in_{name}", a.shape, F32, kind="ExternalInput").ap()
        k.__dict__[name] = ap[0] if name.startswith("x_") else ap
    k.consts = nc.dram_tensor("in_const", (P, C_N), F32, kind="ExternalInput").ap()
    k.alibi = nc.dram_tensor("in_alibi", (P, SWAH, 2 * P), F32, kind="ExternalInput").ap()
    for name, shape in _OUTS:
        ap = nc.dram_tensor(f"out_{name}", shape, F32, kind="ExternalOutput").ap()
        k.__dict__[name] = ap[0] if name.startswith("y_") else ap
    k.x_dram = nc.dram_tensor("x_between", (P, DC, TOK), F32, kind="Internal").ap()
    program(nc, k)
    r = _run(nc, [arrays], core_ids=[0])
    return tuple(r.results[0][f"out_{name}"] for name, _ in _OUTS)
```

```python
import math
from contextlib import ExitStack, contextmanager

import numpy as np
import concourse.bass as bass
from concourse import mybir

F32 = mybir.dt.float32
F32R = mybir.dt.float32r
ACT = mybir.ActivationFunctionType
ALU = mybir.AluOpType
AX = mybir.AxisListType.X

P = 128
D = 1024
SEQ = 1024
DEC = 32
PAST = 1024
DEPTH = 2
TOK = SEQ + DEC
DC = D // P
QT = SEQ // P
TT = QT + 1
NT = 3
TN = TOK // NT
HD = 64
FOXH, SWAH, SWAKV, MLAH = 6, 6, 2, 4
CHUNK = 64
WIN = 128
QLORA, KVLORA, NOPE, ROPE = 256, 128, 64, 32
MQK = NOPE + ROPE
DFF = 2816
FC = DFF // P
CW = 3
EPS = 1e-6
BIG = -1e30
O_FQ, O_FK, O_FV, O_G = 0, 384, 768, 1152
O_SQ, O_SK, O_SV = 1158, 1542, 1670
O_CQ, O_CKV, O_KR = 1798, 2054, 2182
IN_W = 2214
WN = 246
WSTEPS = IN_W // WN
V_G1, V_G2, V_GM, V_CW, V_CB, V_ST = 0, 8, 16, 24, 24 + CW * FC, 24 + (CW + 1) * FC
V_N = V_ST + 2 * FC
R_FQ, R_FK, R_SQ, R_SK = 0, 64, 128, 192
R_CQ, R_CKV, R_MQ, R_MK, R_BF, R_SINK = 256, 512, 640, 736, 832, 838
R_N = 844
SLOPES = [2.0 ** (-8.0 * (h + 1) / SWAH) for h in range(SWAH)]


class Steps:

    def __init__(self, eng, sem, base=0):
        self.eng, self.sem, self.base, self.n = eng, sem, base, 0

    def mark(self, ins):
        ins.then_inc(self.sem, 1)
        self.n += 1
        return self.n

    def wait(self, n):
        self.eng.wait_ge(self.sem, self.base + n)

    def after(self, ins):
        self.wait(self.mark(ins))


def is_first(i):
    return isinstance(i, int) and i == 0


def bcast(ap, shape, *axes):
    for a in axes:
        ap = ap.unsqueeze(a)
    return ap.broadcast_to(shape)


C_ID, C_TRI, C_ONE, C_MFOX, C_MMLA, C_COS = 0, 128, 256, 384, 512, 640
C_SIN = C_COS + TT * ROPE // 2
C_MNEW = C_SIN + TT * ROPE // 2
C_SEL = C_MNEW + DEC
C_BSW = C_SEL + 2 * P
SKEYS = WIN - CHUNK + DEC
C_EPS = C_BSW + 2 * SKEYS
C_N = C_EPS + 1


def const_table():
    c = np.zeros((P, C_N), np.float32)
    p = np.arange(P)
    c[:, C_ID:C_ID + P] = np.eye(P)
    c[:, C_TRI:C_TRI + P] = p[:, None] <= p[None, :]
    c[:, C_ONE:C_ONE + P] = 1
    c[:, C_MFOX:C_MFOX + P] = np.where(p[None, :] <= p[:, None], 0, BIG)
    c[:, C_MMLA:C_MMLA + P] = np.where(p[None, :] // CHUNK <= p[:, None] // CHUNK, 0, BIG)
    half = ROPE // 2
    inv = (np.float32(10000.0) ** (-np.arange(half, dtype=np.float32) / np.float32(half))).astype(np.float32)
    for t in range(TT):
        ang = (np.float32(P * t) + p.astype(np.float32))[:, None] * inv[None, :]
        c[:, C_COS + t * half:C_COS + (t + 1) * half] = np.cos(ang.astype(np.float64))
        c[:, C_SIN + t * half:C_SIN + (t + 1) * half] = np.sin(ang.astype(np.float64))
    q = p % DEC
    c[:, C_MNEW:C_MNEW + DEC] = np.where(np.arange(DEC)[None, :] <= q[:, None], 0, BIG)
    qpos = PAST + q[:, None]
    kpos = PAST - (WIN - CHUNK) + np.arange(SKEYS)[None, :]
    for g in range(2):
        for r in range(P):
            h = 4 * g + r // DEC
            if h < FOXH:
                c[h, C_SEL + g * P + r] = c[32 + h, C_SEL + g * P + r] = 1
                c[r, C_BSW + g * SKEYS:C_BSW + (g + 1) * SKEYS] = -SLOPES[h] * np.abs(qpos[r] - kpos[0])
    c[:, C_EPS] = EPS
    return c


def alibi_table():
    p, j = np.arange(P)[:, None], np.arange(2 * P)[None, :]
    qc, kc = (P + p) // CHUNK, j // CHUNK
    ok = (kc <= qc) & (kc > qc - WIN // CHUNK)
    return np.stack([np.where(ok, -s * np.abs(P + p - j), BIG) for s in SLOPES], 1).astype(np.float32)


class Chip:
    pass


@contextmanager
def x_home(nc, k, name):
    with nc.sbuf_tensor(name, [P, DC, TOK], F32) as place:
        if name == "xT":
            k.xT = place
        yield k.xT


def load_tokens(nc, k):
    with ExitStack() as s:
        xT = s.enter_context(x_home(nc, k, "xT"))
        xin = s.enter_context(nc.sbuf_tensor("xin", [P, 2, D], F32))
        ps = s.enter_context(nc.psum_tensor("xps", [P, 2, DC, P], F32))
        ident = k.const[:, C_ID:C_ID + P]
        sem = k.sems["tok"]
        const_in = sem["const"]
        rows_in, turned, copied = sem["a"], sem["b"], sem["c"]
        with nc.Block() as block:

            @block.sync
            def _(sp):
                sp.dma_start(k.const[:, :], k.consts).then_inc(const_in, 16)
                for t in range(TT):
                    if t >= 2:
                        sp.wait_ge(turned[t % 2], t // 2)
                    n = P if t < QT else DEC
                    src = k.x_prompt[t * P:t * P + n] if t < QT else k.x_sample
                    sp.dma_start(xin[0:n, t % 2, :], src).then_inc(rows_in[t % 2], 16)

            @block.tensor
            def _(pe):
                pe.wait_ge(const_in, 16)
                for t in range(TT):
                    n = P if t < QT else DEC
                    pe.wait_ge(rows_in[t % 2], 16 * (t // 2 + 1))
                    if t >= 2:
                        pe.wait_ge(copied[t % 2], t // 2)
                    for c in range(DC):
                        last = pe.transpose(ps[:, t % 2, c, 0:n], xin[0:n, t % 2, c * P:(c + 1) * P],
                                            ident[0:n, 0:n])
                    last.then_inc(turned[t % 2], 1)

            @block.scalar
            def _(act):
                act.wait_ge(const_in, 16)
                act.activation(k.identr[:, :], k.const[:, C_ID:C_ID + P], ACT.Copy)
                act.activation(k.mfoxr[:, :], k.const[:, C_MFOX:C_MFOX + P], ACT.Copy)
                act.activation(k.mmlar[:, :], k.const[:, C_MMLA:C_MMLA + P], ACT.Copy)
                for t in range(TT):
                    n = P if t < QT else DEC
                    act.wait_ge(turned[t % 2], t // 2 + 1)
                    act.activation(xT[:, :, t * P:t * P + n], ps[:, t % 2, :, 0:n], ACT.Copy)\
                       .then_inc(copied[t % 2], 1)


def store_tokens(nc, k):
    with ExitStack() as s:
        xT = s.enter_context(x_home(nc, k, "xT9"))
        xout = s.enter_context(nc.sbuf_tensor("xout", [P, 2, D], F32))
        ps = s.enter_context(nc.psum_tensor("yps", [P, 2, DC, P], F32))
        ident = k.const[:, C_ID:C_ID + P]
        sem = k.sems["out"]
        turned, copied, stored = sem["b"], sem["c"], sem["s"]
        with nc.Block() as block:

            @block.sync
            def _(sp):
                for t in range(TT):
                    n = P if t < QT else DEC
                    sp.wait_ge(copied[t % 2], t // 2 + 1)
                    dst = k.y_prompt[t * P:t * P + n] if t < QT else k.y_sample
                    sp.dma_start(dst, xout[0:n, t % 2, :]).then_inc(stored[t % 2], 16)
                sp.wait_ge(stored[0], 16 * (TT // 2 + 1))
                sp.wait_ge(stored[1], 16 * (TT // 2))

            @block.tensor
            def _(pe):
                for t in range(TT):
                    n = P if t < QT else DEC
                    if t >= 2:
                        pe.wait_ge(copied[t % 2], t // 2)
                    for c in range(DC):
                        last = pe.transpose(ps[0:n, t % 2, c, :], xT[:, c, t * P:t * P + n], ident)
                    last.then_inc(turned[t % 2], 1)

            @block.scalar
            def _(act):
                for t in range(TT):
                    n = P if t < QT else DEC
                    act.wait_ge(turned[t % 2], t // 2 + 1)
                    if t >= 2:
                        act.wait_ge(stored[t % 2], 16 * (t // 2))
                    act.activation(xout[0:n, t % 2, :], ps[0:n, t % 2, :, :].rearrange("p c n -> p (c n)"),
                                   ACT.Copy).then_inc(copied[t % 2], 1)


class Vectors:

    def __init__(self, nc, k, lay, s):
        self.k, self.lay = k, lay
        self.st = s.enter_context(nc.sbuf_tensor("vstage", [P, 2, P], F32))
        self.ps = s.enter_context(nc.psum_tensor("vps", [P, 2, P], F32))
        sem = k.sems["vec"]
        self.loaded, self.turned, self.rows_in, self.ready, self.scaled = (sem[n] for n in "ltrvd")
        self.rest = V_N - P
        self.feat = [(V_G1, k.g_norm1[lay].rearrange("(c p) -> c p", p=P)),
                     (V_G2, k.g_norm2[lay].rearrange("(c p) -> c p", p=P)),
                     (V_GM, k.g_mix_out[lay].rearrange("(c p) -> c p", p=P)),
                     (V_CW, k.w_ffn_conv[lay].rearrange("w (c p) -> (w c) p", p=P)),
                     (V_CB, k.b_ffn_conv[lay].rearrange("(c p) -> c p", p=P))]
        self.free = [(R_FQ, k.g_fox_q), (R_FK, k.g_fox_k), (R_SQ, k.g_swa_q), (R_SK, k.g_swa_k),
                     (R_CQ, k.g_mla_cq), (R_CKV, k.g_mla_ckv), (R_MQ, k.g_mla_q), (R_MK, k.g_mla_k),
                     (R_BF, k.b_fox_f), (R_SINK, k.swa_sinks)]

    def load(self, sp):
        k, lay, st = self.k, self.lay, self.st
        for at, src in self.feat:
            sp.dma_start(st[at:at + src.shape[0], 0, :], src).then_inc(self.loaded, 16)
        state = k.state_ffn_conv[lay, 0].rearrange("t (c p) -> (t c) p", p=P)
        split = P - V_ST
        sp.dma_start(st[V_ST:P, 0, :], state[0:split]).then_inc(self.loaded, 16)
        sp.dma_start(st[0:self.rest, 1, :], state[split:2 * FC]).then_inc(self.loaded, 16)
        for at, src in self.free:
            sp.dma_start(k.row[:, at:at + src.shape[1]], src[lay].partition_broadcast(P)).then_inc(self.rows_in, 16)

    def turn(self, pe):
        ident, rest = self.k.const[:, C_ID:C_ID + P], self.rest
        pe.wait_ge(self.loaded, 16 * (len(self.feat) + 2))
        pe.transpose(self.ps[:, 0, :], self.st[:, 0, :], ident)
        pe.transpose(self.ps[:, 1, 0:rest], self.st[0:rest, 1, :], ident[0:rest, 0:rest]).then_inc(self.turned, 1)

    def copy(self, act):
        act.wait_ge(self.turned, 1)
        act.activation(self.k.vec[:, 0:P], self.ps[:, 0, :], ACT.Copy)
        act.activation(self.k.vec[:, P:V_N], self.ps[:, 1, 0:self.rest], ACT.Copy).then_inc(self.ready, 1)

    def scale(self, dve):
        row = self.k.row
        dve.wait_ge(self.rows_in, 16 * len(self.free))
        for at, n, d in ((R_FQ, HD, HD), (R_SQ, HD, HD), (R_MQ, MQK, MQK)):
            last = dve.tensor_scalar(row[:, at:at + n], row[:, at:at + n], float(d) ** -0.5, None, ALU.mult)
        last.then_inc(self.scaled, 1)
        dve.wait_ge(self.scaled, 1)
        mq = row[:, R_MQ:R_MQ + MQK]
        dve.tensor_tensor(mq, mq, row[:, R_MK:R_MK + MQK], ALU.mult)


def norm(nc, k, xT, hi, lo, gain, tag, groups, also=None, vectors=None):
    with ExitStack() as s:
        G, HC = len(groups), DC // 2
        T = lambda n, shape: s.enter_context(nc.sbuf_tensor(n + tag, shape, F32))
        sq, hf, rs = T("nsq", [P, 2, DC, TN]), T("nhf", [P, 2, DC, TN]), T("nrs", [P, 2, G, TN])
        ps = s.enter_context(nc.psum_tensor("nps" + tag, [P, 2, G, 512], F32))
        sem = k.sems["norm"]
        squared, pool_squared, summed, logged, inverted, normed, hi_done, low, pool_low = (sem[n] for n in
                                                         ("sq", "ps", "sum", "ln", "rs", "hf", "hi", "lo", "lp"))
        ones = k.const[:, C_ONE:C_ONE + P]
        group_of = [g for g, (a, b) in enumerate(groups) for c in range(a, b)]
        cols = lambda t: slice(t * TN, (t + 1) * TN)
        half = lambda h: slice(h * HC, (h + 1) * HC)
        shared = HC + HC // 2
        with nc.Block() as block:

            @block.sync
            def _(sp):
                if vectors:
                    vectors.load(sp)
                also(sp)

            @block.scalar
            def _(act):
                def square(t):
                    if t >= 2:
                        act.wait_ge(summed, t - 1)
                    act.activation(sq[:, t % 2, half(0)], xT[:, half(0), cols(t)], ACT.Square).then_inc(squared, 1)

                def inverse_root(t):
                    act.wait_ge(summed, t + 1)
                    if t >= 2:
                        act.wait_ge(normed, DC * (t - 1))
                    for g, (a, b) in enumerate(groups):
                        act.activation(rs[:, t % 2, g, :], ps[:, t % 2, g, 0:TN], ACT.Ln, scale=1.0 / (P * (b - a)),
                                       bias=k.const[:, C_EPS:C_EPS + 1]).then_inc(logged, 1)
                    act.wait_ge(logged, G * (t + 1))
                    act.activation(rs[:, t % 2], rs[:, t % 2], ACT.Exp, scale=-0.5).then_inc(inverted, 1)

                square(0)
                square(1)
                inverse_root(0)
                if vectors:
                    vectors.copy(act)
                for t in range(NT):
                    if t + 2 < NT:
                        square(t + 2)
                    if t + 1 < NT:
                        inverse_root(t + 1)
                    for h in range(2):
                        act.wait_ge(normed, DC * t + HC * (h + 1))
                        act.activation(hi[:, half(h), cols(t)], hf[:, t % 2, half(h)], ACT.Copy).then_inc(hi_done, 1)

            @block.tensor
            def _(pe):
                for t in range(NT):
                    if t >= 2:
                        pe.wait_ge(logged, G * (t - 1))
                    for c in range(DC):
                        if c % HC == 0:
                            pe.wait_ge(pool_squared if c else squared, t + 1)
                        g = group_of[c]
                        last = pe.matmul(ps[:, t % 2, g, 0:TN], ones, sq[:, t % 2, c, :],
                                         start=(c == groups[g][0]), stop=(c == groups[g][1] - 1))
                    last.then_inc(summed, 1)
                    if vectors and t == 0:
                        vectors.turn(pe)

            @block.vector
            def _(dve):
                def low_half(t):
                    dve.wait_ge(hi_done, 2 * t + 1)
                    dve.tensor_tensor(lo[:, half(0), cols(t)], hf[:, t % 2, half(0)],
                                      hi[:, half(0), cols(t)].bitcast(F32), ALU.subtract).then_inc(low, 1)

                for t in range(NT):
                    dve.wait_ge(inverted, t + 1)
                    if vectors and t == 0:
                        dve.wait_ge(vectors.ready, 1)
                    if t >= 2:
                        dve.wait_ge(low, t - 1)
                        dve.wait_ge(pool_low, t - 1)
                    for c in range(DC):
                        dve.scalar_tensor_tensor(hf[:, t % 2, c, :], xT[:, c, cols(t)],
                                                 k.vec[:, gain + c:gain + c + 1], rs[:, t % 2, group_of[c], :],
                                                 ALU.mult, ALU.mult).then_inc(normed, 1)
                    if t >= 1:
                        low_half(t - 1)
                low_half(NT - 1)
                dve.wait_ge(hi_done, 2 * NT)
                dve.tensor_tensor(lo[:, shared:DC, cols(NT - 1)], hf[:, (NT - 1) % 2, shared:DC],
                                  hi[:, shared:DC, cols(NT - 1)].bitcast(F32), ALU.subtract)
                if vectors:
                    vectors.scale(dve)

            @block.gpsimd
            def _(pool):
                for t in range(NT):
                    if t >= 2:
                        pool.wait_ge(summed, t - 1)
                    if t:
                        pool.wait_ge(pool_squared, t)
                    x = xT[:, half(1), cols(t)]
                    pool.tensor_tensor(sq[:, t % 2, half(1)], x, x, ALU.mult).then_inc(pool_squared, 1)
                pool.wait_ge(pool_squared, NT)
                for t in range(NT):
                    pool.wait_ge(hi_done, 2 * t + 2)
                    if t:
                        pool.wait_ge(pool_low, t)
                    own = slice(HC, DC if t < NT - 1 else shared)
                    pool.tensor_tensor(lo[:, own, cols(t)], hf[:, t % 2, own],
                                       hi[:, own, cols(t)].bitcast(F32), ALU.subtract).then_inc(pool_low, 1)
    restart(nc, k.lists["norm"])


def w_in_column(step):
    return (WSTEPS - 2 + step) * WN if isinstance(step, int) and step < 2 else (step - 2) * WN


def w_in_steps(upto):
    return 2 if upto > (WSTEPS - 1) * WN else min(2 + -(-upto // WN), WSTEPS)


def w_in_block(k, lay, step):
    return k.w_in[lay].rearrange("(c p) n -> p c n", p=P)[:, :, bass.ds(w_in_column(step), WN)]


def project_in(nc, k, lay, hi, lo, proj, raw, beside):
    with ExitStack() as s:
        whi = s.enter_context(nc.sbuf_tensor("whi", [P, 2, DC, WN], F32R))
        wlo = s.enter_context(nc.sbuf_tensor("wlo", [P, 2, DC, WN], F32R))
        NB = 3
        ps = s.enter_context(nc.psum_tensor("wps", [P, NB, 512], F32))
        sem = k.sems["win"]
        raw_in, hi_done, lo_done, tile_done, tile_free = (sem[n] for n in ("raw", "hi", "lo", "done", "tf"))
        per = TT // NB

        def steps(eng, body):
            for b in range(2):
                body(0, b, b)
            with eng.Fori(1, WSTEPS // 2) as i:
                for b in range(2):
                    body(i, b, 2 * i + b)
            body(WSTEPS // 2, 0, WSTEPS - 1)

        def columns_ready(eng, upto):
            for b in range(NB):
                eng.wait_ge(tile_free[b], per * w_in_steps(upto))

        with nc.Block() as block:

            @block.sync
            def _(sp):
                def body(i, b, step):
                    if is_first(i):
                        return
                    sp.wait_ge(lo_done[b], i)
                    sp.dma_start(raw[:, b], w_in_block(k, lay, step)).then_inc(raw_in[b], 16)
                steps(sp, body)
                beside.load_store(sp, columns_ready)

            @block.vector
            def _(dve):
                beside.vector(dve, columns_ready)

            @block.gpsimd
            def _(pool):
                def body(i, b, step):
                    pool.wait_ge(hi_done[b], i + 1)
                    if not (is_first(i) and b == 0):
                        pool.wait_ge(lo_done[1 - b], i + b)
                    pool.tensor_tensor(wlo[:, b], raw[:, b], whi[:, b].bitcast(F32), ALU.subtract)\
                        .then_inc(lo_done[b], 1)
                steps(pool, body)

            @block.scalar
            def _(act):
                def split(step):
                    i, b = divmod(step, 2)
                    act.wait_ge(raw_in[b], 16 * i + 16)
                    act.activation(whi[:, b], raw[:, b], ACT.Copy).then_inc(hi_done[b], 1)

                split(0)
                for step in range(WSTEPS):
                    if step + 1 < WSTEPS:
                        split(step + 1)
                    for t in range(TT):
                        n, col = P if t < QT else DEC, w_in_column(step)
                        act.wait_ge(tile_done[t % NB], step * per + (t // NB + 1))
                        act.activation(proj[0:n, t, col:col + WN], ps[0:n, t % NB, 0:WN], ACT.Copy)\
                           .then_inc(tile_free[t % NB], 1)
                    if step == w_in_steps(IN_W):
                        beside.scalar_latents(act)
                    if step == w_in_steps(O_G + FOXH):
                        beside.scalar_fox(act)

            @block.tensor
            def _(pe):
                def body(i, b, step):
                    pe.wait_ge(lo_done[b], i + 1)
                    for t in range(TT):
                        n = P if t < QT else DEC
                        if not (is_first(step) and t < NB):
                            pe.wait_ge(tile_free[t % NB], step * per + t // NB)
                        at = slice(t * P, t * P + n)
                        for c in range(DC):
                            for m, (a, w) in enumerate(((hi, whi), (hi, wlo), (lo, whi))):
                                last = pe.matmul(ps[0:n, t % NB, 0:WN], a[:, c, at], w[:, b, c, :],
                                                 start=(c == 0 and m == 0), stop=(c == DC - 1 and m == 2))
                        last.then_inc(tile_done[t % NB], 1)
                steps(pe, body)


class Prepare:
    HF = 2 * FOXH
    LAT_SUMS = 1 + 3 * TT
    LATENTS = LAT_SUMS + 10
    ABS = LATENTS + 2
    FOX_SUMS = ABS + 2 * TT
    ONE_PLUS = FOX_SUMS + 1
    LOGF = ONE_PLUS + 5
    STARTS = LOGF + TT
    FOX_K, FOX_Q = STARTS + 2, STARTS + 4

    def __init__(self, nc, k, lay, s, proj):
        self.k, self.lay, self.proj = k, lay, proj
        T = lambda n, shape: s.enter_context(nc.sbuf_tensor(n, shape, F32))
        self.fs = T("fs", [P, TT, FOXH])
        self.g = T("fgate", [P, 6, TT, FOXH])
        self.cl = T("fcl", [P, TT, FOXH])
        self.fp = T("ffp", [P, QT, FOXH])
        self.pre = T("fpre", [P, 2, TT, FOXH])
        self.sq = T("fsq", [P, self.HF, HD])
        self.ssf, self.ssl = T("ssf", [P, TT, self.HF]), T("ssl", [P, 2, TT])
        sem = k.sems["fox"]
        self.cached, self.stored, self.act_steps, self.dve_steps = (sem[n] for n in ("cl", "st", "act", "dve"))
        self.fox = proj[:, :, O_FQ:O_FV].rearrange("p t (h d) -> p t h d", d=HD)
        self.cq, self.ckv, self.kr = (proj[:, :, a:b] for a, b in ((O_CQ, O_CKV), (O_CKV, O_KR), (O_KR, IN_W)))
        self.STORES = 14

    def load_store(self, sp, columns_ready):
        k, lay, proj, lf = self.k, self.lay, self.proj, self.g[:, 5]
        sp.dma_start(self.cl[:, 0:QT, :], k.cache_fox_logf[lay, 0].rearrange("(t p) h -> p t h", p=P))\
          .then_inc(self.cached, 16)

        def out(dst, src):
            sp.dma_start(dst, src).then_inc(self.stored, 16)

        def out_fox(dst, dst_s, src):
            out(dst[lay, 0].rearrange("(t p) h d -> p t (h d)", p=P), src[:, 0:QT])
            out(dst_s[lay, 0].rearrange("t h d -> t (h d)"), src[0:DEC, QT])
        for new, cache in ((k.swa_k_s, k.cache_swa_k), (k.swa_v_s, k.cache_swa_v)):
            out(new[lay, 0, 0:WIN - DEC], cache[lay, 0, DEC:WIN])
        sp.wait_ge(self.dve_steps, self.LATENTS)
        for dst, dst_s, src in ((k.mla_ckv_p, k.mla_ckv_s, self.ckv), (k.mla_krope_p, k.mla_krope_s, self.kr)):
            out(dst[lay, 0].rearrange("(t p) n -> p t n", p=P), src[:, 0:QT])
            out(dst_s[lay, 0], src[0:DEC, QT])
        columns_ready(sp, O_G)
        out_fox(k.fox_v_p, k.fox_v_s, proj[:, :, O_FV:O_G])
        sp.wait_ge(self.dve_steps, self.LOGF)
        out(k.fox_logf_p[lay, 0].rearrange("(t p) h -> p t h", p=P), lf[:, 0:QT])
        out(k.fox_logf_s[lay, 0], lf[0:DEC, QT])
        sp.wait_ge(self.dve_steps, self.FOX_K)
        out_fox(k.fox_k_p, k.fox_k_s, proj[:, :, O_FK:O_FV])
        columns_ready(sp, O_CQ)
        out(k.swa_v_s[lay, 0, WIN - DEC:WIN].rearrange("t h d -> t (h d)"), proj[0:DEC, QT, O_SV:O_CQ])
        out(k.swa_v_p[lay, 0].rearrange("t h d -> t (h d)"), proj[:, QT - 1, O_SV:O_CQ])

    def scalar_latents(self, act):
        own = Steps(act, self.act_steps)
        eps = self.k.const[:, C_EPS:C_EPS + 1]
        act.wait_ge(self.dve_steps, self.LAT_SUMS)
        own.after(act.activation(self.ssl[:, 0], self.ssl[:, 0], ACT.Ln, scale=1.0 / QLORA, bias=eps))
        own.after(act.activation(self.ssl[:, 1], self.ssl[:, 1], ACT.Ln, scale=1.0 / KVLORA, bias=eps))
        own.after(act.activation(self.ssl[:, :, :], self.ssl[:, :, :], ACT.Exp, scale=-0.5))

    def scalar_fox(self, act):
        x, ax, e, u, r, lf = (self.g[:, n] for n in range(6))
        own = Steps(act, self.act_steps, 3)
        act.wait_ge(self.dve_steps, self.FOX_SUMS)
        own.after(act.activation(e, ax, ACT.Exp, scale=-1.0))
        act.wait_ge(self.dve_steps, self.ONE_PLUS)
        own.after(act.activation(ax, u, ACT.Ln))
        own.after(act.activation(self.ssf[:, :, :], self.ssf[:, :, :], ACT.Ln, scale=1.0 / HD,
                                 bias=self.k.const[:, C_EPS:C_EPS + 1]))
        own.after(act.activation(self.ssf[:, :, :], self.ssf[:, :, :], ACT.Exp, scale=-0.5))

    def vector(self, dve, columns_ready):
        k, proj, cl, pre = self.k, self.proj, self.cl, self.pre
        x, ax, e, u, r, lf = (self.g[:, n] for n in range(6))
        own = Steps(dve, self.dve_steps)

        dve.memset(proj[32:64, QT, :], 0.0)
        own.after(dve.memset(proj[64:128, QT, :], 0.0))
        columns_ready(dve, IN_W)
        sq = self.sq[:, :, :].rearrange("p h d -> p (h d)")
        for t in range(TT):
            lat, w = proj[:, t, O_CQ:O_KR], O_KR - O_CQ
            own.after(dve.tensor_tensor(sq[:, 0:w], lat, lat, ALU.mult))
            own.after(dve.tensor_reduce(self.ssl[:, 0, t:t + 1], sq[:, 0:QLORA], AX, ALU.add))
            own.after(dve.tensor_reduce(self.ssl[:, 1, t:t + 1], sq[:, QLORA:w], AX, ALU.add))
        assert own.n == self.LAT_SUMS
        half = ROPE // 2
        cos = k.const[:, C_COS:C_SIN].rearrange("p (t n) -> p t n", n=half)
        sin = k.const[:, C_SIN:C_MNEW].rearrange("p (t n) -> p t n", n=half)
        x1, x2 = self.kr[:, :, 0:half], self.kr[:, :, half:]
        a, b, c, d = (sq[:, n * TT * half:(n + 1) * TT * half].rearrange("p (t n) -> p t n", n=half) for n in range(4))
        own.after(dve.tensor_tensor(a, x1, cos, ALU.mult))
        own.after(dve.tensor_tensor(b, x2, sin, ALU.mult))
        own.after(dve.tensor_tensor(c, x1, sin, ALU.mult))
        own.after(dve.tensor_tensor(d, x2, cos, ALU.mult))
        own.after(dve.tensor_tensor(x1, a, b, ALU.subtract))
        own.after(dve.tensor_tensor(x2, c, d, ALU.add))
        dve.wait_ge(self.act_steps, 3)
        for n, (v, w, row) in enumerate(((self.cq, QLORA, R_CQ), (self.ckv, KVLORA, R_CKV))):
            own.after(dve.tensor_tensor(v, v, bcast(self.ssl[:, n], [P, TT, w], 2), ALU.mult))
            own.after(dve.tensor_tensor(v, v, bcast(k.row[:, row:row + w], [P, TT, w], 1), ALU.mult))
        assert own.n == self.LATENTS
        columns_ready(dve, O_G + FOXH)
        own.after(dve.tensor_tensor(x, proj[:, :, O_G:O_G + FOXH], bcast(k.row[:, R_BF:R_BF + FOXH], [P, TT, FOXH], 1),
                                    ALU.add))
        own.after(dve.scalar_tensor_tensor(ax, x, -1.0, x, ALU.mult, ALU.max))
        assert own.n == self.ABS
        for t in range(TT):
            own.after(dve.tensor_tensor(self.sq[:, :, :], self.fox[:, t], self.fox[:, t], ALU.mult))
            own.after(dve.tensor_reduce(self.ssf[:, t], self.sq[:, :, :], AX, ALU.add))
        dve.wait_ge(self.act_steps, 4)
        own.after(dve.tensor_scalar(u, e, 1.0, None, ALU.add))
        assert own.n == self.ONE_PLUS
        own.after(dve.tensor_scalar(r, u, -1.0, None, ALU.add))
        own.after(dve.tensor_tensor(r, e, r, ALU.subtract))
        own.after(dve.tensor_scalar(x, x, 0.0, None, ALU.min))
        dve.wait_ge(self.act_steps, 5)
        own.after(dve.tensor_tensor(r, ax, r, ALU.add))
        own.after(dve.tensor_tensor(lf, x, r, ALU.subtract))
        assert own.n == self.LOGF
        dve.wait_ge(self.cached, 16)
        dve.memset(cl[32:64, QT, :], 0.0)
        dve.memset(cl[64:128, QT, :], 0.0)
        dve.tensor_copy(cl[0:DEC, QT, :], lf[0:DEC, QT, :])
        own.after(dve.memset(pre[:, :, 0, :], 0.0))
        for t in range(1, TT):
            if t < QT:
                dve.tensor_tensor(pre[:, 0, t], pre[:, 0, t - 1], lf[:, t - 1], ALU.add)
            own.after(dve.tensor_tensor(pre[:, 1, t], pre[:, 1, t - 1], cl[:, t - 1], ALU.add))
        assert own.n == self.STARTS
        dve.wait_ge(self.act_steps, 7)
        for at, row in ((FOXH, R_FK), (0, R_FQ)):
            v = self.fox[:, :, at:at + FOXH]
            own.after(dve.tensor_tensor(v, v, bcast(self.ssf[:, :, at:at + FOXH], [P, TT, FOXH, HD], 3), ALU.mult))
            own.after(dve.tensor_tensor(v, v, bcast(k.row[:, row:row + HD], [P, TT, FOXH, HD], 1, 1), ALU.mult))
        assert own.n == self.FOX_Q


class SwaHeads:

    def __init__(self, nc, k, lay, s, proj):
        NH = SWAH + SWAKV
        self.k, self.lay, self.proj = k, lay, proj
        self.sq = s.enter_context(nc.sbuf_tensor("ssq", [P, TT, NH, HD], F32))
        self.ss = s.enter_context(nc.sbuf_tensor("sss", [P, TT, NH], F32))
        self.heads = proj[:, :, O_SQ:O_SV].rearrange("p t (h d) -> p t h d", d=HD)
        sem = k.sems["swa"]
        self.pool_steps, self.summed, self.inverse_steps, self.stored = (sem[n] for n in ("p", "sum", "inv", "st"))

    def store(self, sp):
        k, lay = self.k, self.lay
        sp.wait_ge(self.pool_steps, 3)
        for dst, src in ((k.swa_k_s[lay, 0, WIN - DEC:WIN], self.proj[0:DEC, QT, O_SK:O_SV]),
                         (k.swa_k_p[lay, 0], self.proj[:, QT - 1, O_SK:O_SV])):
            sp.dma_start(dst.rearrange("t h d -> t (h d)"), src).then_inc(self.stored, 16)
        sp.wait_ge(self.stored, 32)

    def pool(self, pool):
        own = Steps(pool, self.pool_steps)
        own.after(pool.tensor_tensor(self.sq[:, :, :, :], self.heads, self.heads, ALU.mult))
        pool.wait_ge(self.inverse_steps, 2)
        for a, n, row in ((SWAH, SWAKV, R_SK), (0, SWAH, R_SQ)):
            v = self.heads[:, :, a:a + n]
            own.after(pool.tensor_tensor(v, v, bcast(self.ss[:, :, a:a + n], [P, TT, n, HD], 3), ALU.mult))
            own.after(pool.tensor_tensor(v, v, bcast(self.k.row[:, row:row + HD], [P, TT, n, HD], 1, 1), ALU.mult))

    def vector(self, dve):
        dve.wait_ge(self.pool_steps, 1)
        dve.tensor_reduce(self.ss[:, :, :], self.sq[:, :, :, :], AX, ALU.add).then_inc(self.summed, 1)

    def scalar(self, act):
        own = Steps(act, self.inverse_steps)
        act.wait_ge(self.summed, 1)
        own.after(act.activation(self.ss[:, :, :], self.ss[:, :, :], ACT.Ln, scale=1.0 / HD,
                                 bias=self.k.const[:, C_EPS:C_EPS + 1]))
        own.after(act.activation(self.ss[:, :, :], self.ss[:, :, :], ACT.Exp, scale=-0.5))


def fox_rows(nc, k, prep, frow):
    with ExitStack() as s:
        ps = s.enter_context(nc.psum_tensor("fps", [P, 2, 512], F32))
        psF = s.enter_context(nc.psum_tensor("fpsF", [P, QT, P], F32))
        sem = k.sems["fox"]
        f_done, copied, f_turned, row_hi = (sem[n] for n in ("f", "fc", "ft", "rh"))
        tri, ones = k.const[:, C_TRI:C_TRI + P], k.const[:, C_ONE:C_ONE + P]
        lf, cl, pre, fp, fs = prep.g[:, 5], prep.cl, prep.pre, prep.fp, prep.fs
        with nc.Block() as block:

            @block.sync
            def _(sp):
                sp.wait_ge(prep.stored, 16 * prep.STORES)

            @block.tensor
            def _(pe):
                pe.matmul(ps[:, 0, 0:QT * FOXH], tri, lf[:, 0:QT, :], start=True, stop=False)
                pe.matmul(ps[:, 0, 0:QT * FOXH], ones, pre[:, 0, 0:QT, :], start=False, stop=True)
                pe.matmul(ps[:, 1, 0:TT * FOXH], tri, cl[:, :, :], start=True, stop=False)
                pe.matmul(ps[:, 1, 0:TT * FOXH], ones, pre[:, 1], start=False, stop=True).then_inc(f_done, 1)
                pe.wait_ge(copied, 1)
                for t in range(QT):
                    last = pe.transpose(psF[0:FOXH, t, :], fp[:, t, :], k.const[:, C_ID:C_ID + P])
                last.then_inc(f_turned, 1)

            @block.scalar
            def _(act):
                act.wait_ge(f_turned, 1)
                act.activation(frow[0][:, :], psF[0:FOXH, :, :].rearrange("p t n -> p (t n)"), ACT.Copy,
                               scale=-1.0).then_inc(row_hi, 1)

            @block.vector
            def _(dve):
                dve.wait_ge(f_done, 1)
                dve.tensor_copy(fp[:, :, :], ps[:, 0, 0:QT * FOXH].rearrange("p (t h) -> p t h", h=FOXH))\
                   .then_inc(copied, 1)
                dve.tensor_copy(fs[:, :, :], ps[:, 1, 0:TT * FOXH].rearrange("p (t h) -> p t h", h=FOXH))
                dve.wait_ge(row_hi, 1)
                dve.scalar_tensor_tensor(frow[1][:, :], psF[0:FOXH, :, :].rearrange("p t n -> p (t n)"), -1.0,
                                         frow[0][:, :].bitcast(F32), ALU.mult, ALU.subtract)


def attend_prompt(nc, k, kind, heads, kdim, q_of, k_of, v_of, kv_of, yT, yc, frow=None, alibi=None):
    swa, fox = kind == "swa", kind == "fox"
    pairs = heads // 2
    R = pairs * QT
    AHEAD, RQ = 3, 4

    def first(i):
        return max(i - 1, 0) if swa else 0

    units = []
    for r in range(R):
        i = r % QT
        if i + 1 - first(i) <= 4:
            units.append((r, (0, 1), True))
        else:
            units += [(r, (0,), False), (r, (1,), True)]
    NU = len(units)
    sink = 1 if swa else 0
    with ExitStack() as s:
        T = lambda n, shape, dt=F32: s.enter_context(nc.sbuf_tensor(n + kind, shape, dt))
        qT = [T("qT" + n, [96, RQ, 2, P], F32R) for n in ("hi", "lo")]
        kT = [T("kT" + n, [96, 2, 2, SEQ], F32R) for n in ("hi", "lo")]
        NPR = 3
        pr = T("pr", [P, NPR, 2, 512])
        pT = T("pT", [P, 2, 2, 2 if swa else QT, P])
        st = T("st", [P, 3, NU, 2])
        nmax, tot, rtot = (st[:, n] for n in range(3))
        if swa:
            bias = T("bias", [P, SWAH, 2 * P])
        psS = s.enter_context(nc.psum_tensor("psS" + kind, [P, 2, 2, 512], F32))
        psX = s.enter_context(nc.psum_tensor("psX" + kind, [P, 2, 2, P], F32))
        psT = s.enter_context(nc.psum_tensor("psT" + kind, [P, 8, P], F32))
        psO = s.enter_context(nc.psum_tensor("psO" + kind, [P, 512], F32))
        sem = k.sems["att"]
        (cleared, loaded, row_in, x_done, x_hi, x_lo, scored, maxed, expd, normed, turned, t_low, t_high, mixed,
         y_done, dve_steps, inverted, pool_normed, dve_cleared) = (sem[n] for n in ("clr", "ld", "row", "x", "xh", "xl", "s", "m", "e", "n", "t", "tl",
                                                "th", "o", "y", "d", "iv", "pn", "dc"))
        ident = k.const[:, C_ID:C_ID + P]

        def width(r):
            i = r % QT
            return (i + 1 - first(i)) * P

        shared = [(j, width(r)) for j, (r, es, _) in enumerate(units) if len(es) == 2]

        def shared_to(j):
            return sum(1 for n, _ in shared if n <= j)

        def next_tile(m):
            if 1 <= m <= NU and units[m - 1][2] and units[m - 1][0] + AHEAD < R:
                return units[m - 1][0] + AHEAD

        def units_to(r):
            return sum(1 for u in units if u[0] <= r)

        with nc.Block() as block:

            @block.sync
            def _(sp):
                if swa:
                    sp.dma_start(bias[:, :, :], alibi).then_inc(loaded, 16)
                if fox:
                    for p in range(pairs):
                        if p == 1:
                            sp.wait_ge(cleared, 5)
                        if p >= 2:
                            sp.wait_ge(scored, units_to((p - 1) * QT - 1))
                        for n in range(2):
                            if p == 0:
                                sp.wait_ge((cleared, dve_cleared)[n], 1)
                            for e in range(2):
                                h = 2 * p + e
                                sp.dma_start(kT[n][64:65, p % 2, e, :].bitcast(F32), frow[n][h:h + 1, :].bitcast(F32))\
                                  .then_inc(row_in[p % 2], 16)

            @block.gpsimd
            def _(pool):
                if kdim < 96:
                    jobs = [(kT[0][64:96, 0], 0.0), (qT[0][64:96], 0.0)] + [(qT[0][64:65], 1.0)] * fox + \
                           [(kT[0][64:96, 1], 0.0), (kT[1][64:96, 1], 0.0)]
                    for n, (rows, value) in enumerate(jobs):
                        pool.memset(rows.bitcast(F32), value).then_inc(cleared, 1)
                        pool.wait_ge(cleared, n + 1)
                for n, (j, w) in enumerate(shared):
                    pool.wait_ge(inverted, n + 1)
                    if n:
                        pool.wait_ge(pool_normed, n)
                    v = pr[:, j % NPR, :, 0:w]
                    pool.tensor_tensor(v, v, bcast(rtot[:, j, :], [P, 2, w], 2), ALU.mult).then_inc(pool_normed, 1)

            @block.tensor
            def _(pe):
                def turn_tile(r):
                    p, i = divmod(r, QT)
                    if r:
                        pe.wait_ge(x_lo, r)
                    for e in range(2):
                        h = 2 * p + e
                        pe.transpose(psX[0:kdim, 0, e, :], q_of(h)[:, i, :], ident)
                        last = pe.transpose(psX[0:kdim, 1, e, :], k_of(kv_of(h))[:, i, :], ident)
                    last.then_inc(x_done, 1)

                for r in range(AHEAD):
                    turn_tile(r)
                for m in range(NU + 3):
                    if m < NU:
                        r, es, ends = units[m]
                        p, i = divmod(r, QT)
                        pe.wait_ge(x_lo, r + 1)
                        if kdim < 96 and m == 0:
                            pe.wait_ge(cleared, 2 + fox)
                            pe.wait_ge(dve_cleared, 2)
                        if kdim < 96 and r == QT:
                            pe.wait_ge(cleared, 4 + fox)
                        if fox:
                            pe.wait_ge(row_in[p % 2], 64 * (p // 2 + 1))
                        if m >= 2:
                            pe.wait_ge(expd, m - 1)
                        f, w = first(i) * P, width(r)
                        for e in es:
                            both = len(es) == 2
                            for a in range(0, w, 512):
                                n = min(512, w - a)
                                diag = not swa and a + n == w
                                bank = psS[:, m % 2, e if both else a // 512, :]
                                for j, (x, y) in enumerate(((0, 0), (0, 1), (1, 0))):
                                    last = pe.matmul(bank[:, 0:n], qT[x][:, r % RQ, e, :],
                                                     kT[y][:, p % 2, e, f + a:f + a + n],
                                                     start=(j == 0), stop=(j == 2 and not diag))
                                if diag:
                                    last = pe.matmul(bank[:, n - P:n], k.identr[:, :],
                                                     (k.mfoxr if fox else k.mmlar)[:, :], start=False, stop=True)
                        last.then_inc(scored, 1)
                    if next_tile(m):
                        turn_tile(next_tile(m))
                    j = m - 2
                    if 0 <= j < NU:
                        r, es, _ = units[j]
                        nb = width(r) // P
                        if len(es) == 2:
                            pe.wait_ge(pool_normed, shared_to(j))
                        else:
                            pe.wait_ge(normed, j + 1 - shared_to(j))
                        if j:
                            pe.wait_ge(t_low, j)
                            pe.wait_ge(t_high, j)
                        for n, e in enumerate(es):
                            flat = pr[:, j % NPR, n, :] if len(es) == 2 else \
                                pr[:, j % NPR].rearrange("p e n -> p (e n)")
                            for b in range(nb):
                                last = pe.transpose(psT[:, 4 * n + b, :], flat[:, b * P:(b + 1) * P], ident)
                        last.then_inc(turned, 1)
                    j = m - 3
                    if 0 <= j < NU and units[j][2]:
                        r = units[j][0]
                        p, i = divmod(r, QT)
                        pe.wait_ge(t_low, j + 1)
                        pe.wait_ge(t_high, j + 1)
                        if r:
                            pe.wait_ge(y_done, r)
                        nb = width(r) // P
                        for b in range(nb):
                            for e in range(2):
                                last = pe.matmul(psO[64 * e:64 * e + HD, 0:P],
                                                 v_of(kv_of(2 * p + e), first(i) + b), pT[:, r % 2, e, b, :],
                                                 start=(b == 0), stop=(b == nb - 1))
                        last.then_inc(mixed, 1)

            @block.scalar
            def _(act):
                def high_part(r):
                    p, i = divmod(r, QT)
                    act.wait_ge(x_done, r + 1)
                    act.activation(qT[0][0:kdim, r % RQ, :, :], psX[0:kdim, 0], ACT.Copy)
                    act.activation(kT[0][0:kdim, p % 2, :, i * P:(i + 1) * P], psX[0:kdim, 1], ACT.Copy)\
                       .then_inc(x_hi, 1)

                for r in range(AHEAD):
                    high_part(r)
                for m in range(NU + 3):
                    if next_tile(m):
                        high_part(next_tile(m))
                    j = m - 2
                    if 0 <= j < NU:
                        r, es, _ = units[j]
                        nb = min(4, width(r) // P)
                        act.wait_ge(turned, j + 1)
                        if r >= 2:
                            act.wait_ge(mixed, r - 1)
                        act.activation(pT[:, r % 2, es[0], 0:nb, :], psT[:, 0:nb, :], ACT.Copy).then_inc(t_low, 1)
                    if m < NU:
                        r, es, _ = units[m]
                        w = width(r) + sink
                        act.wait_ge(maxed, m + 1)
                        if m >= NPR:
                            act.wait_ge(turned, m - NPR + 1)
                        for n, e in enumerate(es):
                            src, dst = psS[:, m % 2], pr[:, m % NPR]
                            if len(es) == 2:
                                src, dst = src[:, n, :], dst[:, n, :]
                            else:
                                src, dst = (v.rearrange("p e n -> p (e n)") for v in (src, dst))
                            last = act.activation(dst[:, 0:w], src[:, 0:w], ACT.Exp, bias=nmax[:, m, n:n + 1],
                                                  accum_out=tot[:, m, n:n + 1])
                        last.then_inc(expd, 1)
                    j = m - 3
                    if 0 <= j < NU and units[j][2]:
                        r = units[j][0]
                        p, i = divmod(r, QT)
                        act.wait_ge(mixed, r + 1)
                        act.activation(yT[:, yc + p, i * P:(i + 1) * P], psO[:, 0:P], ACT.Copy).then_inc(y_done, 1)

            @block.vector
            def _(dve):
                own = Steps(dve, dve_steps)

                def low_part(r):
                    p, i = divmod(r, QT)
                    dve.wait_ge(x_hi, r + 1)
                    dve.tensor_tensor(qT[1][0:kdim, r % RQ, :, :], psX[0:kdim, 0],
                                      qT[0][0:kdim, r % RQ, :, :].bitcast(F32), ALU.subtract)
                    at = slice(i * P, (i + 1) * P)
                    dve.tensor_tensor(kT[1][0:kdim, p % 2, :, at], psX[0:kdim, 1],
                                      kT[0][0:kdim, p % 2, :, at].bitcast(F32), ALU.subtract).then_inc(x_lo, 1)

                if kdim < 96:
                    dve.memset(kT[1][64:96, 0].bitcast(F32), 0.0).then_inc(dve_cleared, 1)
                    dve.memset(qT[1][64:96].bitcast(F32), 0.0).then_inc(dve_cleared, 1)
                for r in range(AHEAD):
                    low_part(r)
                if swa:
                    dve.wait_ge(loaded, 16)
                for m in range(NU + 2):
                    if m < NU:
                        r, es, _ = units[m]
                        w, h = width(r), 2 * (r // QT)
                        ne = len(es)
                        dve.wait_ge(scored, m + 1)
                        if swa:
                            v = psS[:, m % 2, :, 0:w]
                            dve.tensor_tensor(v, v, bias[:, h:h + 2, 2 * P - w:2 * P], ALU.add)
                            own.after(dve.tensor_copy(psS[:, m % 2, :, w], k.row[:, R_SINK + h:R_SINK + h + 2]))
                        v = psS[:, m % 2, :, 0:w + sink] if ne == 2 else \
                            psS[:, m % 2].rearrange("p e n -> p (e n)")[:, 0:w]
                        dve.tensor_reduce(nmax[:, m, 0:ne], v, AX, ALU.max, negate=True).then_inc(maxed, 1)
                    j = m - 1
                    if 0 <= j < NU:
                        r, es, _ = units[j]
                        w = width(r)
                        dve.wait_ge(expd, j + 1)
                        inverse = dve.reciprocal(rtot[:, j, 0:len(es)], tot[:, j, 0:len(es)])
                        if len(es) == 2:
                            inverse.then_inc(inverted, 1)
                        else:
                            own.after(inverse)
                            v = pr[:, j % NPR].rearrange("p e n -> p (e n)")[:, 0:w]
                            dve.tensor_scalar(v, v, rtot[:, j, 0:1], None, ALU.mult).then_inc(normed, 1)
                    j = m - 2
                    if 0 <= j < NU:
                        r, es, _ = units[j]
                        nb = width(r) // P
                        dve.wait_ge(turned, j + 1)
                        if r >= 2:
                            dve.wait_ge(mixed, r - 1)
                        if len(es) == 2:
                            dve.tensor_copy(pT[:, r % 2, 1, 0:nb, :], psT[:, 4:4 + nb, :]).then_inc(t_high, 1)
                        else:
                            dve.tensor_copy(pT[:, r % 2, es[0], 4:nb, :], psT[:, 4:nb, :]).then_inc(t_high, 1)
                    if next_tile(m):
                        low_part(next_tile(m))
    restart(nc, k.lists["att"])


def attend_sample(nc, k, kind, heads, q_new, kunits, kdim, row_of, tiles, loads, yT, yc, fs=None, beside=None):
    mla, fox = kind == "mla", kind == "fox"
    keys = sum(t[0] for t in tiles)
    offs = [sum(t[0] for t in tiles[:n]) for n in range(len(tiles))]
    pw = keys if keys <= 512 else keys // 3
    NPC = keys // pw
    G = (heads + 3) // 4
    pairs = heads // 2
    qunits = heads if mla else pairs
    jobs = [(u, list(range(a, min(a + 4, len(tiles))))) for a in range(0, len(tiles), 4)
            for u in [*range(kunits)] + ["f"] * fox]
    pjobs = [(g, list(range(a, min(a + 4, len(tiles))))) for g in range(G) for a in range(0, len(tiles), 4)]
    J, PJ = len(jobs), len(pjobs) // G
    rows = [32 * min(4, heads - 4 * g) for g in range(G)]
    with ExitStack() as s:
        T = lambda n, shape: s.enter_context(nc.sbuf_tensor(n + "_s" + kind, shape, F32))
        kT = T("kT", [P, kunits, keys])
        qz = T("qz", [P, qunits, DEC if mla else 2 * DEC])
        pr = T("pr", [P, G, keys])
        pT = T("pT", [P, G, len(tiles), P])
        st = T("st", [P, 4, G])
        mx, tot, rtot, sk = (st[:, n] for n in range(4))
        sink = T("sink", [P, 2])
        if fox:
            rb, lb, fq = T("rb", [64, keys]), T("lb", [64, G * P]), T("fq", [64, DEC])
        psS = s.enter_context(nc.psum_tensor("psS_s" + kind, [P, NPC, 512], F32))
        psX = s.enter_context(nc.psum_tensor("psX_s" + kind, [P, 2, 4, P], F32))
        psQ = s.enter_context(nc.psum_tensor("psQ_s" + kind, [P, 4, P], F32))
        psO = s.enter_context(nc.psum_tensor("psO_s" + kind, [P, 2, 512], F32))
        sem = k.sems["smp"]
        (cache_in, zeroed, q_turned, q_done, x_done, x_out, k_ready, scored, dve_steps, maxed, expd, normed,
         t_done, t_out, mixed, y_done) = (sem[n] for n in ("in", "z", "qt", "qd", "x", "xo", "k", "s", "d", "m",
                                                           "e", "n", "t", "to", "o", "y"))
        ident = k.const[:, C_ID:C_ID + P]

        engines = (nc.scalar, nc.vector)

        def unload(eng, b):
            for j in range(b, J, 2):
                u, ts = jobs[j]
                c0, w = offs[ts[0]], sum(tiles[t][0] for t in ts)
                eng.wait_ge(x_done, j + 1)
                n = FOXH if u == "f" else (kdim if mla else P)
                full = [t for t in ts if tiles[t][0] == P]
                parts = ([(0, len(full))] if full else []) + [(ts.index(t), 0) for t in ts if tiles[t][0] < P]
                for m, (i, cnt) in enumerate(parts):
                    o = offs[ts[i]]
                    if cnt:
                        src = psX[0:n, b, i:i + cnt, :].rearrange("p t n -> p (t n)")
                        ww = cnt * P
                    else:
                        ww = tiles[ts[i]][0]
                        src = psX[0:n, b, i, 0:ww]
                    dst = rb[0:n, o:o + ww] if u == "f" else kT[0:n, u, o:o + ww]
                    sc = -1.0 if u == "f" else 1.0
                    if u == "f" and len(tiles) - 1 in ts and not cnt:
                        copy(eng, fq[32:32 + FOXH, :], src, 1.0)
                    last = copy(eng, dst, src, sc)
                last.then_inc(x_out[b], 1)

        def copy(eng, dst, src, scale):
            if eng is engines[0]:
                return eng.activation(dst, src, ACT.Copy, scale=scale)
            return eng.tensor_scalar(dst, src, scale, None, ALU.mult)

        def unload_p(eng, j):
            g, ts = pjobs[j]
            eng.wait_ge(t_done, j + 1)
            full = [t for t in ts if tiles[t][0] == P]
            if full:
                last = copy(eng, pT[:, g, full[0]:full[-1] + 1, 0:rows[g]],
                            psX[:, j % 2, 0:len(full), 0:rows[g]], 1.0)
            for t in ts:
                if tiles[t][0] < P:
                    r = tiles[t][0]
                    last = copy(eng, pT[0:r, g, t, 0:rows[g]],
                                psX[0:r, j % 2, ts.index(t), 0:rows[g]], 1.0)
            last.then_inc(t_out[j % 2], 1)

        with nc.Block() as block:

            @block.sync
            def _(sp):
                for n, (dst, src) in enumerate(loads):
                    sp.dma_start(dst, src).then_inc(cache_in[n], 16)
                if beside:
                    beside.store(sp)

            @block.gpsimd
            def _(pool):
                pool.memset(qz[:, :, :], 0.0).then_inc(zeroed, 1)
                if fox:
                    for n, (rows, value) in enumerate(((rb[0:32, :], 0.0), (rb[32:64, :], 1.0), (fq[32:64, :], 0.0))):
                        pool.wait_ge(zeroed, n + 1)
                        pool.memset(rows, value).then_inc(zeroed, 1)
                if beside:
                    pool.wait_ge(zeroed, 4)
                    beside.pool(pool)

            @block.tensor
            def _(pe):
                for u in range(qunits):
                    n = kdim if mla else P
                    last = pe.transpose(psQ[0:n, u, 0:DEC], q_new(u), ident[0:DEC, 0:DEC])
                last.then_inc(q_turned, 1)
                for j, (u, ts) in enumerate(jobs):
                    for n in range(2):
                        if len(loads) > n + 1 and u == 0 and ts[0] == 4 * n:
                            pe.wait_ge(cache_in[n], 16)
                    if j >= 2:
                        pe.wait_ge(x_out[j % 2], j // 2)
                    for n, t in enumerate(ts):
                        r = tiles[t][0]
                        src = fs[0:r, t, :] if u == "f" else tiles[t][1](u)
                        c = FOXH if u == "f" else (kdim if mla else P)
                        last = pe.transpose(psX[0:c, j % 2, n, 0:r], src, ident[0:r, 0:r])
                    last.then_inc(x_done, 1)
                pe.wait_ge(x_out[0], (J + 1) // 2)
                pe.wait_ge(x_out[1], J // 2)
                pe.wait_ge(q_done, 1)
                for g in range(G):
                    if g:
                        pe.wait_ge(expd, g)
                    for a in range(NPC):
                        at = slice(a * pw, (a + 1) * pw)
                        if fox:
                            pe.matmul(psS[0:rows[g], a, 0:pw], lb[:, g * P:g * P + rows[g]], rb[:, at],
                                      start=True, stop=False, skip_group_check=True)
                        if mla:
                            for h in range(4):
                                last = pe.matmul(psS[32 * h:32 * h + DEC, a, 0:pw], qz[0:kdim, h, :],
                                                 kT[0:kdim, h, at], start=True, stop=True)
                        else:
                            for p in range(2 * g, min(2 * g + 2, pairs)):
                                e = 64 * (p % 2)
                                last = pe.matmul(psS[e:e + 64, a, 0:pw], qz[:, p, :], kT[:, p if fox else 0, at],
                                                 start=not fox, stop=True, skip_group_check=True)
                    last.then_inc(scored, 1)
                for j, (g, ts) in enumerate(pjobs):
                    pe.wait_ge(normed, g + 1)
                    if j >= 2:
                        pe.wait_ge(t_out[j % 2], j // 2)
                    for n, t in enumerate(ts):
                        r = tiles[t][0]
                        last = pe.transpose(psX[0:r, j % 2, n, 0:rows[g]], pr[0:rows[g], g, offs[t]:offs[t] + r],
                                            ident[0:rows[g], 0:rows[g]])
                    last.then_inc(t_done, 1)
                pe.wait_ge(t_out[0], (len(pjobs) + 1) // 2)
                pe.wait_ge(t_out[1], len(pjobs) // 2)
                if loads:
                    pe.wait_ge(cache_in[len(loads) - 1], 16)
                for p in range(pairs):
                    g, e = p // 2, 64 * (p % 2)
                    if p >= 2:
                        pe.wait_ge(y_done, 2 * (p - 1))
                    for t, (r, _, v) in enumerate(tiles):
                        last = pe.matmul(psO[:, p % 2, 0:2 * DEC], v(p), pT[0:r, g, t, e:e + 64],
                                         start=(t == 0), stop=(t == len(tiles) - 1))
                    last.then_inc(mixed, 1)

            @block.scalar
            def _(act):
                if fox:
                    act.wait_ge(zeroed, 4)
                unload(engines[0], 0)
                if beside:
                    beside.scalar(act)
                for g in range(G):
                    act.wait_ge(maxed, g + 1)
                    last = act.activation(pr[0:rows[g], g, :].rearrange("p (a n) -> p a n", a=NPC),
                                          psS[0:rows[g], :, 0:pw], ACT.Exp, bias=mx[0:rows[g], g:g + 1],
                                          accum_out=tot[0:rows[g], g:g + 1])
                    if kind == "swa":
                        last = act.activation(sk[0:rows[g], g:g + 1], mx[0:rows[g], g:g + 1], ACT.Exp,
                                              bias=sink[0:rows[g], g:g + 1])
                    last.then_inc(expd, 1)
                for j in range(0, len(pjobs), 2):
                    unload_p(engines[0], j)

            @block.vector
            def _(dve):
                own = Steps(dve, dve_steps)
                dve.wait_ge(q_turned, 1)
                dve.wait_ge(zeroed, 1)
                if mla:
                    last = dve.tensor_copy(qz[0:kdim, :, :], psQ[0:kdim, 0:4, 0:DEC])
                else:
                    for h in range(heads):
                        e, r = 64 * (h % 2), row_of(h)
                        last = dve.tensor_copy(qz[r:r + HD, h // 2, DEC * (h % 2):DEC * (h % 2 + 1)],
                                               psQ[e:e + HD, h // 2, 0:DEC])
                if not fox:
                    last.then_inc(q_done, 1)
                if kind == "swa":
                    for g in range(G):
                        for h in range(4 * g, min(4 * g + 4, heads)):
                            e = 32 * (h % 4)
                            last = dve.tensor_copy(sink[e:e + 32, g:g + 1], k.row[e:e + 32, R_SINK + h:R_SINK + h + 1])
                    own.after(last)
                if fox:
                    dve.wait_ge(zeroed, 4)
                unload(engines[1], 1)
                if fox:
                    dve.wait_ge(x_out[0], (J + 1) // 2)
                    dve.wait_ge(x_out[1], J // 2)
                    dve.tensor_copy(lb[0:32, :], k.const[0:32, C_SEL:C_SEL + G * P])
                    dve.tensor_tensor(lb[32:64, :].rearrange("p (a n) -> p a n", n=DEC),
                                      k.const[32:64, C_SEL:C_SEL + G * P].rearrange("p (a n) -> p a n", n=DEC),
                                      bcast(fq[32:64, :], [32, G * 4, DEC], 1), ALU.mult).then_inc(q_done, 1)
                if beside:
                    beside.vector(dve)
                for g in range(G):
                    R = rows[g]
                    dve.wait_ge(scored, g + 1)
                    if fox:
                        new = psS[0:R, NPC - 1, pw - DEC:pw]
                        own.after(dve.tensor_tensor(new, new, k.const[0:R, C_MNEW:C_MNEW + DEC], ALU.add))
                    if kind == "swa":
                        b = k.const[0:R, C_BSW + g * SKEYS:C_BSW + (g + 1) * SKEYS]
                        own.after(dve.tensor_tensor(psS[0:R, 0, 0:pw], psS[0:R, 0, 0:pw], b, ALU.add))
                    own.after(dve.reduce_max(mx[0:R, g:g + 1], psS[0:R, :, 0:pw], mybir.AxisListType.XY))
                    if kind == "swa":
                        own.after(dve.tensor_tensor(mx[0:R, g:g + 1], mx[0:R, g:g + 1], sink[0:R, g:g + 1], ALU.max))
                    dve.tensor_scalar(mx[0:R, g:g + 1], mx[0:R, g:g + 1], -1.0, None, ALU.mult).then_inc(maxed, 1)
                for g in range(G):
                    R = rows[g]
                    dve.wait_ge(expd, g + 1)
                    if kind == "swa":
                        own.after(dve.tensor_tensor(tot[0:R, g:g + 1], tot[0:R, g:g + 1], sk[0:R, g:g + 1], ALU.add))
                    own.after(dve.reciprocal(rtot[0:R, g:g + 1], tot[0:R, g:g + 1]))
                    dve.tensor_scalar(pr[0:R, g, :], pr[0:R, g, :], rtot[0:R, g:g + 1], None, ALU.mult)\
                       .then_inc(normed, 1)
                for j in range(1, len(pjobs), 2):
                    unload_p(engines[1], j)
                for p in range(pairs):
                    dve.wait_ge(mixed, p + 1)
                    for h in (2 * p, 2 * p + 1):
                        e, r, c = 64 * (h % 2), row_of(h), DEC * (h % 2)
                        dve.tensor_copy(yT[e:e + HD, yc + p, SEQ:TOK], psO[r:r + HD, p % 2, c:c + DEC])\
                           .then_inc(y_done, 1)
    restart(nc, k.lists["smp"])


def mla_prepare(nc, k, lay, proj, qm, km, vm):
    KT = 2 * QT + 1
    ORDER = [*range(QT), 2 * QT, *range(QT, 2 * QT)]
    half = ROPE // 2
    NS = 4
    with ExitStack() as s:
        T = lambda n, shape: s.enter_context(nc.sbuf_tensor("m" + n, shape, F32))
        ckc, krc = T("ckc", [P, QT, KVLORA]), T("krc", [P, QT, ROPE])
        wuq, wukv = T("wuq", [P, 2, MLAH * MQK]), T("wukv", [P, 512])
        cT = T("cT", [P, 2, 3, P])
        rot = T("rot", [P, 2, TT, MLAH, half])
        sqk, sqq = T("sqk", [P, NS, MLAH, MQK]), T("sqq", [P, MLAH, MQK])
        hs = T("hs", [P, KT + TT, MLAH])
        psX = s.enter_context(nc.psum_tensor("mpsX", [P, 2, 512], F32))
        psQ = s.enter_context(nc.psum_tensor("mpsQ", [P, 2, 512], F32))
        psK = s.enter_context(nc.psum_tensor("mpsK", [P, 2, 512], F32))
        sem = k.sems["mla"]
        (w_in, c_in, d, turned, x_out, q_done, k_done, q_out, k_out, k_squared, k_summed,
         q_summed, zeroed, inverse_steps) = (sem[n] for n in (
             "w", "c", "dve", "t", "xo", "q", "k", "qo", "ko", "ksq", "ksum", "qsum", "z", "inv"))
        ident = k.const[:, C_ID:C_ID + P]
        cos = k.const[:, C_COS:C_SIN].rearrange("p (t n) -> p t n", n=half)
        sin = k.const[:, C_SIN:C_MNEW].rearrange("p (t n) -> p t n", n=half)
        cq, ckv, kr = (proj[:, :, a:b] for a, b in ((O_CQ, O_CKV), (O_CKV, O_KR), (O_KR, IN_W)))

        def latents(j):
            if j < QT:
                return P, j
            return (P, None) if j < 2 * QT else (DEC, QT)

        with nc.Block() as block:

            @block.sync
            def _(sp):
                sp.dma_start(wuq[:, :, :], k.w_mla_uq[lay].rearrange("(c p) n -> p c n", p=P)).then_inc(w_in, 16)
                sp.dma_start(wukv[:, :], k.w_mla_ukv[lay]).then_inc(w_in, 16)
                sp.dma_start(ckc[:, :, :], k.cache_mla_ckv[lay, 0].rearrange("(t p) n -> p t n", p=P)).then_inc(c_in, 16)
                sp.dma_start(krc[:, :, :], k.cache_mla_krope[lay, 0].rearrange("(t p) n -> p t n", p=P)).then_inc(c_in, 16)

            @block.gpsimd
            def _(pool):
                for n, rows in enumerate((km[32:64, 2 * QT], km[64:128, 2 * QT], qm[32:64, QT], qm[64:128, QT])):
                    if n:
                        pool.wait_ge(zeroed, n)
                    pool.memset(rows, 0.0).then_inc(zeroed, 1)
                pool.wait_ge(inverse_steps, 4)
                x = km[:, QT:2 * QT]
                pool.tensor_tensor(x, x, bcast(hs[:, 2 * TT:], [P, QT, MLAH, MQK], 3), ALU.mult)

            @block.scalar
            def _(act):
                eps = k.const[:, C_EPS:C_EPS + 1]
                inverse = Steps(act, inverse_steps)

                def inverse_root(x):
                    inverse.after(act.activation(x, x, ACT.Ln, scale=1.0 / MQK, bias=eps))
                    inverse.after(act.activation(x, x, ACT.Exp, scale=-0.5))

                def copy_turned(m):
                    n, t = latents(ORDER[m])
                    act.wait_ge(turned, m + 1)
                    if m >= 2:
                        act.wait_ge(k_done, m - 1)
                    c0 = 0 if t is not None else 2
                    act.activation(cT[:, m % 2, c0:3, 0:n],
                                   psX[:, m % 2, 0:3 * P].rearrange("p (c n) -> p c n", n=P)[:, c0:3, 0:n],
                                   ACT.Copy).then_inc(x_out, 1)

                copy_turned(0)
                for m, j in enumerate(ORDER):
                    n, t = latents(j)
                    if m + 1 < KT:
                        copy_turned(m + 1)
                    act.wait_ge(k_done, m + 1)
                    kv = psK[0:n, m % 2, :].rearrange("p (h e) -> p h e", e=NOPE + HD)
                    act.activation(km[0:n, j, :, 0:NOPE], kv[:, :, 0:NOPE], ACT.Copy)
                    act.activation(vm[0:n, j, :, :], kv[:, :, NOPE:], ACT.Copy).then_inc(k_out, 1)
                    if m == 0:
                        act.wait_ge(d, 3)
                        act.wait_ge(zeroed, 4)
                    if m >= NS:
                        act.wait_ge(k_summed, m - NS + 1)
                    act.wait_ge(k_out, m + 1)
                    act.activation(sqk[:, m % NS], km[:, j], ACT.Square).then_inc(k_squared, 1)
                    if m == TT + 3:
                        act.wait_ge(k_summed, TT)
                        inverse_root(hs[:, 0:TT])
                act.wait_ge(k_summed, KT)
                act.wait_ge(q_summed, 1)
                inverse_root(hs[:, TT:])

            @block.vector
            def _(dve):
                own = Steps(dve, d)
                own.after(dve.tensor_copy(km[:, 0:QT, :, NOPE:], bcast(kr[:, 0:QT], [P, QT, MLAH, ROPE], 2)))
                own.after(dve.tensor_copy(km[0:DEC, 2 * QT, :, NOPE:], bcast(kr[0:DEC, QT], [DEC, MLAH, ROPE], 1)))
                dve.wait_ge(c_in, 32)
                own.after(dve.tensor_copy(km[:, QT:2 * QT, :, NOPE:], bcast(krc[:, :, :], [P, QT, MLAH, ROPE], 2)))

                def sum_keys(m):
                    dve.wait_ge(k_squared, m + 1)
                    dve.tensor_reduce(hs[:, m if m < TT else TT + m], sqk[:, m % NS], AX, ALU.add)\
                       .then_inc(k_summed, 1)

                for t in range(TT):
                    n = P if t < QT else DEC
                    dve.wait_ge(q_done, t + 1)
                    dve.tensor_copy(qm[0:n, t].rearrange("p h e -> p (h e)"), psQ[0:n, t % 2, 0:MLAH * MQK])\
                       .then_inc(q_out, 1)
                    if t:
                        sum_keys(t - 1)
                sum_keys(TT - 1)
                dve.wait_ge(q_out, TT)
                dve.wait_ge(zeroed, 4)
                x1, x2 = qm[:, :, :, NOPE:NOPE + half], qm[:, :, :, NOPE + half:]
                cb, sb = (bcast(a, [P, TT, MLAH, half], 2) for a in (cos, sin))
                dve.tensor_tensor(rot[:, 0], x1, cb, ALU.mult)
                own.after(dve.tensor_tensor(rot[:, 1], x2, sb, ALU.mult))
                own.after(dve.tensor_tensor(rot[:, 0], rot[:, 0], rot[:, 1], ALU.subtract))
                own.after(dve.tensor_tensor(rot[:, 1], x1, sb, ALU.mult))
                own.after(dve.tensor_copy(x1, rot[:, 0]))
                own.after(dve.tensor_tensor(rot[:, 0], x2, cb, ALU.mult))
                own.after(dve.tensor_tensor(x2, rot[:, 0], rot[:, 1], ALU.add))
                for t in range(TT):
                    own.after(dve.tensor_tensor(sqq[:, :, :], qm[:, t], qm[:, t], ALU.mult))
                    last = dve.tensor_reduce(hs[:, TT + t], sqq[:, :, :], AX, ALU.add)
                    if t < TT - 1:
                        own.after(last)
                    else:
                        last.then_inc(q_summed, 1)
                    if TT + t < KT:
                        sum_keys(TT + t)
                dve.wait_ge(inverse_steps, 2)
                for x, a, b in ((km[:, 0:QT], 0, QT), (km[:, 2 * QT:KT], QT, TT)):
                    dve.tensor_tensor(x, x, bcast(hs[:, a:b], [P, b - a, MLAH, MQK], 3), ALU.mult)
                dve.wait_ge(inverse_steps, 4)
                x = qm[:, :, :, :]
                own.after(dve.tensor_tensor(x, x, bcast(hs[:, TT:2 * TT], [P, TT, MLAH, MQK], 3), ALU.mult))
                dve.tensor_tensor(x, x, bcast(k.row[:, R_MQ:R_MQ + MQK], [P, TT, MLAH, MQK], 1, 1), ALU.mult)

            @block.tensor
            def _(pe):
                def turn(m):
                    n, t = latents(ORDER[m])
                    if m >= 2:
                        pe.wait_ge(x_out, m - 1)
                    for c in range(3):
                        if t is None and c < 2:
                            continue
                        src = (ckc[:, ORDER[m] - QT, :] if t is None else
                               (cq[0:n, t, c * P:(c + 1) * P] if c < 2 else ckv[0:n, t, :]))
                        last = pe.transpose(psX[:, m % 2, c * P:c * P + n], src, ident[0:n, 0:n])
                    last.then_inc(turned, 1)

                pe.wait_ge(w_in, 32)
                turn(0)
                for m, j in enumerate(ORDER):
                    if m + 1 == TT:
                        pe.wait_ge(c_in, 32)
                    if m + 1 < KT:
                        turn(m + 1)
                    n, t = latents(j)
                    pe.wait_ge(x_out, m + 1)
                    if t is not None:
                        if m >= 2:
                            pe.wait_ge(q_out, m - 1)
                        for c in range(2):
                            last = pe.matmul(psQ[0:n, m % 2, 0:MLAH * MQK], cT[:, m % 2, c, 0:n], wuq[:, c, :],
                                             start=(c == 0), stop=(c == 1))
                        last.then_inc(q_done, 1)
                    if m >= 2:
                        pe.wait_ge(k_out, m - 1)
                    pe.matmul(psK[0:n, m % 2, :], cT[:, m % 2, 2, 0:n], wukv[:, :], start=True, stop=True)\
                      .then_inc(k_done, 1)


def w_out_block(k, lay, step):
    return k.w_out[lay].rearrange("(c p) n -> p c n", p=P)[:, :, bass.ds(step * P, P)]


def project_out(nc, k, lay, hi, lo, xT, raw):
    with ExitStack() as s:
        whi = s.enter_context(nc.sbuf_tensor("ohi", [P, 2, DC, P], F32R))
        wlo = s.enter_context(nc.sbuf_tensor("olo", [P, 2, DC, P], F32R))
        ps = s.enter_context(nc.psum_tensor("ops", [P, 2, NT, 512], F32))
        sem = k.sems["wout"]
        raw_in, hi_done, lo_done, x_in, tile_done, added = (sem[n] for n in ("raw", "hi", "lo", "x", "done", "add"))

        def steps(eng, body):
            for b in range(2):
                body(0, b)
            with eng.Fori(1, DC // 2) as i:
                for b in range(2):
                    body(i, b)

        with nc.Block() as block:

            @block.sync
            def _(sp):
                def body(i, b):
                    if is_first(i):
                        return
                    sp.wait_ge(lo_done[b], i)
                    sp.dma_start(raw[:, b], w_out_block(k, lay, 2 * i + b)).then_inc(raw_in[b], 16)
                steps(sp, body)

            @block.scalar
            def _(act):
                def body(i, b):
                    act.wait_ge(raw_in[b], 16 * i + 16)
                    if not is_first(i):
                        act.wait_ge(tile_done[b], i * NT)
                    act.activation(whi[:, b], raw[:, b], ACT.Copy).then_inc(hi_done[b], 1)
                steps(act, body)

            @block.gpsimd
            def _(pool):
                def body(i, b):
                    pool.wait_ge(hi_done[b], i + 1)
                    if not (is_first(i) and b == 0):
                        pool.wait_ge(lo_done[1 - b], i + b)
                    pool.tensor_tensor(wlo[:, b], raw[:, b], whi[:, b].bitcast(F32), ALU.subtract)\
                        .then_inc(lo_done[b], 1)
                steps(pool, body)

            @block.tensor
            def _(pe):
                def body(i, b):
                    pe.wait_ge(lo_done[b], i + 1)
                    for t in range(NT):
                        if not is_first(i):
                            pe.wait_ge(added[b], (i - 1) * NT + (t + 1))
                        at = slice(t * TN, (t + 1) * TN)
                        for c in range(DC):
                            for m, (w, a) in enumerate(((whi, hi), (wlo, hi), (whi, lo))):
                                last = pe.matmul(ps[:, b, t, 0:TN], w[:, b, c, :], a[:, c, at],
                                                 start=(c == 0 and m == 0), stop=(c == DC - 1 and m == 2))
                        last.then_inc(tile_done[b], 1)
                steps(pe, body)

            @block.vector
            def _(dve):
                dve.wait_ge(x_in, 16)

                def body(i, b):
                    for t in range(NT):
                        dve.wait_ge(tile_done[b], i * NT + (t + 1))
                        x = xT[:, bass.ds(2 * i + b, 1), t * TN:(t + 1) * TN]
                        dve.tensor_tensor(x, x, ps[:, b, t:t + 1, 0:TN], ALU.add).then_inc(added[b], 1)
                steps(dve, body)


def up_block(k, lay, col):
    return k.w_ffn_up[lay].rearrange("(c p) n -> p c n", p=P)[:, :, bass.ds(col, P)]


def conv_ffn(nc, k, lay, hi, lo, xT, raw):
    PAIRS = FC // 2
    EXT = CW - 1
    RW = TOK + 2 * EXT
    CL = RW - EXT
    SB = SEQ + EXT
    A0, B0, D0, D1, A1, B1 = range(6)
    with ExitStack() as s:
        T = lambda n, shape, dt=F32: s.enter_context(nc.sbuf_tensor("f" + n, shape, dt))
        whi, wlo = T("whi", [P, 6, DC, P], F32R), T("wlo", [P, 6, DC, P], F32R)
        ax = T("ax", [P, 2, RW])
        cb = T("cb", [P, 2, CL])
        uhi, ulo = T("uhi", [P, 2, TOK], F32R), T("ulo", [P, 2, TOK], F32R)
        tail = T("tail", [P, 2 * EXT, FC])
        tl = T("tl", [2 * EXT * FC, P])
        psA = s.enter_context(nc.psum_tensor("fpsA", [P, NT, 512], F32))
        psB = s.enter_context(nc.psum_tensor("fpsB", [P, NT, 512], F32))
        psD = s.enter_context(nc.psum_tensor("fpsD", [P, 2, 512], F32))
        sem = k.sems["ffn"]
        (cleared, raw_in, hi_done, split, a_done, a_out, row_done, conv_steps, conv_done, gelu_done,
         b_done, b_out, u_hi, u_lo, p_done, p_out, t_done, t_out, stored) = (sem[n] for n in (
             "clr", "raw", "hi", "split", "a", "ao", "row", "cs", "conv", "gelu", "b", "bo", "uh", "ul",
             "p", "po", "t", "to", "st"))
        down = k.w_ffn_down[lay].rearrange("(j p) (m n) -> j p m n", p=P, n=P)
        vcw = k.vec[:, V_CW:V_CB].rearrange("p (w c) -> p w c", c=FC)
        vst = k.vec[:, V_ST:V_N].rearrange("p (t c) -> p t c", c=FC)

        def before(g):
            return 6 * g - 2

        def each_round(eng, body):
            body(0, (A0, B0, A1, B1), 0)
            with eng.Fori(1, PAIRS) as g:
                body(g, (A0, B0, D0, D1, A1, B1), before(g))
            body(PAIRS, (D0, D1), before(PAIRS))

        with nc.Block() as block:

            @block.sync
            def _(sp):
                def body(g, roles, n0):
                    for o, r in enumerate(roles):
                        if is_first(g) and o < 2:
                            continue
                        if r in (D0, D1):
                            src = down[bass.ds(2 * (g - 1) + (r - D0), 1)].rearrange("j p m n -> p (j m) n")
                        else:
                            col = (2 * g + (r >= A1)) * P + (DFF if r in (B0, B1) else 0)
                            src = up_block(k, lay, col)
                        sp.wait_ge(split, n0 + (o - 1))
                        sp.dma_start(raw[:, o % 2], src).then_inc(raw_in[o % 2], 16)
                each_round(sp, body)
                sp.wait_ge(t_out, 1)
                row = lambda d: d[lay, 0].rearrange("t (c p) -> (t c) p", p=P)
                sp.dma_start(row(k.ffn_conv_p), tl[0:EXT * FC, :]).then_inc(stored, 16)
                sp.dma_start(row(k.ffn_conv_s), tl[EXT * FC:2 * EXT * FC, :]).then_inc(stored, 16)
                sp.wait_ge(stored, 32)

            @block.gpsimd
            def _(pool):
                for b in range(2):
                    pool.memset(ax[:, b, 0:EXT], 0.0).then_inc(cleared, 1)
                    pool.wait_ge(cleared, b + 1)

                def body(g, roles, n0):
                    for o, r in enumerate(roles):
                        if not (isinstance(g, int) and n0 + o == 0):
                            pool.wait_ge(split, n0 + o)
                        pool.wait_ge(hi_done, n0 + (o + 1))
                        pool.tensor_tensor(wlo[:, r], raw[:, o % 2], whi[:, r].bitcast(F32), ALU.subtract)\
                            .then_inc(split, 1)
                each_round(pool, body)

            @block.tensor
            def _(pe):
                three = lambda a, b: ((a[0], b[0]), (a[1], b[0]), (a[0], b[1]))

                def up_chunk(g, e, n):
                    first = isinstance(g, int) and g == 0 and e == 0
                    for ps, role, done, out in ((psA, (A0, A1)[e], a_done, a_out), (psB, (B0, B1)[e], b_done, b_out)):
                        pe.wait_ge(split, n + 1 if ps is psA else n + 2)
                        for t in range(NT):
                            if not first:
                                pe.wait_ge(out, 6 * g + (3 * e + t - 2))
                            at = slice(t * TN, (t + 1) * TN)
                            for c in range(DC):
                                for m, (w, x) in enumerate(three((whi, wlo), (hi, lo))):
                                    last = pe.matmul(ps[:, t, 0:TN], w[:, role, c, :], x[:, c, at],
                                                     start=(c == 0 and m == 0), stop=(c == DC - 1 and m == 2))
                            last.then_inc(done, 1)

                def down_pair(g, n):
                    pe.wait_ge(split, n + 2)
                    pe.wait_ge(u_lo, 2 * g)
                    for m in range(DC):
                        for t in range(NT):
                            o = m * NT + t
                            pe.wait_ge(p_out[o % 2], 12 * (g - 1) + (o // 2 + 1))
                            at = slice(t * TN, (t + 1) * TN)
                            for e in range(2):
                                for i, (w, x) in enumerate(three((whi, wlo), (uhi, ulo))):
                                    last = pe.matmul(psD[:, o % 2, 0:TN], w[:, D0 + e, m, :], x[:, e, at],
                                                     start=(e == 0 and i == 0), stop=(e == 1 and i == 2))
                            last.then_inc(p_done[o % 2], 1)

                def body(g, roles, n0):
                    o = 0
                    if A0 in roles:
                        up_chunk(g, 0, n0)
                        o += 2
                    if D0 in roles:
                        down_pair(g, n0 + o)
                        o += 2
                    if A1 in roles:
                        up_chunk(g, 1, n0 + o)
                each_round(pe, body)
                pe.wait_ge(row_done, FC)
                pe.transpose(psA[0:2 * EXT * FC, 0, 0:P], tail[:, :, :].rearrange("p t c -> p (t c)"),
                             k.const[:, C_ID:C_ID + P]).then_inc(t_done, 1)

            @block.scalar
            def _(act):
                act.wait_ge(cleared, 2)
                rest = SEQ - 2 * TN

                def high_weights(g, roles, o):
                    peeled = isinstance(g, int)
                    for r in roles:
                        at = (6 * g - 2 if peeled and g else 0 if peeled else before(g)) + o
                        half_at = o // 2 if peeled and g == 0 else 3 * g + (o // 2 - 1)
                        act.wait_ge(raw_in[o % 2], 16 * half_at + 16)
                        if not (peeled and g == 0):
                            if r in (A0, B0):
                                act.wait_ge(b_done, 6 * g - 3)
                            elif r in (A1, B1):
                                act.wait_ge(b_done, 6 * g)
                            else:
                                act.wait_ge(p_out[1], 12 * g - 11)
                        act.activation(whi[:, r], raw[:, o % 2], ACT.Copy).then_inc(hi_done, 1)
                        o += 1

                def rows_of(g, e):
                    ch = 2 * g + e
                    if not (isinstance(g, int) and g == 0):
                        act.wait_ge(conv_done, 2 * g + (e - 1))
                    act.activation(ax[:, e, SB:SB + EXT], vst[:, :, bass.ds(ch, 1)].rearrange("p t c -> p (t c)"), ACT.Copy)
                    for t in range(NT):
                        act.wait_ge(a_done, 6 * g + (3 * e + t + 1))
                        if t < NT - 1:
                            act.activation(ax[:, e, EXT + t * TN:EXT + (t + 1) * TN], psA[:, t, 0:TN], ACT.Copy)\
                               .then_inc(a_out, 1)
                        else:
                            act.activation(ax[:, e, EXT + t * TN:EXT + SEQ], psA[:, t, 0:rest], ACT.Copy)
                            act.activation(ax[:, e, SB + EXT:RW], psA[:, t, rest:TN], ACT.Copy).then_inc(a_out, 1)
                    act.wait_ge(a_out, 6 * g + (3 * e + NT))
                    tl_v = lambda a: tail[:, a:a + EXT, bass.ds(ch, 1)].rearrange("p t c -> p (t c)")
                    act.activation(tl_v(0), ax[:, e, SEQ:SEQ + EXT], ACT.Copy)
                    act.activation(tl_v(EXT), ax[:, e, RW - EXT:RW], ACT.Copy).then_inc(row_done, 1)
                    act.wait_ge(conv_done, 2 * g + (e + 1))
                    act.activation(cb[:, e, :], cb[:, e, :], ACT.Gelu_apprx_tanh).then_inc(gelu_done, 1)

                def high_of(g, e):
                    act.wait_ge(b_out, 6 * g + (3 * e + NT))
                    if not (isinstance(g, int) and g == 0):
                        act.wait_ge(p_done[1], 12 * g)
                    act.activation(uhi[:, e, 0:SEQ], cb[:, e, 0:SEQ], ACT.Copy)
                    act.activation(uhi[:, e, SEQ:TOK], cb[:, e, SB:CL], ACT.Copy).then_inc(u_hi, 1)

                def body(g, last=False):
                    zero = isinstance(g, int) and g == 0
                    if not zero:
                        high_weights(g, (D0, D1), 2)
                    rows_of(g, 0)
                    high_weights(g, (A1, B1), 2 if zero else 4)
                    high_of(g, 0)
                    if not last:
                        high_weights(g + 1, (A0, B0), 0)
                    rows_of(g, 1)
                    if last:
                        high_weights(PAIRS, (D0, D1), 0)
                    high_of(g, 1)

                high_weights(0, (A0, B0), 0)
                body(0)
                with act.Fori(1, PAIRS - 1) as g:
                    body(g)
                body(PAIRS - 1, last=True)
                act.wait_ge(t_done, 1)
                act.activation(tl[:, :], psA[0:2 * EXT * FC, 0, 0:P], ACT.Copy).then_inc(t_out, 1)

            @block.vector
            def _(dve):
                rest = SEQ - 2 * TN
                for b in range(2):
                    dve.memset(cb[:, b, 0:1], 0.0).then_inc(p_out[b], 1)
                    dve.wait_ge(p_out[b], 1)

                def conv_of(g, e):
                    ch = 2 * g + e
                    own = Steps(dve, conv_steps, 4 * g + 2 * e)
                    dve.wait_ge(row_done, 2 * g + (e + 1))
                    if not (isinstance(g, int) and g == 0):
                        dve.wait_ge(u_hi, 2 * g + (e - 1))
                    w = lambda j: vcw[:, j, bass.ds(ch, 1)]
                    c = cb[:, e, :]
                    own.after(dve.tensor_scalar(c, ax[:, e, 0:CL], w(0), k.vec[:, bass.ds(V_CB + ch, 1)], ALU.mult, ALU.add))
                    own.after(dve.scalar_tensor_tensor(c, ax[:, e, 1:1 + CL], w(1), c, ALU.mult, ALU.add))
                    dve.scalar_tensor_tensor(c, ax[:, e, 2:2 + CL], w(2), c, ALU.mult, ALU.add).then_inc(conv_done, 1)

                def gate_of(g, e):
                    dve.wait_ge(gelu_done, 2 * g + (e + 1))
                    for t in range(NT):
                        dve.wait_ge(b_done, 6 * g + (3 * e + t + 1))
                        if t < NT - 1:
                            v = cb[:, e, t * TN:(t + 1) * TN]
                            dve.tensor_tensor(v, v, psB[:, t, 0:TN], ALU.mult).then_inc(b_out, 1)
                        else:
                            v = cb[:, e, t * TN:SEQ]
                            dve.tensor_tensor(v, v, psB[:, t, 0:rest], ALU.mult)
                            v = cb[:, e, SB:CL]
                            dve.tensor_tensor(v, v, psB[:, t, rest:TN], ALU.mult).then_inc(b_out, 1)

                def low_of(g, e):
                    dve.wait_ge(u_hi, 2 * g + (e + 1))
                    dve.tensor_tensor(ulo[:, e, 0:SEQ], cb[:, e, 0:SEQ], uhi[:, e, 0:SEQ].bitcast(F32), ALU.subtract)
                    dve.tensor_tensor(ulo[:, e, SEQ:TOK], cb[:, e, SB:CL], uhi[:, e, SEQ:TOK].bitcast(F32), ALU.subtract)\
                       .then_inc(u_lo, 1)

                def add_pair(g):
                    for m in range(DC):
                        for t in range(NT):
                            o = m * NT + t
                            dve.wait_ge(p_done[o % 2], 12 * (g - 1) + (o // 2 + 1))
                            x = xT[:, m, t * TN:(t + 1) * TN]
                            last = dve.tensor_tensor(x, x, psD[:, o % 2, 0:TN], ALU.add)
                            last.then_inc(p_out[o % 2], 1)

                def body(g, roles, n0):
                    if A0 in roles:
                        conv_of(g, 0)
                        gate_of(g, 0)
                    if D0 in roles:
                        add_pair(g)
                    if A0 in roles:
                        low_of(g, 0)
                        conv_of(g, 1)
                        gate_of(g, 1)
                        low_of(g, 1)
                each_round(dve, body)


def restart(nc, sems):
    with nc.Block() as block:

        @block.gpsimd
        def _(pool):
            for x in sems:
                pool.sem_clear(x)


def program(nc, k):
    alloc = lambda n: nc.alloc_semaphore(n)
    many = lambda n, m: [alloc(f"{n}{i}") for i in range(m)]
    k.sems = {
        "tok": dict(const=alloc("tok_const"), a=many("tok_rows", 2),
                    b=many("tok_turned", 2), c=many("tok_copied", 2)),
        "out": dict(b=many("out_turned", 2), c=many("out_copied", 2), s=many("out_stored", 2)),
    }
    layer, k.lists = [], {}

    def group(name, singles, several=()):
        d = {n: alloc(f"{name}_{n}") for n in singles.split()}
        for n, m in several:
            d[n] = many(f"{name}_{n}", m)
        for v in d.values():
            layer.extend(v if isinstance(v, list) else [v])
        k.sems[name] = d
        k.lists[name] = [x for v in d.values() for x in (v if isinstance(v, list) else [v])]

    group("vec", "l t r v d")
    group("norm", "sq ps sum ln rs hf hi lo lp")
    group("x", "st")
    group("win", "", [("raw", 2), ("hi", 2), ("lo", 2), ("done", 3), ("tf", 3)])
    group("fox", "cl st act dve f fc ft rh")
    group("swa", "p sum inv st")
    group("mla", "w c dve t xo q k qo ko ksq ksum qsum z inv")
    group("att", "clr ld x xh xl s m e n t tl th o y d iv pn dc", [("row", 2)])
    group("smp", "z qt qd x k s d m e n t o y", [("in", 3), ("xo", 2), ("to", 2)])
    group("wout", "x", [("raw", 2), ("hi", 2), ("lo", 2), ("done", 2), ("add", 2)])
    group("ffn", "clr hi split a ao row cs conv gelu b bo uh ul t to st", [("raw", 2), ("p", 2), ("po", 2)])

    with ExitStack() as s:
        T = lambda n, shape, dt=F32: s.enter_context(nc.sbuf_tensor(n, shape, dt))
        k.const = T("const", [P, C_N])
        k.identr, k.mfoxr, k.mmlar = (T(n, [P, P], F32R) for n in ("identr", "mfoxr", "mmlar"))
        k.vec, k.row = T("vec", [P, V_N]), T("row", [P, R_N])
        load_tokens(nc, k)
        with nc.Fori(0, DEPTH) as lay:
            one_layer(nc, k, lay)
            restart(nc, layer)
        store_tokens(nc, k)


def one_layer(nc, k, lay):
    left, right = ExitStack(), ExitStack()

    def lt(n, shape, dt=F32):
        return left.enter_context(nc.sbuf_tensor(n, shape, dt))

    def rt(n, shape, dt=F32, where=right):
        return where.enter_context(nc.sbuf_tensor(n, shape, dt, side="right"))

    def first_blocks(sp, raw, sems, block):
        for b in range(2):
            sp.dma_start(raw[:, b], block(b)).then_inc(sems[b], 16)

    hi, lo = rt("h_hi", [P, DC, TOK], F32R), rt("h_lo", [P, DC, TOK], F32R)
    wraw = rt("wraw", [P, 2, DC, WN])
    with ExitStack() as f:
        xT = f.enter_context(x_home(nc, k, "xT1"))
        x_stored = k.sems["x"]["st"]

        def also(sp):
            sp.dma_start(k.x_dram, xT[:, :, :]).then_inc(x_stored, 16)
            first_blocks(sp, wraw, k.sems["win"]["raw"], lambda b: w_in_block(k, lay, b))
            sp.wait_ge(x_stored, 16)

        norm(nc, k, xT, hi, lo, V_G1, "1", [(0, DC)], also, Vectors(nc, k, lay, f))
    proj = lt("proj", [P, TT, IN_W])
    prepared = ExitStack()
    prep = Prepare(nc, k, lay, prepared, proj)
    project_in(nc, k, lay, hi, lo, proj, wraw, prep)
    right.close()

    yT = rt("yT", [P, DC, TOK])
    with prepared as f:
        fs = prep.fs
        with ExitStack() as f2:
            frow = [f2.enter_context(nc.sbuf_tensor("frow" + n, [FOXH, SEQ], F32R)) for n in ("hi", "lo")]
            fox_rows(nc, k, prep, frow)
            cols = lambda o: (lambda h: proj[:, :, o + HD * h:o + HD * (h + 1)])
            attend_prompt(nc, k, "fox", FOXH, HD, cols(O_FQ), cols(O_FK),
                          lambda h, t: proj[:, t, O_FV + HD * h:O_FV + HD * (h + 1)], lambda h: h, yT, 0, frow=frow)
        kc = f.enter_context(nc.sbuf_tensor("fkc", [P, QT, FOXH * HD], F32))
        vc = f.enter_context(nc.sbuf_tensor("fvc", [P, QT, FOXH * HD], F32))
        loads = [(dst[:, a:b, :], src[lay, 0].rearrange("(t p) h d -> p t (h d)", p=P)[:, a:b])
                 for dst, src, a, b in ((kc, k.cache_fox_k, 0, 4), (kc, k.cache_fox_k, 4, QT), (vc, k.cache_fox_v, 0, QT))]
        tiles = [(P, lambda u, t=t: kc[:, t, P * u:P * (u + 1)], lambda p, t=t: vc[:, t, P * p:P * (p + 1)])
                 for t in range(QT)]
        tiles.append((DEC, lambda u: proj[0:DEC, QT, O_FK + P * u:O_FK + P * (u + 1)],
                      lambda p: proj[0:DEC, QT, O_FV + P * p:O_FV + P * (p + 1)]))
        attend_sample(nc, k, "fox", FOXH, lambda u: proj[0:DEC, QT, O_FQ + P * u:O_FQ + P * (u + 1)], FOXH // 2, P,
                      lambda h: HD * (h % 2), tiles, loads, yT, 0, fs, SwaHeads(nc, k, lay, f, proj))

    attend_prompt(nc, k, "swa", SWAH, HD, cols(O_SQ), cols(O_SK),
                  lambda g, t: proj[:, t, O_SV + HD * g:O_SV + HD * (g + 1)], lambda h: h // (SWAH // SWAKV), yT, 3,
                  alibi=k.alibi)
    with ExitStack() as f:
        old = WIN - CHUNK
        kc = f.enter_context(nc.sbuf_tensor("skc", [old, P], F32))
        vc = f.enter_context(nc.sbuf_tensor("svc", [old, P], F32))
        loads = [(dst[:, :], src[lay, 0, CHUNK:WIN].rearrange("t h d -> t (h d)"))
                 for dst, src in ((kc, k.cache_swa_k), (vc, k.cache_swa_v))]
        tiles = [(old, lambda u: kc[:, :], lambda p: vc[:, :]),
                 (DEC, lambda u: proj[0:DEC, QT, O_SK:O_SV], lambda p: proj[0:DEC, QT, O_SV:O_CQ])]
        attend_sample(nc, k, "swa", SWAH, lambda u: proj[0:DEC, QT, O_SQ + P * u:O_SQ + P * (u + 1)], 1, P,
                      lambda h: HD * (h // (SWAH // SWAKV)), tiles, loads, yT, 3)

    with ExitStack() as f:
        qm = rt("qm", [P, TT, MLAH, MQK], where=f)
        km = rt("km", [P, 2 * QT + 1, MLAH, MQK], where=f)
        vm = rt("vm", [P, 2 * QT + 1, MLAH, HD], where=f)
        mla_prepare(nc, k, lay, proj, qm, km, vm)
        left.close()
        attend_prompt(nc, k, "mla", MLAH, MQK, lambda h: qm[:, :, h, :], lambda h: km[:, :, h, :],
                      lambda h, t: vm[:, t, h, :], lambda h: h, yT, 6)
        tiles = [(P if j < QT else DEC, lambda u, j=j: km[0:P if j < QT else DEC, QT + j, u, :],
                  lambda p, j=j: vm[0:P if j < QT else DEC, QT + j, 2 * p:2 * p + 2, :].rearrange("p h d -> p (h d)"))
                 for j in range(TT)]
        attend_sample(nc, k, "mla", MLAH, lambda h: qm[0:DEC, QT, h, :], MLAH, MQK, lambda h: HD * (h % 2), tiles,
                      [], yT, 6)

    xT = left.enter_context(x_home(nc, k, "xT2"))
    with ExitStack() as f:
        T = lambda n, shape, dt=F32: f.enter_context(nc.sbuf_tensor(n, shape, dt))
        hi, lo, raw = T("y_hi", [P, DC, TOK], F32R), T("y_lo", [P, DC, TOK], F32R), T("oraw", [P, 2, DC, P])

        def also(sp):
            first_blocks(sp, raw, k.sems["wout"]["raw"], lambda b: w_out_block(k, lay, b))
            sp.dma_start(xT[:, :, :], k.x_dram).then_inc(k.sems["wout"]["x"], 16)

        norm(nc, k, yT, hi, lo, V_GM, "2", [(0, 3), (3, 6), (6, 8)], also)
        right.close()
        project_out(nc, k, lay, hi, lo, xT, raw)
    with ExitStack() as f:
        T = lambda n, shape, dt=F32: f.enter_context(nc.sbuf_tensor(n, shape, dt))
        hi, lo, raw = T("g_hi", [P, DC, TOK], F32R), T("g_lo", [P, DC, TOK], F32R), T("fraw", [P, 2, DC, P])

        def also(sp):
            first_blocks(sp, raw, k.sems["ffn"]["raw"], lambda b: up_block(k, lay, b * DFF))

        norm(nc, k, xT, hi, lo, V_G2, "3", [(0, DC)], also)
        conv_ffn(nc, k, lay, hi, lo, xT, raw)
    left.close()


_INS = ['x_prompt', 'x_sample', 'cache_fox_k', 'cache_fox_v', 'cache_fox_logf', 'cache_swa_k', 'cache_swa_v',
        'cache_mla_ckv', 'cache_mla_krope', 'state_ffn_conv', 'g_norm1', 'w_in', 'b_fox_f', 'g_fox_q', 'g_fox_k',
        'g_swa_q', 'g_swa_k', 'swa_sinks', 'g_mla_cq', 'g_mla_ckv', 'w_mla_uq', 'w_mla_ukv', 'g_mla_q', 'g_mla_k',
        'g_mix_out', 'w_out', 'g_norm2', 'w_ffn_up', 'w_ffn_conv', 'b_ffn_conv', 'w_ffn_down']
_STREAM = lambda T, win: [(DEPTH, 1, T, FOXH, HD), (DEPTH, 1, T, FOXH, HD), (DEPTH, 1, T, FOXH),
                          (DEPTH, 1, win, SWAKV, HD), (DEPTH, 1, win, SWAKV, HD), (DEPTH, 1, T, KVLORA),
                          (DEPTH, 1, T, ROPE), (DEPTH, 1, CW - 1, DFF)]
_PARTS = ['fox_k', 'fox_v', 'fox_logf', 'swa_k', 'swa_v', 'mla_ckv', 'mla_krope', 'ffn_conv']
_OUTS = [('y_prompt', (1, SEQ, D)), ('y_sample', (1, DEC, D))] + \
    [(n + '_p', s) for n, s in zip(_PARTS, _STREAM(SEQ, WIN))] + \
    [(n + '_s', s) for n, s in zip(_PARTS, _STREAM(DEC, WIN))]


def kernel(**inputs):
    import concourse.bacc as _bacc
    from concourse.bass_utils import run_bass_kernel_spmd as _run

    nc = _bacc.Bacc("TRN2", target_bir_lowering=False, num_devices=1)
    arrays = {f"in_{name}": np.ascontiguousarray(inputs[name]) for name in _INS}
    arrays["in_const"], arrays["in_alibi"] = const_table(), alibi_table()
    k = Chip()
    for name in _INS:
        a = arrays[f"in_{name}"]
        ap = nc.dram_tensor(f"in_{name}", a.shape, F32, kind="ExternalInput").ap()
        k.__dict__[name] = ap[0] if name.startswith("x_") else ap
    k.consts = nc.dram_tensor("in_const", (P, C_N), F32, kind="ExternalInput").ap()
    k.alibi = nc.dram_tensor("in_alibi", (P, SWAH, 2 * P), F32, kind="ExternalInput").ap()
    for name, shape in _OUTS:
        ap = nc.dram_tensor(f"out_{name}", shape, F32, kind="ExternalOutput").ap()
        k.__dict__[name] = ap[0] if name.startswith("y_") else ap
    k.x_dram = nc.dram_tensor("x_between", (P, DC, TOK), F32, kind="Internal").ap()
    program(nc, k)
    r = _run(nc, [arrays], core_ids=[0])
    return tuple(r.results[0][f"out_{name}"] for name, _ in _OUTS)
```
